# Optimizing a Trainium2 kernel written in Bass

```python
import math
import jax, jax.numpy as jnp
from jax import lax
import numpy as np

D_MODEL = 1024
BATCH = 1
SEQ = 512
DEPTH = 1

GRID_W = 64
CTX_LEN = 256
RET_HEADS = 4
RET_DK = D_MODEL // RET_HEADS
RET_DV = 2 * D_MODEL // RET_HEADS
RET_CHUNK = 128
DIFF_DH = 64
DIFF_HEADS = D_MODEL // (2 * DIFF_DH)
DIFF_DV = 2 * DIFF_DH
Q_BLOCK = 128
N_EXPERTS = 32
TOP_K = 4
D_FF = D_MODEL
SWIGLU_LIMIT = 7.0
SWIGLU_ALPHA = 1.702
MOE_BLOCK = 128
ROPE_BASE = 10000.0
EPS = 1e-6

RET_QK_W = RET_HEADS * RET_DK
RET_V_W = RET_HEADS * RET_DV
DIFF_QK_W = DIFF_HEADS * 2 * DIFF_DH
DIFF_V_W = DIFF_HEADS * DIFF_DV
IN_SPLITS = (RET_QK_W, RET_QK_W, RET_V_W, RET_V_W, DIFF_QK_W, DIFF_QK_W, DIFF_V_W, D_MODEL, D_MODEL)
IN_COLS = sum(IN_SPLITS)

kernel_name = "hybrid_retention_diffattn_moe_dit_block"

def _rmsnorm(x, g):
    xf = x.astype(jnp.float32)
    y = xf * lax.rsqrt(jnp.mean(xf * xf, axis=-1, keepdims=True) + EPS)
    return (y * g.astype(jnp.float32)).astype(x.dtype)

def _modulate(h, shift, scale):
    return h * (1.0 + scale) + shift

def _rope_axis(x, pos):
    half = x.shape[-1] // 2
    inv = ROPE_BASE ** (-jnp.arange(half, dtype=jnp.float32) / half)
    ang = pos.astype(jnp.float32)[:, None] * inv[None, :]
    cos, sin = jnp.cos(ang), jnp.sin(ang)
    x1 = x[..., :half].astype(jnp.float32)
    x2 = x[..., half:].astype(jnp.float32)
    return jnp.concatenate([x1 * cos - x2 * sin, x1 * sin + x2 * cos], axis=-1).astype(x.dtype)

def _rope_2d(x, row, col):
    d2 = x.shape[-1] // 2
    return jnp.concatenate([_rope_axis(x[..., :d2], row), _rope_axis(x[..., d2:], col)], axis=-1)

def _project(h, w_in):
    p = h @ w_in
    return jnp.split(p, np.cumsum(IN_SPLITS)[:-1].tolist(), axis=-1)

def _ret_heads(t, d):
    b, l, _ = t.shape
    return t.reshape(b, l, RET_HEADS, d).transpose(0, 2, 1, 3).astype(jnp.float32)

def _retention_scan(q, k, v, log_gamma, s0):
    b, h, l, _ = q.shape
    dv = v.shape[-1]
    n = l // RET_CHUNK

    def chunks(t):
        return t.reshape(b, h, n, RET_CHUNK, t.shape[-1]).transpose(2, 0, 1, 3, 4)

    j = jnp.arange(RET_CHUNK, dtype=jnp.float32)
    diff = j[:, None] - j[None, :]
    lg = log_gamma.astype(jnp.float32)
    decay_in = jnp.where(diff >= 0, jnp.exp(lg[:, None, None] * jnp.maximum(diff, 0.0)), 0.0)
    q_decay = jnp.exp(lg[:, None] * (j + 1.0))[:, :, None]
    k_decay = jnp.exp(lg[:, None] * (RET_CHUNK - 1.0 - j))[:, :, None]
    chunk_decay = jnp.exp(lg * RET_CHUNK)[:, None, None]

    def step(s, qkv):
        qc, kc, vc = qkv
        inner = jnp.einsum('bhid,bhjd->bhij', qc, kc) * decay_in
        o = jnp.einsum('bhij,bhjv->bhiv', inner, vc) + jnp.einsum('bhid,bhdv->bhiv', qc * q_decay, s)
        s = chunk_decay * s + jnp.einsum('bhjd,bhjv->bhdv', kc * k_decay, vc)
        return s, o

    s_fin, o = lax.scan(step, s0, (chunks(q), chunks(k), chunks(v)))
    return o.transpose(1, 2, 0, 3, 4).reshape(b, h, l, dv), s_fin

def _retention_bidir(q, k, v, log_g_fwd, log_g_bwd, s0_fwd, s0_bwd):
    o_f, s_f = _retention_scan(q, k, v, log_g_fwd, s0_fwd)
    flip = lambda t: t[:, :, ::-1]
    o_b, s_b = _retention_scan(flip(q), flip(k), flip(v), log_g_bwd, s0_bwd)
    return o_f + flip(o_b), s_f, s_b

def _diff_qk(t, g, row, col):
    b, l, _ = t.shape
    t = _rmsnorm(t.reshape(b, l, DIFF_HEADS, 2, DIFF_DH), g).transpose(0, 2, 3, 1, 4)
    if row is not None:
        t = _rope_2d(t, row, col)
    return t[:, :, 0], t[:, :, 1]

def _diff_attend(q1, q2, k1, k2, v, lam):
    scale = DIFF_DH ** -0.5
    s1 = jnp.einsum('bhqd,bhkd->bhqk', q1, k1).astype(jnp.float32) * scale
    s2 = jnp.einsum('bhqd,bhkd->bhqk', q2, k2).astype(jnp.float32) * scale
    a = jax.nn.softmax(s1, axis=-1) - lam * jax.nn.softmax(s2, axis=-1)
    return jnp.einsum('bhqk,bhkv->bhqv', a.astype(v.dtype), v)

def _diff_attend_blocks(q1, q2, k1, k2, v, lam):
    b, h, l, dh = q1.shape
    nb = l // Q_BLOCK
    blk = lambda t: t.reshape(b, h, nb, Q_BLOCK, dh).transpose(2, 0, 1, 3, 4)
    o = lax.map(lambda qq: _diff_attend(qq[0], qq[1], k1, k2, v, lam), (blk(q1), blk(q2)))
    return o.transpose(1, 2, 0, 3, 4).reshape(b, h, l, v.shape[-1])

def _moe(h, router_w, router_b, w1, b1, w2, b2):
    b, l, d = h.shape
    xt = h.reshape(-1, d)
    t = xt.shape[0]
    logits = (xt @ router_w + router_b).astype(jnp.float32)
    top_val, top_idx = lax.top_k(logits, TOP_K)
    gate = jax.nn.softmax(top_val, axis=-1)
    p = t * TOP_K
    expert_flat = top_idx.reshape(-1)
    order = jnp.argsort(expert_flat)
    sorted_e = expert_flat[order]
    counts = jnp.bincount(expert_flat, length=N_EXPERTS)
    padded = (counts + MOE_BLOCK - 1) // MOE_BLOCK * MOE_BLOCK
    pad_end = jnp.cumsum(padded)
    pad_start = pad_end - padded
    cnt_start = jnp.cumsum(counts) - counts
    dest = pad_start[sorted_e] + jnp.arange(p, dtype=jnp.int32) - cnt_start[sorted_e]
    n_blocks = -(-p // MOE_BLOCK) + N_EXPERTS
    rows = n_blocks * MOE_BLOCK
    row_tok = jnp.full((rows,), t, dtype=jnp.int32).at[dest].set((order // TOP_K).astype(jnp.int32))
    row_gate = jnp.zeros((rows,), jnp.float32).at[dest].set(gate.reshape(-1)[order])
    block_e = jnp.minimum(jnp.searchsorted(pad_end, jnp.arange(n_blocks) * MOE_BLOCK, side='right'),
                          N_EXPERTS - 1)
    x_pad = jnp.concatenate([xt, jnp.zeros((1, d), xt.dtype)], axis=0)
    xb = x_pad[row_tok].reshape(n_blocks, MOE_BLOCK, d)

    def expert_block(args):
        xblk, e = args
        hh = xblk @ w1[e] + b1[e]
        glu = jnp.minimum(hh[:, :D_FF], SWIGLU_LIMIT)
        lin = jnp.clip(hh[:, D_FF:], -SWIGLU_LIMIT, SWIGLU_LIMIT)
        act = glu * jax.nn.sigmoid(SWIGLU_ALPHA * glu) * (lin + 1.0)
        return act @ w2[e] + b2[e]

    yb = lax.map(expert_block, (xb, block_e)).reshape(rows, d)
    y = jax.ops.segment_sum(yb * row_gate[:, None].astype(yb.dtype), row_tok, num_segments=t + 1)[:t]
    return y.reshape(b, l, d)

def _layer(x, ctx, c, c_ctx, row, col, layer_idx, need_ctx_out,
           norm1_g, norm2_g, w_mod, b_mod, w_in, ret_decay_logit, ret_norm_g,
           diff_q_norm_g, diff_k_norm_g, diff_lambda, diff_norm_g,
           w_br_ret, w_br_diff, w_out, router_w, router_b, exp_w1, exp_b1, exp_w2, exp_b2):
    b, l, d = x.shape
    mod_l = (jax.nn.silu(c) @ w_mod + b_mod)[:, None, :]
    mod_c = (jax.nn.silu(c_ctx) @ w_mod + b_mod)[None, None, :]
    sh_a, sc_a, g_a, sh_f, sc_f, g_f = jnp.split(mod_l, 6, axis=-1)
    csh_a, csc_a, cg_a, csh_f, csc_f, cg_f = jnp.split(mod_c, 6, axis=-1)

    hl = _modulate(_rmsnorm(x, norm1_g), sh_a, sc_a)
    hc = _modulate(_rmsnorm(ctx, norm1_g), csh_a, csc_a)
    rq, rk, rv, rg, dq, dk, dv, ga, gb = _project(hl, w_in)
    crq, crk, crv, crg, cdq, cdk, cdv, cga, cgb = _project(hc, w_in)

    log_g = jax.nn.log_sigmoid(ret_decay_logit.astype(jnp.float32))
    qs = RET_DK ** -0.5
    lq = _rope_2d(_ret_heads(rq, RET_DK) * qs, row, col)
    lk = _rope_2d(_ret_heads(rk, RET_DK), row, col)
    lv = _ret_heads(rv, RET_DV)
    cq = _ret_heads(crq, RET_DK) * qs
    ck = _ret_heads(crk, RET_DK)
    cv = _ret_heads(crv, RET_DV)
    s0 = jnp.zeros((b, RET_HEADS, RET_DK, RET_DV), jnp.float32)
    ret_c, s_f, s_b = _retention_bidir(cq, ck, cv, log_g[0], log_g[1], s0, s0)
    ret_l, _, _ = _retention_bidir(lq, lk, lv, log_g[0], log_g[1], s_f, s_b)

    def ret_branch(o, gate):
        y = _rmsnorm(o, ret_norm_g[:, None, :])
        y = y.transpose(0, 2, 1, 3).reshape(o.shape[0], o.shape[2], RET_V_W).astype(gate.dtype)
        return (y * jax.nn.silu(gate)) @ w_br_ret

    lambda_init = 0.8 - 0.6 * math.exp(-0.3 * layer_idx)
    lp = diff_lambda.astype(jnp.float32)
    lam = jnp.exp(jnp.sum(lp[0] * lp[1])) - jnp.exp(jnp.sum(lp[2] * lp[3])) + lambda_init
    lq1, lq2 = _diff_qk(dq, diff_q_norm_g, row, col)
    lk1, lk2 = _diff_qk(dk, diff_k_norm_g, row, col)
    cq1, cq2 = _diff_qk(cdq, diff_q_norm_g, None, None)
    ck1, ck2 = _diff_qk(cdk, diff_k_norm_g, None, None)
    lvd = dv.reshape(b, l, DIFF_HEADS, DIFF_DV).transpose(0, 2, 1, 3)
    cvd = cdv.reshape(b, ctx.shape[1], DIFF_HEADS, DIFF_DV).transpose(0, 2, 1, 3)
    k1_all = jnp.concatenate([ck1, lk1], axis=2)
    k2_all = jnp.concatenate([ck2, lk2], axis=2)
    v_all = jnp.concatenate([cvd, lvd], axis=2)
    diff_l = _diff_attend_blocks(lq1, lq2, k1_all, k2_all, v_all, lam)

    def diff_branch(o):
        y = _rmsnorm(o, diff_norm_g) * (1.0 - lambda_init)
        y = y.transpose(0, 2, 1, 3).reshape(o.shape[0], o.shape[2], DIFF_V_W)
        return y @ w_br_diff

    def merge(yr, yd, gate_r, gate_d):
        return (jax.nn.sigmoid(gate_r) * yr + jax.nn.sigmoid(gate_d) * yd) @ w_out

    x_new = x + g_a * merge(ret_branch(ret_l, rg), diff_branch(diff_l), ga, gb)
    x_new = x_new + g_f * _moe(_modulate(_rmsnorm(x_new, norm2_g), sh_f, sc_f),
                               router_w, router_b, exp_w1, exp_b1, exp_w2, exp_b2)
    if need_ctx_out:
        diff_c = _diff_attend(cq1, cq2, ck1, ck2, cvd, lam)
        ctx = ctx + cg_a * merge(ret_branch(ret_c, crg), diff_branch(diff_c), cga, cgb)
        ctx = ctx + cg_f * _moe(_modulate(_rmsnorm(ctx, norm2_g), csh_f, csc_f),
                                router_w, router_b, exp_w1, exp_b1, exp_w2, exp_b2)
    return x_new, ctx

def setup_inputs(seed: int = 0) -> dict:
    key = jax.random.key(seed)
    ks = jax.random.split(key, 32)
    f32 = jnp.float32
    nrm = lambda k, shape, s: jax.random.normal(k, shape, f32) * s
    decay_base = jnp.asarray(np.log(2.0 ** (5 + np.arange(RET_HEADS)) - 1.0), f32)
    return {
        "x": nrm(ks[0], (BATCH, SEQ, D_MODEL), 1.0),
        "c": nrm(ks[1], (BATCH, D_MODEL), 1.0),
        "ctx": nrm(ks[2], (BATCH, CTX_LEN, D_MODEL), 1.0),
        "c_ctx": nrm(ks[3], (D_MODEL,), 1.0),
        "norm1_g": 1.0 + nrm(ks[4], (DEPTH, D_MODEL), 0.1),
        "norm2_g": 1.0 + nrm(ks[5], (DEPTH, D_MODEL), 0.1),
        "w_mod": nrm(ks[6], (DEPTH, D_MODEL, 6 * D_MODEL), 0.5 * D_MODEL ** -0.5),
        "b_mod": nrm(ks[7], (DEPTH, 6 * D_MODEL), 0.02),
        "w_in": nrm(ks[8], (DEPTH, D_MODEL, IN_COLS), D_MODEL ** -0.5),
        "ret_decay_logit": decay_base[None, None, :] + nrm(ks[9], (DEPTH, 2, RET_HEADS), 0.1),
        "ret_norm_g": 1.0 + nrm(ks[10], (DEPTH, RET_HEADS, RET_DV), 0.1),
        "diff_q_norm_g": 1.0 + nrm(ks[11], (DEPTH, DIFF_DH), 0.1),
        "diff_k_norm_g": 1.0 + nrm(ks[12], (DEPTH, DIFF_DH), 0.1),
        "diff_lambda": nrm(ks[13], (DEPTH, 4, DIFF_DH), 0.1),
        "diff_norm_g": 1.0 + nrm(ks[14], (DEPTH, DIFF_DV), 0.1),
        "w_br_ret": nrm(ks[15], (DEPTH, RET_V_W, D_MODEL), RET_V_W ** -0.5),
        "w_br_diff": nrm(ks[16], (DEPTH, DIFF_V_W, D_MODEL), DIFF_V_W ** -0.5),
        "w_out": nrm(ks[17], (DEPTH, D_MODEL, D_MODEL), D_MODEL ** -0.5),
        "router_w": nrm(ks[18], (DEPTH, D_MODEL, N_EXPERTS), D_MODEL ** -0.5),
        "router_b": nrm(ks[19], (DEPTH, N_EXPERTS), 0.01),
        "exp_w1": nrm(ks[20], (DEPTH, N_EXPERTS, D_MODEL, 2 * D_FF), D_MODEL ** -0.5),
        "exp_b1": nrm(ks[21], (DEPTH, N_EXPERTS, 2 * D_FF), 0.02),
        "exp_w2": nrm(ks[22], (DEPTH, N_EXPERTS, D_FF, D_MODEL), D_FF ** -0.5),
        "exp_b2": nrm(ks[23], (DEPTH, N_EXPERTS, D_MODEL), 0.02),
    }

def reference(x, c, ctx, c_ctx, norm1_g, norm2_g, w_mod, b_mod, w_in, ret_decay_logit, ret_norm_g,
              diff_q_norm_g, diff_k_norm_g, diff_lambda, diff_norm_g, w_br_ret, w_br_diff, w_out,
              router_w, router_b, exp_w1, exp_b1, exp_w2, exp_b2):
    n_tok = x.shape[1]
    ROWS = n_tok // GRID_W
    row = jnp.repeat(jnp.arange(ROWS, dtype=jnp.int32), GRID_W)
    col = jnp.tile(jnp.arange(GRID_W, dtype=jnp.int32), ROWS)
    for i in range(DEPTH):
        x, ctx = _layer(x, ctx, c, c_ctx, row, col, i, i < DEPTH - 1,
                        norm1_g[i], norm2_g[i], w_mod[i], b_mod[i], w_in[i], ret_decay_logit[i], ret_norm_g[i],
                        diff_q_norm_g[i], diff_k_norm_g[i], diff_lambda[i], diff_norm_g[i],
                        w_br_ret[i], w_br_diff[i], w_out[i], router_w[i], router_b[i],
                        exp_w1[i], exp_b1[i], exp_w2[i], exp_b2[i])
    return x


_drawn_inputs = setup_inputs


def setup_inputs(seed=0):
    import zlib

    import numpy as np

    out = dict(_drawn_inputs(seed))
    spreads = {}
    factors = {'ret_norm_g': 3.147,
     'diff_q_norm_g': 5.822,
     'diff_k_norm_g': 6.012,
     'diff_lambda': 8.0,
     'diff_norm_g': 2.776,
     'router_b': 4.099,
     'exp_b1': 8.0,
     'exp_b2': 8.0}
    for name, (base, spread) in spreads.items():
        noise = np.random.default_rng([zlib.crc32(name.encode()), seed]).standard_normal(out[name].shape)
        drawn = base * np.exp(spread * noise) if base else spread * noise
        out[name] = __import__('jax').numpy.asarray(drawn.astype(out[name].dtype))
    for name, factor in factors.items():
        out[name] = (out[name] * factor).astype(out[name].dtype)
    return out
```

```python
from contextlib import ExitStack

import concourse.bass as bass
from concourse import mybir

F32 = mybir.dt.float32
F32R = mybir.dt.float32r
BF16 = mybir.dt.bfloat16
I32 = mybir.dt.int32
U32 = mybir.dt.uint32
ALU = mybir.AluOpType
ACT = mybir.ActivationFunctionType
AX = mybir.AxisListType

P = 128
D = 1024
KC = D // P
L = 512
LT = L // P
C = 256
CT = C // P
T = L + C
TT = T // P
COL = 512
KH = 4
NRAW = 4
NSPL = 2
ERAW = 6
ESPL = 4

RET_HEADS = 4
DK = D // RET_HEADS
DV = 2 * D // RET_HEADS
GRID_W = 64
GRID_H = L // GRID_W
DH = 64
HG = 4
GROUPS = 2
N_EXPERTS = 32
TOP_K = 4
LIMIT = 7.0
ALPHA = 1.702
EPS = 1e-6
LAMBDA_INIT = 0.2
MAX_BLOCKS = L * TOP_K // P - 1 + N_EXPERTS
OVER = MAX_BLOCKS - N_EXPERTS
ITEMS = MAX_BLOCKS + 1

RQ, RK, RV, RG, DQ, DKK, DVV, GA, GB = 0, 1024, 2048, 4096, 6144, 7168, 8192, 9216, 10240

MOD0, MOD_N = 0, 24
RET0, RET_N = 24, 8
GA0 = RET0 + RET_N * RET_HEADS
DIFF0, DIFF_N = GA0 + 4, 8
GB0 = DIFF0 + DIFF_N * GROUPS
OUT0 = GB0 + 4
MOE0, MOE_N = OUT0 + 4, 12

C_ID = 0
C_TRI = C_ID + P
C_WIN = C_TRI + P
WIN = 2 * L - P
C_ROPE_R = C_WIN + WIN
C_ROPE_D = C_ROPE_R + 2 * GRID_H + 2 * GRID_W
C_IOTA = C_ROPE_D + LT * 2 * DH
C_TOK = C_IOTA + N_EXPERTS
C_THR = C_TOK + LT
C_CODE = C_THR + 1
C_EXP = C_CODE + 1
C_EYE3 = C_EXP + 1
N_CONST = C_EYE3 + N_EXPERTS

A_WORDS = 17920
A_X, A_BMOD, A_SQ = 0, 6144, 12288
A_RAWQK = 0
A_QT, A_KT, A_V, A_GATE, A_DEC, A_TMP = 3072, 4096, 5632, 8704, 10752, 12288
A_ACC = A_WORDS - 4096
A_PROB = 0
A_AT = 3072
A_OY, A_DV, A_DQT, A_DKT = 4608, 5632, 8704, 10752
A_ACC2 = 0
A_XN = 4096
A_GFB, A_GAB, A_A2B, A_SH2B = 8192, 9216, 10240, 11264
A_H2T = 0
A_HT = 12288
A_BIAS = 14336
A_BSRC, A_BR = 10240, 1024
A_TX = 13824
A_GAP = 13312
A_RT = 15872
A_EW = 10240
A_XG, A_Y, A_GS, A_LS, A_TH, A_AC = 0, 1024, 2048, 2560, 3072, 9216


def at(i, per, k):
    return i * per + k


class Steps:

    def __init__(self, eng, sem, base=0):
        self.eng, self.sem, self.base, self.k = eng, sem, base, 0

    def did(self, ins):
        ins.then_inc(self.sem, 1)
        self.k += 1

    def wait(self):
        self.eng.wait_ge(self.sem, self.base + self.k)


def build(nc, a, scratch):
    mod_d, h2_d, list_d, acc_d, accr_d = scratch
    ctx = ExitStack()
    with ctx:
        def sb(name, shape, dt=F32):
            return ctx.enter_context(nc.sbuf_tensor(name, shape, dt))

        def sem(name):
            return ctx.enter_context(nc.semaphore(name))

        cst = sb("cst", [P, N_CONST])
        raw = sb("raw", [P, NRAW, KH, COL])
        whi = sb("whi", [P, NSPL, KH, COL], F32R)
        wlo = sb("wlo", [P, NSPL, KH, COL], F32R)
        hhi = sb("hhi", [P, KC, T], F32R)
        hlo = sb("hlo", [P, KC, T], F32R)
        yhi = sb("yhi", [P, KH, L], F32R)
        ylo = sb("ylo", [P, KH, L], F32R)
        ar = sb("ar", [P, A_WORDS])
        cc = sb("cc", [P, KC, 2])
        ct = sb("ct", [P, KC, 2])
        mcols = sb("mcols", [P, 5, KC])
        ones = sb("ones", [P, 16])
        ss = sb("ss", [P, 16])
        sm = sb("sm", [P, 16])
        rs = sb("rs", [P, 16])
        half = sb("half", [P, 16])
        hsc = sb("hsc", [P, RET_HEADS, 8])
        hs = sb("hs", [P, 8])
        gqk = sb("gqk", [P, 2, DH])
        dng = sb("dng", [P, 1])
        lam = sb("lam", [P, 8])
        nmx = sb("nmx", [P, 2, 2])
        den = sb("den", [P, 2, 2])
        rd = sb("rd", [P, 2, 2])
        sel = sb("sel", [P, P], BF16)
        small = sb("small", [P, 32])

        def F(off, *shape):
            n = 1
            for s in shape:
                n *= s
            v = ar[:, off:off + n]
            if len(shape) == 1:
                return v
            names = "abc"[:len(shape)]
            return v.rearrange("p (%s) -> p %s" % (" ".join(names), " ".join(names)),
                               **{names[k]: shape[k] for k in range(len(shape) - 1)})

        ps = ctx.enter_context(nc.psum_tensor("ps", [P, 8, 512], F32))
        psf = ps[:, :, :].rearrange("p b n -> p (b n)")
        ident = cst[:, C_ID:C_ID + P]

        s_const = sem("s_const")
        s_cvec = sem("s_cvec")
        s_small = sem("s_small")
        s_x = sem("s_x")
        s_bmod = sem("s_bmod")
        raw_loaded = [sem(f"raw_loaded{k}") for k in range(NRAW)]
        mod_stored = sem("mod_stored")
        mod_cols = sem("mod_cols")
        s_init = sem("s_init")
        hi_made = sem("hi_made")
        lo_made = sem("lo_made")
        w_used = sem("w_used")
        mod_used = sem("mod_used")
        e_loaded = [sem(f"e_loaded{k}") for k in range(ERAW)]
        e_hi = sem("e_hi")
        e_lo = sem("e_lo")
        e_used = sem("e_used")
        dve_pre = sem("dve_pre")
        pool_pre = sem("pool_pre")
        c_tanh = sem("c_tanh")
        c_silu = sem("c_silu")
        mod_rows = sem("mod_rows")
        x_sq = sem("x_sq")
        x_rstd = sem("x_rstd")
        x_normed = sem("x_normed")
        h_turned = sem("h_turned")
        h_hi = sem("h_hi")
        h_lo = sem("h_lo")
        mod_vec = sem("mod_vec")
        pre_done = sem("pre_done")
        r_head = sem("r_head")
        r_exp = sem("r_exp")
        r_arg = sem("r_arg")
        r_step = sem("r_step")
        qk_out = sem("qk_out")
        rope_done = sem("rope_done")
        v_out = sem("v_out")
        g_tanh = sem("g_tanh")
        g_out = sem("g_out")
        sc_done = sem("sc_done")
        pt_done = sem("pt_done")
        o_done = sem("o_done")
        o_sq = sem("o_sq")
        o_rstd = sem("o_rstd")
        pool_r = sem("pool_r")
        y_done = sem("y_done")
        yt_done = sem("yt_done")
        yt_hi = sem("yt_hi")
        yt_lo = sem("yt_lo")
        br_done = sem("br_done")
        br_out = sem("br_out")
        gg_done = sem("gg_done")
        gg_tanh = sem("gg_tanh")
        gg_out = sem("gg_out")
        accr_stored = sem("accr_stored")
        accr_back = sem("accr_back")
        q_raw = sem("q_raw")
        q_sum = sem("q_sum")
        q_rstd = sem("q_rstd")
        q_ready = sem("q_ready")
        q_turned = sem("q_turned")
        q_out = sem("q_out")
        dv_out = sem("dv_out")
        d_step = sem("d_step")
        pool_d = sem("pool_d")
        s_middle = sem("s_middle")
        s_done = sem("s_done")
        mx_done = sem("mx_done")
        p_done = sem("p_done")
        a_done = sem("a_done")
        at_turned = sem("at_turned")
        at_out = sem("at_out")
        ov_done = sem("ov_done")
        ob_out = sem("ob_out")
        ob_sum = sem("ob_sum")
        ob_rstd = sem("ob_rstd")
        yd_done = sem("yd_done")
        yd_turned = sem("yd_turned")
        yd_hi = sem("yd_hi")
        yd_lo = sem("yd_lo")
        bd_done = sem("bd_done")
        bd_out = sem("bd_out")
        m_sum = sem("m_sum")
        m_hi = sem("m_hi")
        m_lo = sem("m_lo")
        vec2 = sem("vec2")
        x_again = sem("x_again")
        xn_done = sem("xn_done")
        tail = sem("tail")
        n2_sq = sem("n2_sq")
        n2_rstd = sem("n2_rstd")
        pool_t = sem("pool_t")
        n2_done = sem("n2_done")
        h2_stored = [sem(f"h2_stored{k}") for k in range(2)]
        h2_turned = sem("h2_turned")
        h2_out = sem("h2_out")
        lg_done = sem("lg_done")
        m_ready = sem("m_ready")
        pos_done = sem("pos_done")
        g_exp = sem("g_exp")
        g_arg = sem("g_arg")
        route_ready = sem("route_ready")
        cnt_done = sem("cnt_done")
        flag_ready = sem("flag_ready")
        opos_done = sem("opos_done")
        oh_ready = sem("oh_ready")
        items_done = sem("items_done")
        items_ready = sem("items_ready")
        listed = sem("listed")
        list_back = sem("list_back")
        b_loaded = sem("b_loaded")
        b_ready = sem("b_ready")
        pool_m = sem("pool_m")
        pool_tick = sem("pool_tick")
        acc_zeroed = sem("acc_zeroed")
        gathered = sem("gathered")
        xt_turned = sem("xt_turned")
        xt_hi = sem("xt_hi")
        xt_lo = sem("xt_lo")
        sel_ready = sem("sel_ready")
        sel_used = sem("sel_used")
        cur_ready = sem("cur_ready")
        glu_min = sem("glu_min")
        glu_tanh = sem("glu_tanh")
        act_done = sem("act_done")
        moe_step = sem("moe_step")
        act_turned = sem("act_turned")
        act_hi = sem("act_hi")
        act_lo = sem("act_lo")
        y_out = sem("y_out")
        y_added = sem("y_added")
        acc_back = sem("acc_back")
        res_ready = sem("res_ready")
        stored = sem("stored")
        e_all = sem("e_all")

        hh = [h[:, :, :].rearrange("p a b -> p (a b)").rearrange("p (s k n) -> p s k n", s=3, k=KH) for h in (hhi, hlo)]
        e_raw = [raw[:, k, :, :] for k in range(NRAW)] + [F(A_EW + k * KH * COL, KH, COL) for k in range(2)]
        e_whi = [whi[:, 0, :, :], whi[:, 1, :, :], hh[0][:, 0], hh[0][:, 1]]
        e_wlo = [wlo[:, 0, :, :], wlo[:, 1, :, :], hh[1][:, 0], hh[1][:, 1]]

        items_i = sb("items_i", [1, 2 * ITEMS], I32)
        count_i = sb("count_i", [1, 2], I32)
        cur = sb("cur", [P, 2], I32)
        nxt = sb("nxt", [P, 2], I32)
        lamt = F(A_GAP, 4, DH)
        linit = F(A_GAP + 4 * DH, N_EXPERTS, 2).bitcast(I32)
        lgt = F(A_GAP + 4 * DH + 2 * N_EXPERTS, 4, 8)
        lgx = F(A_GAP + 4 * DH + 2 * N_EXPERTS + 32, 8)
        rt = [A_RT]

        def R(*shape):
            n = 1
            for x in shape:
                n *= x
            rt[0] += n
            assert rt[0] <= A_WORDS
            return F(rt[0] - n, *shape)

        rw = R(KC, N_EXPERTS)
        rb = R(N_EXPERTS)
        topi = R(LT, 8).bitcast(U32)
        topv = R(LT, 8)
        topf = R(LT, 8)
        gate = R(LT, TOP_K)
        gsum = R(LT, 2)
        logit = R(LT, N_EXPERTS)
        onehot = R(LT * TOP_K, N_EXPERTS)
        mask3 = R(LT, 3 * N_EXPERTS)
        slot = R(LT * TOP_K)
        junk32 = R(N_EXPERTS)
        lrow = R(LT * TOP_K).bitcast(I32)
        lval = R(LT * TOP_K, 2).bitcast(I32)
        listsb = R(4 * N_EXPERTS, 2).bitcast(I32)
        allone = R(P)

        block = ctx.enter_context(nc.Block())

        def act_gate(act, hi, used, base, done):
            per = 0
            for cg in range(2):
                hi(base, per, 0, 2 * cg + 2)
                hi(base, per, 0, 2 * cg + 3)
                used(base, per, 0, 2 * cg + 1)
                for f in range(4):
                    c = 4 * cg + f
                    if c >= 2:
                        act.wait_ge(gg_out, done + c - 1)
                    act.activation(F(A_TMP if base == GA0 else A_OY, 2, 512)[:, c % 2, :], ps[:, c, :],
                                   ACT.Tanh, scale=0.5).then_inc(gg_tanh, 1)

        def bias_thirds(dve, tl, bias):
            V = nc.vector
            r1 = F(A_BR, D)
            dve.wait_ge(b_loaded, 32)
            for c in range(3):
                cols = slice(c * 1024, (c + 1) * 1024)
                src = F(A_BSRC, 3 * D)[0:32, cols]
                tl.did(V.tensor_copy(bias[0:32, cols], src))
                tl.wait()
                tl.did(V.tensor_tensor(r1[0:32, :], src, bias[0:32, cols], ALU.subtract))
                tl.wait()
                tl.did(V.tensor_copy(bias[32:64, cols], r1[0:32, :]))
                tl.wait()
                tl.did(V.tensor_copy(src, bias[32:64, cols]))
                tl.wait()
                ins = V.tensor_tensor(bias[64:96, cols], r1[0:32, :], src, ALU.subtract)
                if c < 2:
                    tl.did(ins)
                else:
                    ins.then_inc(b_ready, 1)

        def dve_gate(dve, lo, base, done):
            V = nc.vector
            acc = F(A_ACC, KC, L)
            per = 0
            for j in range(1, 4):
                lo(base, per, 0, j)
                if j == 3:
                    lo(base, per, 0, 4)
                if j % 2 == 1:
                    for f in range(4):
                        c = 2 * (j - 1) + f
                        dve.wait_ge(gg_tanh, done + c + 1)
                        if base == GA0:
                            if c == 0:
                                dve.wait_ge(br_out, KC * RET_HEADS)
                        elif c == 0:
                            dve.wait_ge(bd_out, KC * GROUPS)
                        V.scalar_tensor_tensor(out=acc[:, c, :],
                                               in0=F(A_TMP if base == GA0 else A_OY, 2, 512)[:, c % 2, :], scalar=1.0,
                                               in1=acc[:, c, :], op0=ALU.add, op1=ALU.mult).then_inc(gg_out, 1)

        @block.sync
        def _(sp):
            def load(src, base, per, i, j, cols=COL):
                m = base - RET0 + j - NRAW + 1
                if base == MOD0:
                    if j >= NRAW:
                        sp.wait_ge(mod_used, j - NRAW + 1)
                elif isinstance(i, int) and per * i + base - RET0 + j < NRAW:
                    sp.wait_ge(mod_used, MOD_N - NRAW + j + 1)
                else:
                    sp.wait_ge(hi_made, at(i, per, m))
                    sp.wait_ge(lo_made, at(i, per, m))
                dst = raw[:, j % NRAW, :, :]
                if cols != COL:
                    dst = dst.rearrange("p k (s n) -> p (k s) n", n=cols)
                sp.dma_start(dst, src).then_inc(raw_loaded[j % NRAW], 16)

            def rows(w, r0, c0, n=COL):
                return w[r0:r0 + KH * P, c0:c0 + n].rearrange("(k p) n -> p k n", p=P)

            w_in, w_mod = a["w_in"], a["w_mod"]
            for j in range(NRAW):
                load(rows(w_mod, (j % 2) * KH * P, (j // 2) * COL), MOD0, 0, 0, j)
            for t in range(TT):
                src = a["x"] if t < LT else a["ctx"]
                sp.dma_start(F(A_X, TT, D)[:, t, :], src[(t % LT) * P:(t % LT + 1) * P, :]).then_inc(s_x, 16)
            for j in range(NRAW, MOD_N):
                load(rows(w_mod, (j % 2) * KH * P, (j // 2) * COL), MOD0, 0, 0, j)
            def ret_head(h, js):
                for j in js:
                    if j < 2:
                        load(w_in[:, bass.ds(h * DK + (RQ, RK)[j], DK)].rearrange("(k p) n -> p k n", p=P),
                             RET0, RET_N, h, j, cols=DK)
                    elif j < 6:
                        c0 = RV if j < 4 else RG
                        load(w_in[(j % 2) * KH * P:(j % 2 + 1) * KH * P, bass.ds(h * DV + c0, DV)].rearrange(
                            "(k p) n -> p k n", p=P), RET0, RET_N, h, j)
                    else:
                        load(a["w_br_ret"][bass.ds(h * DV, DV), (j - 6) * COL:(j - 5) * COL].rearrange(
                            "(k p) n -> p k n", p=P), RET0, RET_N, h, j)

            ret_head(0, range(NRAW))
            sp.wait_ge(mod_rows, 12)
            sp.dma_start(mod_d, F(A_BMOD, 6 * D)[0:2, :]).then_inc(mod_stored, 16)
            sp.wait_ge(mod_stored, 16)
            for k, (r, c0) in enumerate([(0, 0), (0, D), (1, 0), (1, D)]):
                sp.dma_start(mcols[:, k, :], mod_d[r, c0:c0 + D].rearrange("(k p) -> p k", p=P),
                             allow_slow_non_contiguous=True).then_inc(mod_cols, 16)
            ret_head(0, range(NRAW, RET_N))
            with sp.Fori(1, RET_HEADS) as h:
                ret_head(h, range(RET_N))
            for j in range(4):
                load(rows(w_in, (j % 2) * KH * P, GA + (j // 2) * COL), GA0, 0, 0, j)

            def diff_group(g, js):
                for j in js:
                    if j < 6:
                        c0 = (DQ, DKK, DVV)[j // 2]
                        load(w_in[(j % 2) * KH * P:(j % 2 + 1) * KH * P, bass.ds(g * COL + c0, COL)].rearrange(
                            "(k p) n -> p k n", p=P), DIFF0, DIFF_N, g, j)
                    else:
                        load(a["w_br_diff"][bass.ds(g * COL, COL), (j - 6) * COL:(j - 5) * COL].rearrange(
                            "(k p) n -> p k n", p=P), DIFF0, DIFF_N, g, j)

            with sp.Fori(0, GROUPS) as g:
                diff_group(g, range(DIFF_N))
            for j in range(4):
                load(rows(w_in, (j % 2) * KH * P, GB + (j // 2) * COL), GB0, 0, 0, j)
            for j in range(4):
                load(rows(a["w_out"], (j % 2) * KH * P, (j // 2) * COL), OUT0, 0, 0, j)
            sp.wait_ge(bd_out, 16)
            sp.wait_ge(accr_stored, 16)
            sp.dma_start(F(A_ACC2, 4096), accr_d).then_inc(accr_back, 16)
            sp.wait_ge(gg_out, 16)
            for t in range(LT):
                sp.dma_start(F(A_XN, LT, D)[:, t, :], a["x"][t * P:(t + 1) * P, :]).then_inc(x_again, 16)
            for off, src in ((A_GFB, mod_d[0:1, 5 * D:6 * D]), (A_GAB, mod_d[0:1, 2 * D:3 * D]),
                             (A_A2B, mod_d[0:1, 4 * D:5 * D]), (A_SH2B, mod_d[0:1, 3 * D:4 * D]),
                             (A_HT, a["norm2_g"])):
                sp.dma_start(F(off, D), src.broadcast_to((P, D))).then_inc(vec2, 16)

            sp.wait_ge(m_lo, KC)
            sp.dma_start(rw[:, :, :], a["router_w"].rearrange("(k p) n -> p k n", p=P)).then_inc(vec2, 16)
            sp.dma_start(rb[:, :], a["router_b"].broadcast_to((P, N_EXPERTS))).then_inc(vec2, 16)

            W1COL = (0, 2, 1, 3)

            def moe_block(e, i, j):
                jj = j % MOE_N
                one = slice(e, e + 1) if isinstance(e, int) else bass.ds(e, 1)
                if jj < 8:
                    src = a["exp_w1"][one, (jj % 2) * KH * P:(jj % 2 + 1) * KH * P,
                                      W1COL[jj // 2] * COL:(W1COL[jj // 2] + 1) * COL]
                else:
                    src = a["exp_w2"][one, (jj - 8) // 2 * KH * P:((jj - 8) // 2 + 1) * KH * P,
                                      (jj % 2) * COL:(jj % 2 + 1) * COL]
                if isinstance(i, int) and j < ERAW:
                    if j < NRAW:
                        sp.wait_ge(hi_made, OUT0 - RET0 + j + 1)
                        sp.wait_ge(lo_made, OUT0 - RET0 + j + 1)
                    else:
                        sp.wait_ge(b_ready, 1)
                else:
                    sp.wait_ge(e_lo, at(i, MOE_N, j - ERAW + 1))
                sp.dma_start(e_raw[j % ERAW], src.rearrange("o (k p) n -> p (o k) n", p=P)).then_inc(
                    e_loaded[j % ERAW], 16)

            for j in range(NRAW):
                moe_block(0, 0, j)
            for t in range(LT):
                sp.wait_ge(n2_done, t + 1)
                sp.dma_start(h2_d[t * P:(t + 1) * P, :], F(A_HT, 2, D)[:, t % 2, :]).then_inc(h2_stored[t % 2], 16)
            for k in range(2):
                sp.wait_ge(h2_stored[k], 16 * LT // 2)
            sp.wait_ge(h2_turned, 2 * LT)
            bsrc = F(A_BSRC, 3 * D)
            sp.dma_start(bsrc[0:N_EXPERTS, 0:2 * D], a["exp_b1"]).then_inc(b_loaded, 16)
            sp.dma_start(bsrc[0:N_EXPERTS, 2 * D:3 * D], a["exp_b2"]).then_inc(b_loaded, 16)
            for j in range(NRAW, MOE_N + ESPL):
                moe_block(j // MOE_N, 0, j)
            with sp.Fori(1, N_EXPERTS - 1) as i:
                for j in range(ESPL, MOE_N):
                    moe_block(i, i, j)
                for j in range(MOE_N, MOE_N + ESPL):
                    moe_block(i + 1, i, j)
            sp.wait_ge(items_ready, 1)
            n_items = sp.value_load(count_i[0:1, 0:1], min_val=N_EXPERTS, max_val=MAX_BLOCKS)
            with sp.Fori(N_EXPERTS - 1, MAX_BLOCKS) as i:
                with sp.If(i < n_items):
                    e = sp.value_load(items_i[0:1, bass.ds(i + ITEMS, 1)], min_val=0, max_val=N_EXPERTS - 1)
                    e1 = sp.value_load(items_i[0:1, bass.ds(i + ITEMS + 1, 1)], min_val=0, max_val=N_EXPERTS - 1)
                    for j in range(ESPL, MOE_N):
                        moe_block(e, i, j)
                    for j in range(MOE_N, MOE_N + ESPL):
                        moe_block(e1, i, j)

            sp.wait_ge(e_all, 1)
            for t in range(LT):
                sp.dma_start(F(A_XG if t == 0 else A_Y if t == 1 else A_GS if t == 2 else A_HT, D),
                             acc_d[t * P:(t + 1) * P, :]).then_inc(acc_back, 16)
            for t in range(LT):
                sp.wait_ge(res_ready, t + 1)
                sp.dma_start(a["out"][t * P:(t + 1) * P, :], F(A_XN, LT, D)[:, t, :]).then_inc(stored, 16)
            sp.wait_ge(stored, 16 * LT)

        @block.gpsimd
        def _(pool):
            st = Steps(pool, pool_pre)
            pool.dma_start(cc[:, :, 0:1], a["c"].rearrange("o (k p) -> p k o", p=P),
                           allow_slow_non_contiguous=True).then_inc(s_cvec, 16)
            pool.dma_start(cc[:, :, 1:2], a["c_ctx"].rearrange("(o k p) -> p k o", p=P, o=1),
                           allow_slow_non_contiguous=True).then_inc(s_cvec, 16)
            pool.dma_start(cst[:, :], a["consts"]).then_inc(s_const, 16)
            pool.dma_start(F(A_BMOD, 6 * D)[0:2, :], a["b_mod"].broadcast_to((2, 6 * D))).then_inc(s_bmod, 16)
            pool.dma_start(mcols[:, 4, :], a["norm1_g"].rearrange("o (k p) -> p (o k)", p=P),
                           allow_slow_non_contiguous=True).then_inc(s_small, 16)
            pool.dma_start(lgx[:, :], a["ret_decay_logit"].rearrange("o n -> o n").broadcast_to((P, 8))).then_inc(s_small, 16)
            for h in range(RET_HEADS):
                pool.dma_start(hsc[:, h, 4:8], a["ret_norm_g"][h, :].rearrange("(c p) -> p c", p=P),
                           allow_slow_non_contiguous=True).then_inc(s_small, 16)
            pool.dma_start(gqk[:, 0, :], a["diff_q_norm_g"].broadcast_to((P, DH))).then_inc(s_small, 16)
            pool.dma_start(gqk[:, 1, :], a["diff_k_norm_g"].broadcast_to((P, DH))).then_inc(s_small, 16)
            pool.dma_start(dng[:, :], a["diff_norm_g"].rearrange("o p -> p o"),
                           allow_slow_non_contiguous=True).then_inc(s_small, 16)
            pool.dma_start(lamt[:, :, :].rearrange("p a b -> p (a b)"),
                           a["diff_lambda"].broadcast_to((P, 4 * DH))).then_inc(s_small, 16)
            pool.memset(half[:, :], -0.5)
            pool.memset(ones[:, :], 1.0)
            st.did(pool.memset(small[:, :], 0.0))
            st.did(pool.memset(linit[:, :, :], 0))
            st.did(pool.memset(cur[:, :], 0))
            st.wait()
            st.did(pool.iota(linit[:, :, 0:1], [[0, N_EXPERTS]], base=L, channel_multiplier=1))
            st.wait()
            for b in range(4):
                pool.dma_start(list_d[b * P * N_EXPERTS:(b + 1) * P * N_EXPERTS, :].rearrange(
                    "(p e) w -> p (e w)", e=N_EXPERTS), linit[:, :, :].rearrange("p e w -> p (e w)")).then_inc(s_init, 16)

            def hold():
                pool.sem_inc(pool_tick, 1)

            def rstd(src, n, mean, st, out=None, m0=0):
                hold()
                st.did(pool.tensor_scalar(sm[:, m0:m0 + n], src, 1.0 / mean, EPS, ALU.mult, ALU.add))
                st.wait()
                return pool.tensor_tensor(out=rs[:, 0:n] if out is None else out, in0=sm[:, m0:m0 + n],
                                          in1=half[:, 0:n], op=ALU.pow)

            pool.wait_ge(x_sq, TT)
            rstd(ss[:, 0:TT], TT, D, st).then_inc(x_rstd, 1)
            with pool.Fori(0, RET_HEADS) as h:
                pool.wait_ge(o_sq, at(h, LT, LT))
                rstd(ss[:, 0:LT], LT, DV, Steps(pool, pool_r, h)).then_inc(o_rstd, 1)
            pool.wait_ge(accr_stored, 16)
            pool.memset(F(A_ACC, 4096), 0.0).then_inc(acc_zeroed, 1)
            with pool.Fori(0, GROUPS) as g:
                for t in range(LT + TT):
                    pool.wait_ge(q_sum, at(g, LT + TT, t + 1))
                    rstd(ss[:, 0:8], 8, DH, Steps(pool, pool_d, at(g, LT + TT + LT, t))).then_inc(q_rstd, 1)
                for t in range(LT):
                    pool.wait_ge(ob_sum, at(g, LT, t + 1))
                    rstd(ss[:, 8:12], HG, 2 * DH, Steps(pool, pool_d, at(g, LT + TT + LT, LT + TT + t)),
                         out=rs[:, 8:12]).then_inc(ob_rstd, 1)
            pool.wait_ge(m_lo, KC)
            pool.memset(allone, 1.0)
            for t in range(LT):
                pool.wait_ge(n2_sq, t + 1)
                rstd(ss[:, t:t + 1], 1, D, Steps(pool, pool_t, t), out=rs[:, t:t + 1], m0=t).then_inc(n2_rstd, 1)
            pool.wait_ge(cnt_done, 1)
            stt = Steps(pool, pool_t, LT)
            stt.did(pool.memset(F(A_XG, D), 0.0))
            stt.wait()
            pool.dma_start(h2_d[L:L + P, :], F(A_XG, D)).then_inc(s_init, 16)
            for t in range(LT + 1):
                pool.dma_start(acc_d[t * P:(t + 1) * P, :], F(A_XG, D)).then_inc(s_init, 16)
            pool.wait_ge(route_ready, 1)
            pool.wait_ge(s_init, 16 * (4 + 2 + LT))
            for n in range(LT * TOP_K):
                pool.indirect_dma_start(list_d, bass.IndirectOffsetOnAxis(ap=lrow[:, n:n + 1], axis=0),
                                        lval[:, n, :], None).then_inc(listed, 16)
            pool.wait_ge(listed, 16 * LT * TOP_K)
            pool.dma_start(listsb[:, :, :].rearrange("p (b e) w -> p b (e w)", b=4),
                           list_d.rearrange("(b p e) w -> p b (e w)", p=P, e=N_EXPERTS)).then_inc(list_back, 16)
            pool.wait_ge(items_ready, 1)
            pool.wait_ge(list_back, 16)
            n_items = pool.value_load(count_i[0:1, 0:1], min_val=N_EXPERTS, max_val=MAX_BLOCKS)

            def gather():
                pool.indirect_dma_start(F(A_XG, D), None, h2_d,
                                        bass.IndirectOffsetOnAxis(ap=nxt[:, 0:1], axis=0)).then_inc(gathered, 16)

            pool.tensor_copy(nxt[:, :], listsb[:, 0, :]).then_inc(pool_m, 1)
            eye3 = cst[0:96, C_EYE3:C_EYE3 + N_EXPERTS]
            pool.tensor_copy(sel[0:96, :], eye3[:, 0:1].broadcast_to((96, P))).then_inc(sel_ready, 1)
            pool.wait_ge(pool_m, 1)
            for k in range(2):
                pool.wait_ge(h2_stored[k], 16 * LT // 2)
            gather()
            with pool.Fori(0, MAX_BLOCKS) as i:
                with pool.If(i < n_items):
                    code = pool.value_load(items_i[0:1, bass.ds(i, 1)], min_val=0, max_val=4 * N_EXPERTS - 1)
                    code1 = pool.value_load(items_i[0:1, bass.ds(i + 1, 1)], min_val=0, max_val=4 * N_EXPERTS - 1)
                    e1 = pool.value_load(items_i[0:1, bass.ds(i + ITEMS + 1, 1)], min_val=0, max_val=N_EXPERTS - 1)
                    pool.tensor_copy(cur[:, :], listsb[:, bass.ds(code, 1), :].rearrange(
                        "p o w -> p (o w)")).then_inc(cur_ready, 1)
                    pool.wait_ge(xt_turned, at(i, 2, 2))
                    pool.wait_ge(gathered, at(i, 16, 16))
                    hold()
                    pool.tensor_copy(nxt[:, :], listsb[:, bass.ds(code1, 1), :].rearrange(
                        "p o w -> p (o w)")).then_inc(pool_m, 1)
                    pool.wait_ge(pool_m, at(i, 1, 2))
                    hold()
                    gather()
                    pool.wait_ge(sel_used, at(i, 1, 1))
                    hold()
                    pool.tensor_copy(sel[0:96, :], cst[0:96, bass.ds(e1 + C_EYE3, 1)].broadcast_to(
                        (96, P))).then_inc(sel_ready, 1)
                    pool.wait_ge(y_out, at(i, 2, 4))
                    hold()
                    pool.indirect_dma_start(acc_d, bass.IndirectOffsetOnAxis(ap=cur[:, 0:1], axis=0),
                                            F(A_Y, D), None, compute_op=ALU.add).then_inc(y_added, 16)
                    pool.wait_ge(y_added, at(i, 16, 16))
                    hold()
            pool.wait_ge(gathered, n_items * 16 + 16)
            hold()
            pool.memset(cur[:, :], 0).then_inc(e_all, 1)

        @block.scalar
        def _(act):
            def hi(base, per, i, j):
                s = j % NRAW
                if not (isinstance(i, int) and per * i + base + j - RET0 < NSPL):
                    act.wait_ge(w_used, at(i, per, base - RET0 + j - NSPL + 1))
                act.wait_ge(raw_loaded[s], at(i, 16 * per // NRAW, 16 * (base // NRAW + j // NRAW + 1)))
                act.activation(whi[:, j % NSPL, :, :], raw[:, s, :, :], ACT.Copy).then_inc(hi_made, 1)

            act.wait_ge(s_cvec, 32)
            act.activation(ct[:, :, :], cc[:, :, :], ACT.Tanh, scale=0.5).then_inc(c_tanh, 1)
            act.wait_ge(r_arg, 1)
            act.activation(lgt[:, 1, :], lgt[:, 0, :], ACT.Exp).then_inc(r_exp, 1)
            act.activation(lam[:, 2:4], lam[:, 0:2], ACT.Exp).then_inc(r_exp, 1)
            for t in range(TT):
                act.wait_ge(s_x, 16 * TT)
                if t:
                    act.wait_ge(x_sq, t)
                act.activation(F(A_SQ, D), F(A_X, TT, D)[:, t, :], ACT.Square,
                               accum_out=ss[:, t:t + 1]).then_inc(x_sq, 1)
            act.wait_ge(mod_vec, 1)
            for k in range(KC):
                act.wait_ge(h_turned, k + 1)
                act.activation(hhi[:, k, 0:L], ps[:, 2 * (k % 4), :], ACT.Identity,
                               bias=mcols[:, 0, k:k + 1], scale=mcols[:, 1, k:k + 1]).then_inc(h_hi, 1)
                act.activation(hhi[:, k, L:T], ps[:, 2 * (k % 4) + 1, 0:C], ACT.Identity,
                               bias=mcols[:, 2, k:k + 1], scale=mcols[:, 3, k:k + 1]).then_inc(h_hi, 1)
            hi(RET0, RET_N, 0, 0)
            hi(RET0, RET_N, 0, 1)

            def used(base, per, i, j):
                act.wait_ge(w_used, at(i, per, base - RET0 + j + 1))

            with act.Fori(0, RET_HEADS) as h:
                B = (RET0, RET_N, h)
                act.wait_ge(r_head, at(h, 3, 3))
                act.activation(F(A_DEC, 1536)[:, 0:WIN], F(A_DEC, 1536)[:, 0:WIN], ACT.Exp).then_inc(r_exp, 1)
                act.activation(F(A_DEC, 1536)[:, WIN:WIN + 640], cst[:, C_WIN + 256:C_WIN + WIN], ACT.Exp,
                               scale=hs[:, 0:1], bias=hs[:, 2:3]).then_inc(r_exp, 1)
                act.activation(F(A_TMP, 1024)[:, 0:640], cst[:, C_WIN + 256:C_WIN + WIN], ACT.Exp,
                               scale=hs[:, 1:2], bias=hs[:, 3:4]).then_inc(r_exp, 1)
                hi(*B, 2)
                hi(*B, 3)
                used(*B, 1)
                rawqk = F(A_RAWQK, 4, L)
                for f in range(4):
                    act.activation(rawqk[:, f, :], ps[:, f, :], ACT.Copy,
                                   scale=DK ** -0.5 if f < 2 else 1.0).then_inc(qk_out, 1)
                act.activation(F(A_KT, 2, T)[:, :, L:T], ps[:, 4, :].rearrange("p (c n) -> p c n", c=2),
                               ACT.Copy).then_inc(qk_out, 1)
                hi(*B, 4)
                hi(*B, 5)
                used(*B, 3)
                for t in range(TT):
                    act.activation(F(A_V, TT, DV)[:, t, :], ps[:, (5 + t) % 8, :], ACT.Copy).then_inc(v_out, 1)
                hi(*B, 6)
                hi(*B, 7)
                used(*B, 5)
                for t in range(LT):
                    act.activation(F(A_GATE, LT, DV)[:, t, :], ps[:, 3 + t, :], ACT.Tanh,
                                   scale=0.5).then_inc(g_tanh, 1)
                for t in range(LT):
                    act.wait_ge(o_done, at(h, LT, t + 1))
                    if t:
                        act.wait_ge(o_sq, at(h, LT, t))
                    act.activation(F(A_TMP, L), ps[:, (5 + t) % 8, :], ACT.Square,
                                   accum_out=ss[:, t:t + 1]).then_inc(o_sq, 1)
                for c in range(4):
                    act.wait_ge(yt_done, at(h, LT, LT))
                    act.activation(yhi[:, c, :], ps[:, 1 + c, :], ACT.Identity,
                                   scale=hs[:, 4 + c:5 + c]).then_inc(yt_hi, 1)
                hi(*B, 8)
                hi(*B, 9)
            act_gate(act, hi, used, GA0, 0)
            act.wait_ge(s_init, 16 * 4)
            act.wait_ge(gg_out, KC)
            act.dma_start(accr_d, F(A_ACC, 4096)).then_inc(accr_stored, 16)

            with act.Fori(0, GROUPS) as g:
                B = (DIFF0, DIFF_N, g)
                hi(*B, 2)
                hi(*B, 3)
                rawt = F(A_PROB, TT, 512)

                def tile_out(n, bank):
                    act.activation(rawt[:, n % TT, :], ps[:, bank, :], ACT.Copy).then_inc(q_raw, 1)

                used(*B, 1)
                for t in range(LT):
                    tile_out(t, t)
                hi(*B, 4)
                hi(*B, 5)
                used(*B, 3)
                for t in range(TT):
                    n = LT + t
                    if n >= TT:
                        q = n - TT
                        act.wait_ge(q_turned, at(g, LT + TT, q + 1))
                        act.activation(F(A_DQT, HG, L)[:, :, q * P:(q + 1) * P],
                                       ps[:, 2 + q % 2, :].rearrange("p (c n) -> p c n", c=HG),
                                       ACT.Copy).then_inc(q_out, 1)
                    tile_out(n, (4 + t) % 8)
                hi(*B, 6)
                hi(*B, 7)
                used(*B, 5)
                for t in range(TT):
                    act.activation(F(A_DV, TT, 512)[:, t, :], ps[:, (4 + t) % 8, :],
                                   ACT.Copy).then_inc(dv_out, 1)
                for t in range(TT):
                    act.wait_ge(q_turned, at(g, LT + TT, LT + t + 1))
                    act.activation(F(A_DKT, HG, T)[:, :, t * P:(t + 1) * P],
                                   ps[:, 2 + t % 2, :].rearrange("p (c n) -> p c n", c=HG),
                                   ACT.Copy).then_inc(q_out, 1)
                NU = LT * HG

                def softmax(u):
                    act.wait_ge(mx_done, at(g, NU, u + 1))
                    for s in range(2):
                        act.activation(F(A_PROB, 2, 2, T)[:, u % 2, s, :],
                                       psf[:, (u % 2) * 1536 + s * T:(u % 2) * 1536 + (s + 1) * T],
                                       ACT.Exp, bias=nmx[:, u % 2, s:s + 1], scale=DH ** -0.5,
                                       accum_out=den[:, u % 2, s:s + 1]).then_inc(p_done, 1)

                def turned_out(u):
                    act.wait_ge(at_turned, at(g, NU, u + 1))
                    act.activation(F(A_AT, 2, T)[:, u % 2, :], psf[:, (u % 2) * 1536:(u % 2) * 1536 + T],
                                   ACT.Copy).then_inc(at_out, 1)

                def y_high(qt):
                    act.wait_ge(yd_turned, at(g, LT, qt + 1))
                    act.activation(yhi[:, :, qt * P:(qt + 1) * P],
                                   ps[:, 6 + qt % 2, :].rearrange("p (c n) -> p c n", c=HG),
                                   ACT.Identity, scale=dng[:, 0:1]).then_inc(yd_hi, 1)

                softmax(0)
                for u in range(NU):
                    turned_out(u)
                    if u + 1 < NU:
                        softmax(u + 1)
                    if u % HG == 2 and u > HG:
                        y_high(u // HG - 1)
                y_high(LT - 1)
                hi(*B, 8)
                hi(*B, 9)
            act_gate(act, hi, used, GB0, 8)

            for c in range(KC):
                act.wait_ge(m_sum, c + 1)
                act.activation(hhi[:, c, 0:L], F(A_ACC, KC, L)[:, c, :], ACT.Copy, scale=0.5).then_inc(m_hi, 1)
            for j in range(2, 4):
                hi(OUT0, 0, 0, j)
            for t in range(LT):
                act.wait_ge(xn_done, LT + t + 1)
                if t:
                    act.wait_ge(n2_sq, t)
                act.activation(F(A_ACC2, D), F(A_XN, LT, D)[:, t, :], ACT.Square,
                               accum_out=ss[:, t:t + 1]).then_inc(n2_sq, 1)
            act.wait_ge(n2_sq, LT)
            for t in range(LT):
                for q in range(2):
                    act.wait_ge(h2_turned, 2 * t + q + 1)
                    act.activation(F(A_H2T, KC, L)[:, 4 * q:4 * q + 4, t * P:(t + 1) * P],
                                   ps[:, q, :].rearrange("p (c n) -> p c n", c=4), ACT.Copy).then_inc(h2_out, 1)
            act.wait_ge(g_arg, LT)
            for t in range(LT):
                act.activation(gate[:, t, :], topv[:, t, 4:8], ACT.Exp,
                               accum_out=gsum[:, t, 0:1]).then_inc(g_exp, 1)
            def hi_e(i, j):
                if isinstance(i, int):
                    act.wait_ge(w_used, MOE0 - RET0)
                else:
                    act.wait_ge(e_used, at(i, MOE_N, j - ESPL + 1))
                act.wait_ge(e_loaded[j % ERAW], at(i, 16 * MOE_N // ERAW, 16 * (j // ERAW + 1)))
                act.activation(e_whi[j % ESPL], e_raw[j % ERAW], ACT.Copy).then_inc(e_hi, 1)

            xthi = yhi[:, 0:2, :].rearrange("p a (k n) -> p (a k) n", n=P)
            acthi = ylo[:, 0:2, :].rearrange("p a (k n) -> p (a k) n", n=P)

            def x_high(n):
                for q in range(2):
                    act.wait_ge(xt_turned, n + q)
                    act.activation(xthi[:, 4 * q:4 * q + 4, :], ps[:, q, :].rearrange("p (c n) -> p c n", c=4),
                                   ACT.Copy).then_inc(xt_hi, 1)

            for j in range(ESPL):
                hi_e(0, j)
            act.wait_ge(items_ready, 1)
            n_items = act.value_load(count_i[0:1, 0:1], min_val=N_EXPERTS, max_val=MAX_BLOCKS)
            x_high(1)
            act.sem_inc(y_out, 2)
            with act.Fori(0, MAX_BLOCKS) as i:
                with act.If(i < n_items):
                    def tanh(hf):
                        act.wait_ge(glu_min, at(i, 2, hf + 1))
                        act.activation(F(A_TH, COL), F(A_GS, COL), ACT.Tanh, scale=0.5 * ALPHA).then_inc(glu_tanh, 1)

                    def act_high(hf):
                        act.wait_ge(act_turned, at(i, 2, hf + 1))
                        act.activation(acthi[:, 4 * hf:4 * hf + 4, :],
                                       ps[:, 2 * hf, :].rearrange("p (c n) -> p c n", c=4),
                                       ACT.Copy, scale=0.5).then_inc(act_hi, 1)

                    hi_e(i, 4)
                    tanh(0)
                    for j in range(5, 9):
                        hi_e(i, j)
                    tanh(1)
                    act_high(0)
                    for j in range(9, 12):
                        hi_e(i, j)
                    x_high(at(i, 2, 3))
                    hi_e(i, 12)
                    hi_e(i, 13)
                    act_high(1)
                    hi_e(i, 14)
                    hi_e(i, 15)
                    act.wait_ge(cur_ready, at(i, 1, 1))
                    act.wait_ge(e_used, at(i, MOE_N, MOE_N))
                    for c in range(2):
                        act.activation(F(A_Y, D)[:, c * COL:(c + 1) * COL], ps[:, 6 + c, :], ACT.Copy,
                                       scale=cur[:, 1:2].bitcast(F32)).then_inc(y_out, 1)

        @block.vector
        def _(dve):
            V = nc.vector
            st = Steps(dve, dve_pre)

            def lo(base, per, i, j):
                s = j % NRAW
                dve.wait_ge(hi_made, at(i, per, base - RET0 + j + 1))
                dve.wait_ge(raw_loaded[s], at(i, 16 * per // NRAW, 16 * (base // NRAW + j // NRAW + 1)))
                V.tensor_tensor(wlo[:, j % NSPL, :, :], raw[:, s, :, :], whi[:, j % NSPL, :, :].bitcast(F32),
                                ALU.subtract).then_inc(lo_made, 1)

            def branch_ready(base, per, i, done, f):
                if f % 4 == 3:
                    dve.wait_ge(w_used, at(i, per, base - RET0 + 6 + f // 4 + 1))
                else:
                    dve.wait_ge(done, at(i, 6, f // 4 * 3 + f % 4 + 1))

            dve.wait_ge(c_tanh, 1)
            st.did(V.scalar_tensor_tensor(out=ct[:, :, :], in0=ct[:, :, :], scalar=1.0, in1=cc[:, :, :],
                                          op0=ALU.add, op1=ALU.mult))
            st.wait()
            V.tensor_scalar(ct[:, :, :], ct[:, :, :], 0.5, None, ALU.mult).then_inc(c_silu, 1)
            dve.wait_ge(s_small, 16 * 10)
            st.did(V.tensor_scalar(lgt[:, 2, :], lgx[:, :], -1.0, None, ALU.mult))
            st.wait()
            st.did(V.tensor_tensor(lgt[:, 0, :], lgx[:, :], lgt[:, 2, :], ALU.min))
            st.did(V.tensor_tensor(lamt[:, 0:4:2, :], lamt[:, 0:4:2, :], lamt[:, 1:4:2, :], ALU.mult))
            st.wait()
            V.tensor_reduce(lam[:, 0:2], lamt[:, 0:4:2, :], AX.X, ALU.add).then_inc(r_arg, 1)
            dve.wait_ge(r_exp, 2)
            st.did(V.tensor_scalar(lgt[:, 2, :], lgt[:, 1, :], 2.0, None, ALU.add))
            st.wait()
            st.did(V.reciprocal(lgt[:, 3, :], lgt[:, 2, :]))
            st.wait()
            st.did(V.tensor_tensor(lgt[:, 1, :], lgt[:, 1, :], lgt[:, 3, :], ALU.mult))
            st.wait()
            st.did(V.tensor_tensor(lgt[:, 2, :], lgt[:, 1, :], lgt[:, 1, :], ALU.mult))
            st.wait()
            st.did(V.tensor_scalar(lgt[:, 3, :], lgt[:, 2, :], 2.0 / 17, 2.0 / 15, ALU.mult, ALU.add))
            for n in (13, 11, 9, 7, 5, 3, 1):
                st.wait()
                st.did(V.tensor_tensor(lgt[:, 3, :], lgt[:, 3, :], lgt[:, 2, :], ALU.mult))
                st.wait()
                st.did(V.tensor_scalar(lgt[:, 3, :], lgt[:, 3, :], 2.0 / n, None, ALU.add))
            st.wait()
            st.did(V.tensor_tensor(lgt[:, 3, :], lgt[:, 3, :], lgt[:, 1, :], ALU.mult))
            st.did(V.tensor_scalar(lgt[:, 0, :], lgx[:, :], 0.0, None, ALU.min))
            st.wait()
            st.did(V.tensor_tensor(lgt[:, 0, :], lgt[:, 0, :], lgt[:, 3, :], ALU.subtract))
            st.wait()
            lf = lgt[:, 0, 0:RET_HEADS].unsqueeze(2)
            lb = lgt[:, 0, RET_HEADS:8].unsqueeze(2)
            st.did(V.tensor_scalar(hsc[:, :, 0:1], lf, 1.0, None, ALU.mult))
            st.did(V.tensor_scalar(hsc[:, :, 1:2], lb, -1.0, None, ALU.mult))
            st.did(V.tensor_scalar(hsc[:, :, 2:3], lf, float(C), None, ALU.mult))
            st.did(V.tensor_scalar(hsc[:, :, 3:4], lb, float(L), None, ALU.mult))
            st.did(V.tensor_scalar(hsc[:, :, 4:8], hsc[:, :, 4:8], 0.5, None, ALU.mult))
            st.did(V.tensor_scalar(dng[:, :], dng[:, :], 1.0 - LAMBDA_INIT, None, ALU.mult))
            st.did(V.tensor_tensor(lam[:, 4:5], lam[:, 3:4], lam[:, 2:3], ALU.subtract))
            st.wait()
            st.did(V.tensor_scalar(lam[:, 5:6], lam[:, 4:5], -LAMBDA_INIT, None, ALU.add))
            dve.wait_ge(s_const, 16)

            dve.wait_ge(s_bmod, 16)
            bm = F(A_BMOD, 12, COL)
            for c in range(12):
                dve.wait_ge(mod_used, 2 * c + 2)
                V.tensor_tensor(bm[0:2, c, :], ps[0:2, c % 8, :], bm[0:2, c, :], ALU.add).then_inc(mod_rows, 1)
            dve.wait_ge(x_rstd, 1)
            for t in range(TT):
                V.tensor_scalar(F(A_X, TT, D)[:, t, :], F(A_X, TT, D)[:, t, :], rs[:, t:t + 1], None,
                                ALU.mult).then_inc(x_normed, 1)
            dve.wait_ge(mod_cols, 64)
            st.did(V.scalar_tensor_tensor(out=mcols[:, 1, :], in0=mcols[:, 1, :], scalar=1.0, in1=mcols[:, 4, :],
                                          op0=ALU.add, op1=ALU.mult))
            V.scalar_tensor_tensor(out=mcols[:, 3, :], in0=mcols[:, 3, :], scalar=1.0, in1=mcols[:, 4, :],
                                   op0=ALU.add, op1=ALU.mult).then_inc(mod_vec, 1)
            dve.wait_ge(mod_vec, 1)
            tm = F(A_SQ, 2, COL)
            for k in range(KC):
                for s, (n0, n1) in enumerate(((0, L), (L, T))):
                    dve.wait_ge(h_hi, 2 * k + s + 1)
                    if k:
                        dve.wait_ge(h_lo, 2 * (k - 1) + s + 1)
                    st.did(V.tensor_scalar(tm[:, s, 0:n1 - n0], ps[:, 2 * (k % 4) + s, 0:n1 - n0],
                                           mcols[:, 2 * s + 1, k:k + 1], mcols[:, 2 * s, k:k + 1], ALU.mult, ALU.add))
                    st.wait()
                    V.tensor_tensor(hlo[:, k, n0:n1], tm[:, s, 0:n1 - n0], hhi[:, k, n0:n1].bitcast(F32),
                                    ALU.subtract).then_inc(h_lo, 1)
            acc = F(A_ACC, KC, L)
            st.did(V.memset(acc[:, 0:KC, :], 0.0))
            dve.wait_ge(h_lo, 2 * KC)
            st.wait()
            lo(RET0, RET_N, 0, 0)
            RS = 7
            with dve.Fori(0, RET_HEADS) as h:
                B = (RET0, RET_N, h)
                sr = Steps(dve, r_step, h * RS)
                win = cst[:, C_WIN:C_WIN + WIN]
                dec = F(A_DEC, 1536)
                V.tensor_scalar(hs[:, :], hsc[:, bass.ds(h, 1), :].rearrange("p o n -> p (o n)"), 1.0, None,
                                ALU.mult).then_inc(r_head, 1)
                dve.wait_ge(r_head, at(h, 3, 1))
                sr.did(V.tensor_scalar(dec[:, 0:WIN], win, 0.0, hs[:, 0:1], ALU.max, ALU.mult))
                V.tensor_scalar(F(A_TMP, 1024)[:, 0:WIN], win, 0.0, hs[:, 1:2], ALU.min, ALU.mult).then_inc(r_head, 1)
                sr.wait()
                dve.wait_ge(r_head, at(h, 3, 2))
                V.tensor_tensor(dec[:, 0:WIN], dec[:, 0:WIN], F(A_TMP, 1024)[:, 0:WIN], ALU.add).then_inc(r_head, 1)
                lo(*B, 1)
                dve.wait_ge(r_exp, at(h, 3, 5))
                sr.did(V.tensor_tensor(dec[:, WIN:WIN + 640], dec[:, WIN:WIN + 640], F(A_TMP, 1024)[:, 0:640], ALU.add))
                sr.did(V.tensor_tensor(dec[:, L - P:L], dec[:, L - P:L], ident, ALU.add))
                lo(*B, 2)
                lo(*B, 3)
                rawqk = F(A_RAWQK, 4, L)
                tmp = F(A_TMP, 2, L)
                c0 = C_ROPE_R
                sr.wait()
                for f in range(4):
                    dve.wait_ge(qk_out, at(h, 5, f + 1))
                    if f:
                        dve.wait_ge(rope_done, at(h, 4, f))
                    if f % 2 == 0:
                        cos = cst[:, c0:c0 + GRID_H].unsqueeze(2).broadcast_to((P, GRID_H, GRID_W))
                        sin = cst[:, c0 + GRID_H:c0 + 2 * GRID_H].unsqueeze(2).broadcast_to((P, GRID_H, GRID_W))
                    else:
                        b0 = c0 + 2 * GRID_H
                        cos = cst[:, b0:b0 + GRID_W].unsqueeze(1).broadcast_to((P, GRID_H, GRID_W))
                        sin = cst[:, b0 + GRID_W:b0 + 2 * GRID_W].unsqueeze(1).broadcast_to((P, GRID_H, GRID_W))
                    grid = lambda v: v.rearrange("p (r c) -> p r c", c=GRID_W)
                    V.tensor_tensor(grid(tmp[:, 0, :]), grid(rawqk[:, f, :]), cos, ALU.mult)
                    V.tensor_tensor(grid(tmp[0:64, 1, :]), grid(rawqk[64:128, f, :]), sin[64:128], ALU.mult)
                    sr.did(V.tensor_tensor(grid(tmp[64:128, 1, :]), grid(rawqk[0:64, f, :]), sin[0:64], ALU.mult))
                    sr.wait()
                    dst = F(A_QT, 2, L)[:, f, :] if f < 2 else F(A_KT, 2, T)[:, f - 2, 0:L]
                    V.tensor_tensor(dst, tmp[:, 0, :], tmp[:, 1, :], ALU.add).then_inc(rope_done, 1)
                lo(*B, 4)
                lo(*B, 5)
                lo(*B, 6)
                gt = F(A_GATE, LT, DV)
                for t in range(LT):
                    dve.wait_ge(g_tanh, at(h, LT, t + 1))
                    V.scalar_tensor_tensor(out=gt[:, t, :], in0=gt[:, t, :], scalar=1.0, in1=ps[:, 3 + t, :],
                                           op0=ALU.add, op1=ALU.mult).then_inc(g_out, 1)
                lo(*B, 7)
                sr.wait()
                for m in range(TT):
                    dve.wait_ge(sc_done, at(h, TT, m + 1))
                    w0 = L - P - P * m if m < LT else WIN + P - P * (m - LT)
                    V.tensor_tensor(F(A_RAWQK, TT, L)[:, m, :], ps[:, (7 + m) % 8, :], dec[:, w0:w0 + L],
                                    ALU.mult).then_inc(pt_done, 1)
                dve.wait_ge(o_rstd, at(h, 1, 1))
                dve.wait_ge(g_out, at(h, LT, LT))
                for t in range(LT):
                    V.scalar_tensor_tensor(out=gt[:, t, :], in0=ps[:, (5 + t) % 8, :], scalar=rs[:, t:t + 1],
                                           in1=gt[:, t, :], op0=ALU.mult, op1=ALU.mult).then_inc(y_done, 1)
                for c in range(4):
                    dve.wait_ge(yt_hi, at(h, 4, c + 1))
                    V.scalar_tensor_tensor(out=ylo[:, c, :], in0=ps[:, 1 + c, :], scalar=hs[:, 4 + c:5 + c],
                                           in1=yhi[:, c, :].bitcast(F32), op0=ALU.mult,
                                           op1=ALU.subtract).then_inc(yt_lo, 1)
                for f in range(KC):
                    if f == 4:
                        lo(*B, 8)
                    branch_ready(*B, br_done, f)
                    V.tensor_tensor(acc[:, f, :], acc[:, f, :], ps[:, f, :], ALU.add).then_inc(br_out, 1)
                assert sr.k == RS, sr.k
            dve_gate(dve, lo, GA0, 0)

            sq = F(A_AT, 3, 512)
            with dve.Fori(0, GROUPS) as g:
                B = (DIFF0, DIFF_N, g)
                NQ = LT + TT
                NU = LT * HG
                DS = 8 * 7 + 2 * 2 + 4 * NU + 2 * LT
                sd = Steps(dve, d_step, g * DS)
                lo(*B, 1)
                lo(*B, 2)
                lo(*B, 3)
                rawt = F(A_PROB, TT, 512)

                def norm_rope(n):
                    r = rawt[:, n % TT, :]
                    heads = lambda v: v.rearrange("p (g d) -> p g d", d=DH)
                    is_k, t = (0, n) if n < LT else (1, n - LT)
                    dve.wait_ge(q_raw, at(g, NQ, n + 1))
                    if n:
                        dve.wait_ge(q_ready, at(g, NQ, n))
                    sd.did(V.tensor_tensor(sq[:, 2, :], r, r, ALU.mult))
                    sd.wait()
                    V.tensor_reduce(ss[:, 0:8], heads(sq[:, 2, :]), AX.X, ALU.add).then_inc(q_sum, 1)
                    sd.did(V.tensor_tensor(heads(r), heads(r), gqk[:, is_k, :].unsqueeze(1).broadcast_to((P, 8, DH)),
                                           ALU.mult))
                    sd.wait()
                    if t < LT:
                        tab = cst[:, C_ROPE_D + t * 2 * DH:C_ROPE_D + (t + 1) * 2 * DH]
                        cos = tab[:, 0:DH].unsqueeze(1).broadcast_to((P, 8, DH))
                        V.tensor_tensor(heads(sq[:, 0, :]), heads(r), cos, ALU.mult)
                        halves = lambda v: v.rearrange("p (g s d) -> p g s d", s=2, d=16)
                        sin = tab[:, DH:2 * DH].rearrange("p (a s d) -> p a s d", s=2, d=16)
                        for hf in range(2):
                            for ax in range(2):
                                pick = lambda v, s: v.rearrange("p (g x s d) -> p g x s d", x=2, s=2, d=16)[:, :, ax, s, :]
                                sd.did(V.tensor_tensor(pick(sq[:, 1, :], hf), pick(r, 1 - hf),
                                                       sin[:, ax, hf, :].unsqueeze(1).broadcast_to((P, 8, 16)),
                                                       ALU.mult))
                        sd.wait()
                        sd.did(V.tensor_tensor(r, sq[:, 0, :], sq[:, 1, :], ALU.add))
                        sd.wait()
                    dve.wait_ge(q_rstd, at(g, NQ, n + 1))
                    V.tensor_tensor(heads(r), heads(r), rs[:, 0:8].unsqueeze(2).broadcast_to((P, 8, DH)),
                                    ALU.mult).then_inc(q_ready, 1)

                for n in range(LT):
                    norm_rope(n)
                lo(*B, 4)
                lo(*B, 5)
                for n in range(LT, TT):
                    norm_rope(n)
                lo(*B, 6)
                for n in range(TT, NQ):
                    norm_rope(n)
                lo(*B, 7)

                def biggest(u):
                    dve.wait_ge(s_done, at(g, NU, u + 1))
                    s0 = (u % 2) * 1536
                    sd.did(V.tensor_reduce(nmx[:, u % 2, :], psf[:, s0:s0 + 2 * T].rearrange(
                        "p (s n) -> p s n", s=2), AX.X, ALU.max))
                    sd.wait()
                    V.tensor_scalar(nmx[:, u % 2, :], nmx[:, u % 2, :], -(DH ** -0.5), None, ALU.mult).then_inc(mx_done, 1)

                def combine(u):
                    pr = F(A_PROB, 2, 2, T)[:, u % 2]
                    dve.wait_ge(p_done, at(g, 2 * NU, 2 * u + 2))
                    sd.did(V.reciprocal(rd[:, u % 2, :], den[:, u % 2, :]))
                    sd.wait()
                    sd.did(V.tensor_tensor(rd[:, u % 2, 1:2], rd[:, u % 2, 1:2], lam[:, 5:6], ALU.mult))
                    sd.wait()
                    sd.did(V.tensor_scalar(pr[:, 1, :], pr[:, 1, :], rd[:, u % 2, 1:2], None, ALU.mult))
                    sd.wait()
                    V.scalar_tensor_tensor(out=pr[:, 0, :], in0=pr[:, 0, :], scalar=rd[:, u % 2, 0:1], in1=pr[:, 1, :],
                                           op0=ALU.mult, op1=ALU.add).then_inc(a_done, 1)

                def out_tile(qt):
                    ob = F(A_OY, 2, 512)
                    heads = lambda v: v.rearrange("p (g d) -> p g d", d=2 * DH)
                    dve.wait_ge(ov_done, at(g, NU, HG * qt + HG))
                    sd.did(V.tensor_copy(ob[:, 0, :], ps[:, 6 + qt % 2, :]))
                    sd.wait()
                    if qt:
                        dve.wait_ge(yd_turned, at(g, LT, qt))
                    sd.did(V.tensor_tensor(ob[:, 1, :], ob[:, 0, :], ob[:, 0, :], ALU.mult))
                    sd.wait()
                    V.tensor_reduce(ss[:, 8:12], heads(ob[:, 1, :]), AX.X, ALU.add).then_inc(ob_sum, 1)
                    dve.wait_ge(ob_rstd, at(g, LT, qt + 1))
                    V.tensor_tensor(heads(ob[:, 1, :]), heads(ob[:, 0, :]),
                                    rs[:, 8:12].unsqueeze(2).broadcast_to((P, HG, 2 * DH)), ALU.mult).then_inc(yd_done, 1)

                def y_low(qt):
                    dve.wait_ge(yd_hi, at(g, LT, qt + 1))
                    cols = lambda v: v[:, :, qt * P:(qt + 1) * P]
                    V.scalar_tensor_tensor(out=cols(ylo), in0=ps[:, 6 + qt % 2, :].rearrange("p (c n) -> p c n", c=HG),
                                           scalar=dng[:, 0:1], in1=cols(yhi).bitcast(F32), op0=ALU.mult,
                                           op1=ALU.subtract).then_inc(yd_lo, 1)

                for u in range(NU):
                    biggest(u)
                    combine(u)
                    if u % HG == 1 and u > HG:
                        out_tile(u // HG - 1)
                    if u % HG == 3 and u > HG:
                        y_low(u // HG - 1)
                out_tile(LT - 1)
                y_low(LT - 1)
                dve.wait_ge(acc_zeroed, 1)
                for f in range(KC):
                    if f == 4:
                        lo(*B, 8)
                    branch_ready(*B, bd_done, f)
                    V.tensor_tensor(acc[:, f, :], acc[:, f, :], ps[:, f, :], ALU.add).then_inc(bd_out, 1)
                assert sd.k == DS, sd.k
            dve_gate(dve, lo, GB0, 8)

            tl = Steps(dve, tail)
            dve.wait_ge(accr_back, 16)
            dve.wait_ge(gg_out, 16)
            acc2 = F(A_ACC2, KC, L)
            for c in range(KC):
                V.tensor_tensor(acc[:, c, :], acc[:, c, :], acc2[:, c, :], ALU.add).then_inc(m_sum, 1)
            for c in range(KC):
                dve.wait_ge(m_hi, c + 1)
                V.scalar_tensor_tensor(out=hlo[:, c, 0:L], in0=acc[:, c, :], scalar=0.5, in1=hhi[:, c, 0:L].bitcast(F32),
                                       op0=ALU.mult, op1=ALU.subtract).then_inc(m_lo, 1)
            for j in range(1, 4):
                lo(OUT0, 0, 0, j)
            xn = F(A_XN, LT, D)
            dve.wait_ge(x_again, 16 * LT)
            dve.wait_ge(vec2, 16 * 7)
            tl.did(V.scalar_tensor_tensor(out=F(A_A2B, D), in0=F(A_A2B, D), scalar=1.0, in1=F(A_HT, D),
                                          op0=ALU.add, op1=ALU.mult))
            for c in range(2):
                dve.wait_ge(w_used, OUT0 - RET0 + 2 * c + 2)
                for t in range(LT):
                    tmpx = F(A_TX, 4, COL)[:, t, :]
                    tl.did(V.tensor_tensor(tmpx, ps[:, 4 * c + t, :], F(A_GAB, D)[:, c * COL:(c + 1) * COL], ALU.mult))
                    tl.wait()
                    V.tensor_tensor(xn[:, t, c * COL:(c + 1) * COL], xn[:, t, c * COL:(c + 1) * COL], tmpx,
                                    ALU.add).then_inc(xn_done, 1)
            for t in range(LT):
                ht = F(A_HT, 2, D)[:, t % 2, :]
                dve.wait_ge(n2_rstd, t + 1)
                if t >= 2:
                    dve.wait_ge(h2_turned, 2 * (t - 2) + 2)
                    dve.wait_ge(h2_stored[t % 2], 16 * (t // 2))
                tl.did(V.scalar_tensor_tensor(out=ht, in0=xn[:, t, :], scalar=rs[:, t:t + 1], in1=F(A_A2B, D),
                                              op0=ALU.mult, op1=ALU.mult))
                tl.wait()
                V.tensor_tensor(ht, ht, F(A_SH2B, D), ALU.add).then_inc(n2_done, 1)
            iota = cst[:, C_IOTA:C_IOTA + N_EXPERTS]
            for t in range(LT):
                dve.wait_ge(lg_done, t + 1)
                tl.did(V.tensor_tensor(logit[:, t, :], ps[:, 2 + t % 2, 0:N_EXPERTS], rb[:, :], ALU.add))
                tl.wait()
                tl.did(V.max(topv[:, t, :], logit[:, t, :]))
                tl.wait()
                tl.did(V.max_index(topi[:, t, :], topv[:, t, :], logit[:, t, :]))
                tl.wait()
                tl.did(V.tensor_copy(topf[:, t, :], topi[:, t, :]))
                V.tensor_scalar(topv[:, t, 4:8], topv[:, t, 0:4], topv[:, t, 0:1], None, ALU.subtract).then_inc(g_arg, 1)
                tl.wait()
                for k in range(TOP_K):
                    tl.did(V.tensor_scalar(onehot[:, t * TOP_K + k, :], iota, topf[:, t, k:k + 1], None, ALU.is_equal))
                tl.wait()
                tl.did(V.tensor_tensor(mask3[:, t, 0:32], onehot[:, t * TOP_K, :], onehot[:, t * TOP_K + 1, :], ALU.add))
                tl.did(V.tensor_tensor(mask3[:, t, 32:64], onehot[:, t * TOP_K + 2, :], onehot[:, t * TOP_K + 3, :],
                                       ALU.add))
                tl.wait()
                tl.did(V.tensor_tensor(mask3[:, t, 0:32], mask3[:, t, 0:32], mask3[:, t, 32:64], ALU.add))
                tl.wait()
                tl.did(V.tensor_copy(mask3[:, t, 32:64], mask3[:, t, 0:32]))
                V.tensor_copy(mask3[:, t, 64:96], mask3[:, t, 0:32]).then_inc(m_ready, 1)
            tl.wait()
            for t in range(LT):
                dve.wait_ge(g_exp, t + 1)
                tl.did(V.reciprocal(gsum[:, t, 1:2], gsum[:, t, 0:1]))
            tl.wait()
            lvf = lval[:, :, :].bitcast(F32)
            for t in range(LT):
                tl.did(V.tensor_scalar(lvf[:, t * TOP_K:(t + 1) * TOP_K, 1:2], gate[:, t, :].unsqueeze(2),
                                       gsum[:, t, 1:2], None, ALU.mult))
                tl.did(V.tensor_copy(lval[:, t * TOP_K:(t + 1) * TOP_K, 0:1],
                                     cst[:, C_TOK + t:C_TOK + t + 1].unsqueeze(1).broadcast_to((P, TOP_K, 1))))
            dve.wait_ge(pos_done, LT)
            for t in range(LT):
                for k in range(TOP_K):
                    n = t * TOP_K + k
                    tl.wait()
                    tl.did(V.tensor_tensor_reduce(out=junk32[:, :], in0=onehot[:, n, :], in1=ps[:, 4 + t, 0:N_EXPERTS],
                                                  scale=1.0, scalar=0.0, op0=ALU.mult, op1=ALU.add,
                                                  accum_out=slot[:, n:n + 1]))
            tl.wait()
            tl.did(V.tensor_scalar(slot[:, :], slot[:, :], float(N_EXPERTS), None, ALU.mult))
            tl.wait()
            V.tensor_tensor(lrow[:, :].rearrange("p (t k) -> p t k", k=TOP_K),
                            slot[:, :].rearrange("p (t k) -> p t k", k=TOP_K), topf[:, :, 0:TOP_K],
                            ALU.add).then_inc(route_ready, 1)
            dve.wait_ge(cnt_done, 1)
            V.tensor_scalar(small[0:96, 0:1], ps[0:96, 0, 0:1], cst[0:96, C_THR:C_THR + 1], None,
                            ALU.is_gt).then_inc(flag_ready, 1)
            dve.wait_ge(opos_done, 1)
            tl.did(V.tensor_copy(small[0:96, 1:2], ps[0:96, 0, 0:1]))
            tl.wait()
            dve.wait_ge(flag_ready, 1)
            V.tensor_scalar(small[0:96, 8:8 + OVER + 1], iota[0:96, 0:OVER + 1], small[0:96, 1:2], small[0:96, 0:1],
                            ALU.is_equal, ALU.mult).then_inc(oh_ready, 1)
            dve.wait_ge(items_done, 1)
            for q in range(2):
                tl.did(V.tensor_copy(items_i[0:1, q * ITEMS:q * ITEMS + N_EXPERTS], iota[0:1, :]))
                tl.did(V.tensor_copy(items_i[0:1, q * ITEMS + N_EXPERTS:(q + 1) * ITEMS],
                                     ps[0:1, 0, q * (OVER + 1):(q + 1) * (OVER + 1)]))
            V.tensor_scalar(count_i[0:1, 0:1], ps[0:1, 0, 2 * (OVER + 1):2 * (OVER + 1) + 1], float(N_EXPERTS), None,
                            ALU.add).then_inc(items_ready, 1)
            bias = F(A_BIAS, 1536).bitcast(BF16)
            bias_thirds(dve, tl, bias)
            xthi = yhi[:, 0:2, :].rearrange("p a (k n) -> p (a k) n", n=P)
            xtlo = yhi[:, 2:4, :].rearrange("p a (k n) -> p (a k) n", n=P)
            acthi = ylo[:, 0:2, :].rearrange("p a (k n) -> p (a k) n", n=P)
            actlo = ylo[:, 2:4, :].rearrange("p a (k n) -> p (a k) n", n=P)

            def x_low(n):
                for q in range(2):
                    dve.wait_ge(xt_hi, n + q)
                    V.tensor_tensor(xtlo[:, 4 * q:4 * q + 4, :], ps[:, q, :].rearrange("p (c n) -> p c n", c=4),
                                    xthi[:, 4 * q:4 * q + 4, :].bitcast(F32), ALU.subtract).then_inc(xt_lo, 1)

            def lo_e(i, j):
                dve.wait_ge(e_hi, at(i, MOE_N, j + 1))
                dve.wait_ge(e_loaded[j % ERAW], at(i, 16 * MOE_N // ERAW, 16 * (j // ERAW + 1)))
                V.tensor_tensor(e_wlo[j % ESPL], e_raw[j % ERAW], e_whi[j % ESPL].bitcast(F32),
                                ALU.subtract).then_inc(e_lo, 1)

            for j in range(ESPL):
                lo_e(0, j)
            dve.wait_ge(items_ready, 1)
            n_items = dve.value_load(count_i[0:1, 0:1], min_val=N_EXPERTS, max_val=MAX_BLOCKS)
            x_low(1)
            MS = 4
            with dve.Fori(0, MAX_BLOCKS) as i:
                with dve.If(i < n_items):
                    ms = Steps(dve, moe_step, i * MS)

                    def used(j):
                        dve.wait_ge(e_used, at(i, MOE_N, j + 1))

                    def glu(hf):
                        used(4 * hf + 1)
                        V.tensor_scalar(F(A_GS, COL), ps[:, 2 + 2 * hf, :], LIMIT, None, ALU.min).then_inc(glu_min, 1)

                    def activate(hf):
                        used(4 * hf + 3)
                        ms.did(V.tensor_scalar(F(A_LS, COL), ps[:, 3 + 2 * hf, :], -LIMIT, LIMIT, ALU.max, ALU.min))
                        dve.wait_ge(glu_tanh, at(i, 2, hf + 1))
                        ms.did(V.scalar_tensor_tensor(out=F(A_GS, COL), in0=F(A_TH, COL), scalar=1.0, in1=F(A_GS, COL),
                                                      op0=ALU.add, op1=ALU.mult))
                        ms.wait()
                        V.scalar_tensor_tensor(out=F(A_AC, 2, COL)[:, hf, :], in0=F(A_LS, COL), scalar=1.0,
                                               in1=F(A_GS, COL), op0=ALU.add, op1=ALU.mult).then_inc(act_done, 1)

                    def act_low(hf):
                        dve.wait_ge(act_hi, at(i, 2, hf + 1))
                        V.scalar_tensor_tensor(out=actlo[:, 4 * hf:4 * hf + 4, :],
                                               in0=ps[:, 2 * hf, :].rearrange("p (c n) -> p c n", c=4), scalar=0.5,
                                               in1=acthi[:, 4 * hf:4 * hf + 4, :].bitcast(F32), op0=ALU.mult,
                                               op1=ALU.subtract).then_inc(act_lo, 1)

                    lo_e(i, 4)
                    glu(0)
                    lo_e(i, 5)
                    lo_e(i, 6)
                    activate(0)
                    lo_e(i, 7)
                    lo_e(i, 8)
                    dve.wait_ge(act_done, at(i, 2, 1))
                    glu(1)
                    act_low(0)
                    for j in range(9, 12):
                        lo_e(i, j)
                    activate(1)
                    x_low(at(i, 2, 3))
                    lo_e(i, 12)
                    lo_e(i, 13)
                    act_low(1)
                    lo_e(i, 14)
                    lo_e(i, 15)
                    assert ms.k == MS
            fin = Steps(dve, tail, tl.k)
            dve.wait_ge(acc_back, 16 * LT)
            for t in range(LT):
                s = F(A_XG if t == 0 else A_Y if t == 1 else A_GS if t == 2 else A_HT, D)
                fin.did(V.tensor_tensor(s, s, F(A_GFB, D), ALU.mult))
            fin.wait()
            for t in range(LT):
                s = F(A_XG if t == 0 else A_Y if t == 1 else A_GS if t == 2 else A_HT, D)
                V.tensor_tensor(xn[:, t, :], xn[:, t, :], s, ALU.add).then_inc(res_ready, 1)

        @block.tensor
        def _(pe):
            def mm(out, lhsT, rhs, start, stop, skip=False):
                return pe.matmul(out, lhsT, rhs, start=start, stop=stop, skip_group_check=skip)

            def split_ready(base, per, i, j):
                pe.wait_ge(lo_made, at(i, per, base - RET0 + j + 1))

            def proj_tokens(base, per, i, j0, tiles, bank, ready=None, xh=None, xl=None):
                xh, xl = xh or hhi, xl or hlo
                for kh in range(2):
                    j = j0 + kh
                    split_ready(base, per, i, j)
                    for kq in range(KH):
                        kk = KH * kh + kq
                        for t in range(tiles):
                            if kk == 0 and ready:
                                ready(t)
                            o = ps[:, bank(t), :]
                            wh, wl = whi[:, j % NSPL, kq, :], wlo[:, j % NSPL, kq, :]
                            lh, ll = xh[:, kk, t * P:(t + 1) * P], xl[:, kk, t * P:(t + 1) * P]
                            mm(o, lh, wh, kk == 0, False)
                            mm(o, lh, wl, False, False)
                            last = mm(o, ll, wh, False, kk == KC - 1)
                    last.then_inc(w_used, 1)

            def branch(base, per, i, done, ready):
                for jj in range(2):
                    j = 6 + jj
                    split_ready(base, per, i, j)
                    for f in range(4):
                        c = 4 * jj + f
                        ready(c)
                        for kq in range(KH):
                            wh = whi[:, j % NSPL, kq, f * P:(f + 1) * P]
                            wl = wlo[:, j % NSPL, kq, f * P:(f + 1) * P]
                            o = ps[:, c, :]
                            mm(o, wh, yhi[:, kq, :], kq == 0, False)
                            mm(o, wh, ylo[:, kq, :], False, False)
                            last = mm(o, wl, yhi[:, kq, :], False, kq == KH - 1)
                        last.then_inc(done if f < 3 else w_used, 1)

            def gates(base, ready):
                for cg in range(2):
                    for kh in range(2):
                        j = 2 * cg + kh
                        split_ready(base, 0, 0, j)
                        for kq in range(KH):
                            kk = KH * kh + kq
                            for f in range(4):
                                if kk == 0:
                                    ready(4 * cg + f)
                                wh = whi[:, j % NSPL, kq, f * P:(f + 1) * P]
                                wl = wlo[:, j % NSPL, kq, f * P:(f + 1) * P]
                                o = ps[:, 4 * cg + f, :]
                                mm(o, wh, hhi[:, kk, 0:L], kk == 0, False)
                                mm(o, wh, hlo[:, kk, 0:L], False, False)
                                last = mm(o, wl, hhi[:, kk, 0:L], False, kk == KC - 1)
                        last.then_inc(w_used, 1)

            pe.wait_ge(c_silu, 1)
            for c in range(12):
                for kh in range(2):
                    j = 2 * c + kh
                    pe.wait_ge(raw_loaded[j % NRAW], 16 * (j // NRAW + 1))
                    if c >= 8 and kh == 0:
                        pe.wait_ge(mod_rows, c - 7)
                    for kq in range(KH):
                        kk = KH * kh + kq
                        last = mm(ps[0:2, c % 8, :], ct[:, kk, :], raw[:, j % NRAW, kq, :], kk == 0, kk == KC - 1)
                    last.then_inc(mod_used, 1)
            pe.wait_ge(s_const, 16)
            pe.wait_ge(x_normed, TT)
            pe.wait_ge(mod_rows, 12)
            for k in range(KC):
                if k >= 4:
                    pe.wait_ge(h_lo, 2 * (k - 4) + 2)
                for t in range(TT):
                    o = ps[:, 2 * (k % 4) + t // LT, (t % LT) * P:(t % LT + 1) * P]
                    last = pe.transpose(o, F(A_X, TT, D)[:, t, k * P:(k + 1) * P], ident)
                last.then_inc(h_turned, 1)
            pe.wait_ge(h_lo, 2 * KC)

            with pe.Fori(0, RET_HEADS) as h:
                B = (RET0, RET_N, h)
                for s in range(2):
                    split_ready(*B, s)
                    sh, sl = (w[:, s, :, :].rearrange("p k (s n) -> p (k s) n", n=DK) for w in (whi, wlo))
                    for kk in range(KC):
                        for f in (2 * s, 2 * s + 1):
                            c = f % 2
                            wh, wl = sh[:, kk, c * P:(c + 1) * P], sl[:, kk, c * P:(c + 1) * P]
                            o = ps[:, f, :]
                            first, end = kk == 0, kk == KC - 1
                            mm(o, wh, hhi[:, kk, 0:L], first, False)
                            mm(o, wh, hlo[:, kk, 0:L], False, False)
                            last = mm(o, wl, hhi[:, kk, 0:L], False, end)
                            if s == 1:
                                oc = ps[:, 4, c * C:(c + 1) * C]
                                mm(oc, wh, hhi[:, kk, L:T], first and c == 0, False, True)
                                mm(oc, wh, hlo[:, kk, L:T], False, False, True)
                                last = mm(oc, wl, hhi[:, kk, L:T], False, end and c == 1, True)
                    last.then_inc(w_used, 1)

                def v_ready(t):
                    if t == 3:
                        pe.wait_ge(qk_out, at(h, 5, 1))
                    elif t > 3:
                        pe.wait_ge(qk_out, at(h, 5, t - 2))

                proj_tokens(*B, 2, TT, lambda t: (5 + t) % 8, v_ready)

                def g_ready(t):
                    if t < 2:
                        pe.wait_ge(qk_out, at(h, 5, 4 + t))
                    else:
                        pe.wait_ge(v_out, at(h, TT, t - 1))

                proj_tokens(*B, 4, LT, lambda t: 3 + t, g_ready)
                qT, kT = F(A_QT, 2, L), F(A_KT, 2, T)
                pe.wait_ge(rope_done, at(h, 4, 4))
                pe.wait_ge(v_out, at(h, TT, TT))
                for m in range(TT):
                    if m >= 4:
                        pe.wait_ge(g_out, at(h, LT, m - 3))
                    for c in range(2):
                        last = mm(ps[:, (7 + m) % 8, :], kT[:, c, m * P:(m + 1) * P], qT[:, c, :], c == 0, c == 1)
                    last.then_inc(sc_done, 1)
                pe.wait_ge(g_out, at(h, LT, LT))
                for m in range(TT):
                    pe.wait_ge(pt_done, at(h, TT, m + 1))
                    for t in range(LT):
                        if m == 0 and t == 2:
                            pe.wait_ge(pt_done, at(h, TT, 2))
                        last = mm(ps[:, (5 + t) % 8, :], F(A_RAWQK, TT, L)[:, m, t * P:(t + 1) * P],
                                  F(A_V, TT, DV)[:, m, :], m == 0, m == TT - 1)
                        if m == TT - 1:
                            last.then_inc(o_done, 1)
                for t in range(LT):
                    pe.wait_ge(y_done, at(h, LT, t + 1))
                    for c in range(4):
                        last = pe.transpose(ps[:, 1 + c, t * P:(t + 1) * P],
                                            F(A_GATE, LT, DV)[:, t, c * P:(c + 1) * P], ident)
                    last.then_inc(yt_done, 1)
                pe.wait_ge(yt_lo, at(h, 4, 4))
                branch(*B, br_done, lambda c: None)
                pe.wait_ge(br_out, at(h, KC, 8))

            gates(GA0, lambda c: None)

            with pe.Fori(0, GROUPS) as g:
                B = (DIFF0, DIFF_N, g)
                NQ, NU = LT + TT, LT * HG
                pe.wait_ge(gg_out, 8)
                proj_tokens(*B, 0, LT, lambda t: t)

                def k_ready(t):
                    if t >= 4:
                        pe.wait_ge(q_raw, at(g, NQ, t - 3))

                proj_tokens(*B, 2, TT, lambda t: (4 + t) % 8, k_ready)

                def turn(n):
                    pe.wait_ge(q_ready, at(g, NQ, n + 1))
                    if n % NQ >= 2:
                        pe.wait_ge(q_out, at(g, NQ, n - 1))
                    for c in range(HG):
                        last = pe.transpose(ps[:, 2 + (n % 2), c * P:(c + 1) * P],
                                            F(A_PROB, TT, 512)[:, n % TT, c * P:(c + 1) * P], ident)
                    last.then_inc(q_turned, 1)

                pe.wait_ge(q_raw, at(g, NQ, 4))
                for n in range(LT):
                    turn(n)

                def dv_ready(t):
                    pe.wait_ge(q_raw, at(g, NQ, LT + t + 1))

                proj_tokens(*B, 4, TT, lambda t: (4 + t) % 8, dv_ready)
                for n in range(LT, NQ):
                    turn(n)
                qT, kT = F(A_DQT, HG, L), F(A_DKT, HG, T)
                vv = F(A_DV, TT, 512)

                def scores(u):
                    qt, c = u // HG, u % HG
                    s0 = (u % 2) * 3
                    for s in range(2):
                        q = qT[s * DH:(s + 1) * DH, c, qt * P:(qt + 1) * P]
                        k = kT[s * DH:(s + 1) * DH, c, :]
                        cuts = ((512, 768), (0, 512)) if s == 0 else ((256, 768), (0, 256))
                        for n, (k0, k1) in enumerate(cuts):
                            col = s * T + k0
                            if s == 1 and n == 1:
                                pe.wait_ge(s_middle, at(g, NU, u + 1))
                            last = mm(psf[:, s0 * 512 + col:s0 * 512 + col + k1 - k0], q, k[:, k0:k1], True, True)
                            if s == 0 and n == 0:
                                last.then_inc(s_middle, 1)
                    last.then_inc(s_done, 1)

                def turn_probs(u):
                    pe.wait_ge(a_done, at(g, NU, u + 1))
                    s0 = (u % 2) * 1536
                    for m in range(TT):
                        last = pe.transpose(psf[:, s0 + m * P:s0 + (m + 1) * P],
                                            F(A_PROB, 2, 2, T)[:, u % 2, 0, m * P:(m + 1) * P], ident)
                    last.then_inc(at_turned, 1)

                def values(u):
                    qt, c = u // HG, u % HG
                    pe.wait_ge(at_out, at(g, NU, u + 1))
                    for m in range(TT):
                        last = mm(ps[:, 6 + qt % 2, c * P:(c + 1) * P], F(A_AT, 2, T)[:, u % 2, m * P:(m + 1) * P],
                                  vv[:, m, c * P:(c + 1) * P], m == 0, m == TT - 1)
                    last.then_inc(ov_done, 1)

                def turn_y(qt):
                    pe.wait_ge(yd_done, at(g, LT, qt + 1))
                    for c in range(HG):
                        last = pe.transpose(ps[:, 6 + qt % 2, c * P:(c + 1) * P],
                                            F(A_OY, 2, 512)[:, 1, c * P:(c + 1) * P], ident)
                    last.then_inc(yd_turned, 1)

                pe.wait_ge(q_out, at(g, NQ, NQ))
                pe.wait_ge(dv_out, at(g, TT, TT))
                scores(0)
                scores(1)
                for u in range(NU):
                    turn_probs(u)
                    if u >= 1:
                        if (u - 1) % HG == 0 and u - 1 >= 2 * HG:
                            pe.wait_ge(yd_lo, at(g, LT, (u - 1) // HG - 1))
                        values(u - 1)
                    if u % HG == 2 and u > HG:
                        turn_y(u // HG - 1)
                    if u + 2 < NU:
                        pe.wait_ge(at_out, at(g, NU, u + 1))
                        scores(u + 2)
                values(NU - 1)
                turn_y(LT - 1)
                pe.wait_ge(yd_lo, at(g, LT, LT))
                branch(*B, bd_done, lambda c: None)
                pe.wait_ge(bd_out, at(g, KC, 8))
            gates(GB0, lambda c: None)
            pe.wait_ge(gg_out, 16)
            pe.wait_ge(m_lo, KC)
            proj_tokens(OUT0, 0, 0, 0, LT, lambda t: t)
            proj_tokens(OUT0, 0, 0, 2, LT, lambda t: 4 + t)
            for t in range(LT):
                pe.wait_ge(n2_done, t + 1)
                if t == 0:
                    pe.wait_ge(xn_done, 8)
                for q in range(2):
                    if t:
                        pe.wait_ge(h2_out, 2 * (t - 1) + q + 1)
                    for c in range(4):
                        k = 4 * q + c
                        last = pe.transpose(ps[:, q, c * P:(c + 1) * P],
                                            F(A_HT, 2, D)[:, t % 2, k * P:(k + 1) * P], ident)
                    last.then_inc(h2_turned, 1)
                pe.wait_ge(h2_out, 2 * t + 2)
                if t >= 2:
                    pe.wait_ge(m_ready, t - 1)
                for k in range(KC):
                    last = mm(ps[:, 2 + t % 2, 0:N_EXPERTS], F(A_H2T, KC, L)[:, k, t * P:(t + 1) * P], rw[:, k, :],
                              k == 0, k == KC - 1)
                last.then_inc(lg_done, 1)
            tri = cst[:, C_TRI:C_TRI + P]
            pe.wait_ge(pool_pre, 1)
            for t in range(LT):
                pe.wait_ge(m_ready, t + 1)
                for s in range(t):
                    mm(ps[:, 4 + t, 0:N_EXPERTS], allone, mask3[:, s, 0:32], s == 0, False)
                last = mm(ps[:, 4 + t, 0:N_EXPERTS], tri, mask3[:, t, 0:32], t == 0, True)
                last.then_inc(pos_done, 1)
            for t in range(LT):
                last = mm(ps[0:96, 0, 0:1], mask3[:, t, :], ones[:, 0:1], t == 0, t == LT - 1)
            last.then_inc(cnt_done, 1)
            pe.wait_ge(flag_ready, 1)
            mm(ps[0:96, 0, 0:1], tri[0:96, 0:96], small[0:96, 0:1], True, True).then_inc(opos_done, 1)
            pe.wait_ge(oh_ready, 1)
            oh = small[0:96, 8:8 + OVER + 1]
            mm(ps[0:1, 0, 0:OVER + 1], cst[0:96, C_CODE:C_CODE + 1], oh, True, True)
            mm(ps[0:1, 0, OVER + 1:2 * OVER + 2], cst[0:96, C_EXP:C_EXP + 1], oh, True, True)
            mm(ps[0:1, 0, 2 * OVER + 2:2 * OVER + 3], small[0:96, 0:1], ones[0:96, 0:1], True, True).then_inc(items_done, 1)

            xthi = yhi[:, 0:2, :].rearrange("p a (k n) -> p (a k) n", n=P)
            xtlo = yhi[:, 2:4, :].rearrange("p a (k n) -> p (a k) n", n=P)
            acthi = ylo[:, 0:2, :].rearrange("p a (k n) -> p (a k) n", n=P)
            actlo = ylo[:, 2:4, :].rearrange("p a (k n) -> p (a k) n", n=P)
            bias = F(A_BIAS, 1536).bitcast(BF16)
            W1COL = (0, 2, 1, 3)

            def turn_x():
                for q in range(2):
                    for c in range(4):
                        k = 4 * q + c
                        last = pe.transpose(ps[:, q, c * P:(c + 1) * P], F(A_XG, D)[:, k * P:(k + 1) * P], ident)
                    last.then_inc(xt_turned, 1)

            pe.wait_ge(items_ready, 1)
            n_items = pe.value_load(count_i[0:1, 0:1], min_val=N_EXPERTS, max_val=MAX_BLOCKS)
            pe.wait_ge(gathered, 16)
            turn_x()
            pe.wait_ge(b_ready, 1)
            with pe.Fori(0, MAX_BLOCKS) as i:
                with pe.If(i < n_items):
                    def up(gidx):
                        for kh in range(2):
                            j = 2 * gidx + kh
                            pe.wait_ge(e_lo, at(i, MOE_N, j + 1))
                            for kq in range(KH):
                                kk = KH * kh + kq
                                o = ps[:, 2 + gidx, :]
                                wh, wl = e_whi[j % ESPL][:, kq, :], e_wlo[j % ESPL][:, kq, :]
                                if kk == 0:
                                    c = W1COL[gidx]
                                    mm(o, sel[0:96, :], bias[0:96, c * COL:(c + 1) * COL], True, False)
                                mm(o, xthi[:, kk, :], wh, False, False)
                                mm(o, xthi[:, kk, :], wl, False, False)
                                last = mm(o, xtlo[:, kk, :], wh, False, kk == KC - 1)
                            last.then_inc(e_used, 1)

                    def down(kh):
                        for c in range(2):
                            j = 8 + 2 * kh + c
                            pe.wait_ge(e_lo, at(i, MOE_N, j + 1))
                            o = ps[:, 6 + c, :]
                            if kh == 0:
                                last = mm(o, sel[0:96, :], bias[0:96, 2048 + c * COL:2048 + (c + 1) * COL], True, False)
                                if c == 1:
                                    last.then_inc(sel_used, 1)
                            for kq in range(KH):
                                kk = KH * kh + kq
                                wh, wl = e_whi[j % ESPL][:, kq, :], e_wlo[j % ESPL][:, kq, :]
                                mm(o, acthi[:, kk, :], wh, False, False)
                                mm(o, acthi[:, kk, :], wl, False, False)
                                last = mm(o, actlo[:, kk, :], wh, False, kk == KC - 1)
                            last.then_inc(e_used, 1)

                    def turn_act(hf):
                        pe.wait_ge(act_done, at(i, 2, hf + 1))
                        for c in range(4):
                            last = pe.transpose(ps[:, 2 * hf, c * P:(c + 1) * P],
                                                F(A_AC, 2, COL)[:, hf, c * P:(c + 1) * P], ident)
                        last.then_inc(act_turned, 1)

                    pe.wait_ge(xt_lo, at(i, 2, 2))
                    pe.wait_ge(sel_ready, at(i, 1, 1))
                    up(0)
                    up(1)
                    up(2)
                    turn_act(0)
                    up(3)
                    pe.wait_ge(gathered, at(i, 16, 32))
                    pe.wait_ge(act_lo, at(i, 2, 1))
                    turn_x()
                    pe.wait_ge(y_out, at(i, 2, 2))
                    down(0)
                    turn_act(1)
                    pe.wait_ge(act_lo, at(i, 2, 2))
                    down(1)


_INS = {
    "x": (L, D), "c": (1, D), "ctx": (C, D), "c_ctx": (D,), "norm1_g": (1, D), "norm2_g": (1, D),
    "w_mod": (D, 6 * D), "b_mod": (1, 6 * D), "w_in": (D, 11 * D), "ret_decay_logit": (1, 8),
    "ret_norm_g": (RET_HEADS, DV), "diff_q_norm_g": (1, DH), "diff_k_norm_g": (1, DH),
    "diff_lambda": (1, 4 * DH), "diff_norm_g": (1, 2 * DH), "w_br_ret": (2 * D, D), "w_br_diff": (D, D),
    "w_out": (D, D), "router_w": (D, N_EXPERTS), "router_b": (1, N_EXPERTS),
    "exp_w1": (N_EXPERTS, D, 2 * D), "exp_b1": (N_EXPERTS, 2 * D),
    "exp_w2": (N_EXPERTS, D, D), "exp_b2": (N_EXPERTS, D),
}


def constants(np):
    c = np.zeros((P, N_CONST), np.float32)
    p = np.arange(P)
    c[:, C_ID:C_ID + P] = np.eye(P)
    c[:, C_TRI:C_TRI + P] = p[:, None] < p[None, :]
    c[:, C_WIN:C_WIN + WIN] = np.arange(WIN)[None, :] - (L - P) - p[:, None]

    def angles(half, pos):
        inv = np.float32(10000.0) ** (-np.arange(half, dtype=np.float32) / np.float32(half))
        return pos.astype(np.float32)[None, :] * inv.astype(np.float32)[:, None]

    sign = np.where(p < 64, 1.0, -1.0)[:, None]
    o = C_ROPE_R
    for n in (GRID_H, GRID_W):
        ang = angles(DK // 4, np.arange(n))[p % (DK // 4)].astype(np.float64)
        c[:, o:o + n] = np.cos(ang)
        c[:, o + n:o + 2 * n] = sign * np.sin(ang)
        o += 2 * n
    for t in range(LT):
        tok = t * P + p
        tab = np.zeros((P, 2, 2, 2, 16))
        for ax, pos in enumerate((tok // GRID_W, tok % GRID_W)):
            ang = angles(DH // 4, pos).T.astype(np.float64)
            for s in range(2):
                tab[:, 0, ax, s] = np.cos(ang)
                tab[:, 1, ax, s] = np.sin(ang) * (-1.0 if s == 0 else 1.0)
        c[:, C_ROPE_D + t * 2 * DH:C_ROPE_D + (t + 1) * 2 * DH] = tab.reshape(P, 2 * DH)
        c[:, C_TOK + t] = tok
    c[:, C_IOTA:C_IOTA + N_EXPERTS] = np.arange(N_EXPERTS)[None, :]
    c[:, C_THR] = P * (p // 32 + 1)
    c[:, C_CODE] = p + 32
    c[:, C_EXP] = p % 32
    c[:, C_EYE3:C_EYE3 + N_EXPERTS] = (p % 32)[:, None] == np.arange(32)[None, :]
    return c


def kernel(**inputs):
    import numpy as np
    import concourse.bacc as bacc
    from concourse.bass_utils import run_bass_kernel_spmd

    nc = bacc.Bacc("TRN2", target_bir_lowering=False, num_devices=1)
    arrays, aps = {}, {}
    for name, shape in _INS.items():
        arrays[f"in_{name}"] = np.ascontiguousarray(np.asarray(inputs[name]).reshape(shape))
        aps[name] = nc.dram_tensor(f"in_{name}", shape, F32, kind="ExternalInput").ap()
    arrays["in_consts"] = constants(np)
    aps["consts"] = nc.dram_tensor("in_consts", (P, N_CONST), F32, kind="ExternalInput").ap()
    aps["out"] = nc.dram_tensor("out_x", (L, D), F32, kind="ExternalOutput").ap()
    scratch = (
        nc.dram_tensor("mod_rows_d", (2, 6 * D), F32, kind="Internal").ap(),
        nc.dram_tensor("h2_d", (L + P, D), F32, kind="Internal").ap(),
        nc.dram_tensor("list_d", (L * N_EXPERTS, 2), I32, kind="Internal").ap(),
        nc.dram_tensor("acc_d", (L + P, D), F32, kind="Internal").ap(),
        nc.dram_tensor("accr_d", (P, 4096), F32, kind="Internal").ap(),
    )
    build(nc, aps, scratch)
    r = run_bass_kernel_spmd(nc, [arrays], core_ids=[0])
    return r.results[0]["out_x"].reshape(1, L, D)
```

```python
from contextlib import ExitStack

import concourse.bass as bass
from concourse import mybir

F32 = mybir.dt.float32
F32R = mybir.dt.float32r
BF16 = mybir.dt.bfloat16
I32 = mybir.dt.int32
U32 = mybir.dt.uint32
ALU = mybir.AluOpType
ACT = mybir.ActivationFunctionType
AX = mybir.AxisListType

P = 128
D = 1024
KC = D // P
L = 512
LT = L // P
C = 256
CT = C // P
T = L + C
TT = T // P
COL = 512
KH = 4
NRAW = 4
NSPL = 2
ERAW = 6
ESPL = 4

RET_HEADS = 4
DK = D // RET_HEADS
DV = 2 * D // RET_HEADS
GRID_W = 64
GRID_H = L // GRID_W
DH = 64
HG = 4
GROUPS = 2
N_EXPERTS = 32
TOP_K = 4
LIMIT = 7.0
ALPHA = 1.702
EPS = 1e-6
LAMBDA_INIT = 0.2
MAX_BLOCKS = L * TOP_K // P - 1 + N_EXPERTS
OVER = MAX_BLOCKS - N_EXPERTS
ITEMS = MAX_BLOCKS + 1

RQ, RK, RV, RG, DQ, DKK, DVV, GA, GB = 0, 1024, 2048, 4096, 6144, 7168, 8192, 9216, 10240

MOD0, MOD_N = 0, 24
RET0, RET_N = 24, 8
GA0 = RET0 + RET_N * RET_HEADS
DIFF0, DIFF_N = GA0 + 4, 8
GB0 = DIFF0 + DIFF_N * GROUPS
OUT0 = GB0 + 4
MOE0, MOE_N = OUT0 + 4, 12

C_ID = 0
C_TRI = C_ID + P
C_WIN = C_TRI + P
WIN = 2 * L - P
C_ROPE_R = C_WIN + WIN
C_ROPE_D = C_ROPE_R + 2 * GRID_H + 2 * GRID_W
C_IOTA = C_ROPE_D + LT * 2 * DH
C_TOK = C_IOTA + N_EXPERTS
C_THR = C_TOK + LT
C_CODE = C_THR + 1
C_EXP = C_CODE + 1
C_EYE3 = C_EXP + 1
N_CONST = C_EYE3 + N_EXPERTS

A_WORDS = 17920
A_X, A_BMOD, A_SQ = 6144, 0, 12288
A_RAWQK = 0
A_QT, A_KT, A_V, A_GATE, A_DEC, A_TMP = 3072, 4096, 5632, 8704, 10752, 12288
A_ACC = A_WORDS - 4096
A_PROB = 0
A_AT = 3072
A_OY, A_DV, A_DQT, A_DKT = 4608, 5632, 8704, 10752
A_ACC2 = 0
A_XN = 4096
A_GFB, A_GAB, A_A2B, A_SH2B = 8192, 9216, 10240, 11264
A_H2T = 0
A_HT = 12288
A_BIAS = 14336
A_BSRC, A_BR = 1024, 0
A_GAP = 13312
A_RT = 15872
A_EW = 10240
A_XG, A_Y, A_GS, A_LS, A_TH, A_AC = 0, 1024, 2048, 2560, 3072, 9216


MOD_A = 2 * D // COL
MOD_BEFORE = {3: (4, 5, 6), 4: (7,), 5: (8,), 6: (9,), 7: (10,)}


def mod_bank(c):
    return c if c < MOD_A else 6 + c % 2


def branch_bank(c):
    return (5 + c) % 8


TURN_K = (1, 2, 3, 4, 5)


def at(i, per, k):
    return i * per + k


class Steps:

    def __init__(self, eng, sem, base=0):
        self.eng, self.sem, self.base, self.k = eng, sem, base, 0

    def did(self, ins):
        ins.then_inc(self.sem, 1)
        self.k += 1

    def wait(self):
        self.eng.wait_ge(self.sem, self.base + self.k)


def build(nc, a, scratch):
    mod_d, h2_d, list_d, acc_d, accr_d = scratch
    ctx = ExitStack()
    with ctx:
        def sb(name, shape, dt=F32):
            return ctx.enter_context(nc.sbuf_tensor(name, shape, dt))

        def sem(name):
            return ctx.enter_context(nc.semaphore(name))

        cst = sb("cst", [P, N_CONST])
        raw = sb("raw", [P, NRAW, KH, COL])
        whi = sb("whi", [P, NSPL, KH, COL], F32R)
        wlo = sb("wlo", [P, NSPL, KH, COL], F32R)
        hhi = sb("hhi", [P, KC, T], F32R)
        hlo = sb("hlo", [P, KC, T], F32R)
        yhi = sb("yhi", [P, KH, L], F32R)
        ylo = sb("ylo", [P, KH, L], F32R)
        ar = sb("ar", [P, A_WORDS])
        cc = sb("cc", [P, KC, 2])
        ct = sb("ct", [P, KC, 2])
        mcols = sb("mcols", [P, 5, KC])
        ones = sb("ones", [P, 16])
        ss = sb("ss", [P, 16])
        sm = sb("sm", [P, 16])
        rs = sb("rs", [P, 16])
        rs2 = sb("rs2", [P, 8])
        half = sb("half", [P, 16])
        hsc = sb("hsc", [P, RET_HEADS, 8])
        hs = sb("hs", [P, 8])
        gqk = sb("gqk", [P, 2, DH])
        dng = sb("dng", [P, 1])
        lam = sb("lam", [P, 8])
        nmx = sb("nmx", [P, 2, 2])
        den = sb("den", [P, 2, 2])
        rd = sb("rd", [P, 2, HG, 2])
        ratio = sb("ratio", [P, 2, 1])
        yscale = sb("yscale", [P, HG])
        sel = sb("sel", [P, P], BF16)
        small = sb("small", [P, 32])

        def F(off, *shape):
            n = 1
            for s in shape:
                n *= s
            v = ar[:, off:off + n]
            if len(shape) == 1:
                return v
            names = "abc"[:len(shape)]
            return v.rearrange("p (%s) -> p %s" % (" ".join(names), " ".join(names)),
                               **{names[k]: shape[k] for k in range(len(shape) - 1)})

        ps = ctx.enter_context(nc.psum_tensor("ps", [P, 8, 512], F32))
        psf = ps[:, :, :].rearrange("p b n -> p (b n)")
        ident = cst[:, C_ID:C_ID + P]

        s_const = sem("s_const")
        s_cvec = sem("s_cvec")
        s_small = sem("s_small")
        s_x = sem("s_x")
        s_bmod = sem("s_bmod")
        raw_loaded = [sem(f"raw_loaded{k}") for k in range(NRAW)]
        mod_stored = sem("mod_stored")
        mod_cols = sem("mod_cols")
        s_init = sem("s_init")
        hi_made = sem("hi_made")
        lo_made = sem("lo_made")
        w_used = sem("w_used")
        mod_used = sem("mod_used")
        e_loaded = [sem(f"e_loaded{k}") for k in range(ERAW)]
        e_hi = sem("e_hi")
        e_lo = sem("e_lo")
        e_used = sem("e_used")
        dve_pre = sem("dve_pre")
        pool_pre = sem("pool_pre")
        c_tanh = sem("c_tanh")
        c_silu = sem("c_silu")
        mod_rows = sem("mod_rows")
        x_sq = sem("x_sq")
        x_rstd = sem("x_rstd")
        x_normed = sem("x_normed")
        h_turned = sem("h_turned")
        h_hi = sem("h_hi")
        h_lo = sem("h_lo")
        mod_vec = sem("mod_vec")
        pre_done = sem("pre_done")
        r_head = sem("r_head")
        r_exp = sem("r_exp")
        r_arg = sem("r_arg")
        r_step = sem("r_step")
        qk_out = sem("qk_out")
        rope_done = sem("rope_done")
        v_out = sem("v_out")
        g_tanh = sem("g_tanh")
        g_out = sem("g_out")
        sc_done = sem("sc_done")
        pt_done = sem("pt_done")
        o_done = sem("o_done")
        o_sq = sem("o_sq")
        o_rstd = sem("o_rstd")
        pool_r = sem("pool_r")
        y_done = sem("y_done")
        yt_done = sem("yt_done")
        yt_hi = sem("yt_hi")
        yt_lo = sem("yt_lo")
        br_done = sem("br_done")
        br_out = sem("br_out")
        gg_done = sem("gg_done")
        gg_tanh = sem("gg_tanh")
        gg_out = sem("gg_out")
        accr_stored = sem("accr_stored")
        accr_back = sem("accr_back")
        q_raw = sem("q_raw")
        q_sq = sem("q_sq")
        q_sum = sem("q_sum")
        q_rstd = sem("q_rstd")
        q_ready = sem("q_ready")
        q_turned = sem("q_turned")
        q_out = sem("q_out")
        dv_out = sem("dv_out")
        d_step = sem("d_step")
        pool_d = sem("pool_d")
        s_middle = sem("s_middle")
        s_done = sem("s_done")
        mx_done = sem("mx_done")
        p_done = sem("p_done")
        a_done = sem("a_done")
        at_turned = sem("at_turned")
        at_out = sem("at_out")
        ov_done = sem("ov_done")
        ob_out = sem("ob_out")
        ob_sum = sem("ob_sum")
        ob_rstd = sem("ob_rstd")
        yd_done = sem("yd_done")
        yd_turned = sem("yd_turned")
        yd_hi = sem("yd_hi")
        yd_lo = sem("yd_lo")
        bd_done = sem("bd_done")
        bd_out = sem("bd_out")
        m_sum = sem("m_sum")
        m_hi = sem("m_hi")
        m_lo = sem("m_lo")
        xp_done = sem("xp_done")
        vec2 = sem("vec2")
        rw_loaded = sem("rw_loaded")
        x_again = sem("x_again")
        xn_done = sem("xn_done")
        tail = sem("tail")
        n2_sq = sem("n2_sq")
        n2_rstd = sem("n2_rstd")
        pool_t = sem("pool_t")
        n2_done = sem("n2_done")
        h2_stored = [sem(f"h2_stored{k}") for k in range(2)]
        h2_turned = sem("h2_turned")
        h2_out = sem("h2_out")
        lg_done = sem("lg_done")
        m_ready = sem("m_ready")
        pos_done = sem("pos_done")
        ones_made = sem("ones_made")
        g_exp = sem("g_exp")
        g_arg = sem("g_arg")
        route_ready = sem("route_ready")
        cnt_done = sem("cnt_done")
        flag_ready = sem("flag_ready")
        opos_done = sem("opos_done")
        oh_ready = sem("oh_ready")
        items_done = sem("items_done")
        items_ready = sem("items_ready")
        listed = sem("listed")
        list_back = sem("list_back")
        b_loaded = sem("b_loaded")
        pool_m = sem("pool_m")
        pool_tick = sem("pool_tick")
        acc_zeroed = sem("acc_zeroed")
        gathered = sem("gathered")
        xt_turned = sem("xt_turned")
        xt_hi = sem("xt_hi")
        xt_lo = sem("xt_lo")
        sel_ready = sem("sel_ready")
        sel_used = sem("sel_used")
        cur_ready = sem("cur_ready")
        glu_min = sem("glu_min")
        glu_tanh = sem("glu_tanh")
        act_done = sem("act_done")
        moe_step = sem("moe_step")
        act_turned = sem("act_turned")
        act_hi = sem("act_hi")
        act_lo = sem("act_lo")
        y_out = sem("y_out")
        y_added = sem("y_added")
        acc_back = [sem(f"acc_back{t}") for t in range(LT)]
        res_ready = sem("res_ready")
        stored = sem("stored")

        hh = [h[:, :, :].rearrange("p a b -> p (a b)").rearrange("p (s k n) -> p s k n", s=3, k=KH) for h in (hhi, hlo)]
        e_raw = [raw[:, k, :, :] for k in range(NRAW)] + [F(A_EW + k * KH * COL, KH, COL) for k in range(2)]
        e_whi = [whi[:, 0, :, :], whi[:, 1, :, :], hh[0][:, 0], hh[0][:, 1]]
        e_wlo = [wlo[:, 0, :, :], wlo[:, 1, :, :], hh[1][:, 0], hh[1][:, 1]]

        mhi = [yhi[:, c, :] if c < KH else hhi[:, c, 0:L] for c in range(KC)]
        mlo = [ylo[:, c, :] if c < KH else hlo[:, c, 0:L] for c in range(KC)]

        items_i = sb("items_i", [1, 2 * ITEMS], I32)
        count_i = sb("count_i", [1, 2], I32)
        cur = sb("cur", [P, 2], I32)
        nxt = sb("nxt", [P, 2], I32)
        lamt = F(A_GAP, 4, DH)
        linit = F(A_GAP + 4 * DH, N_EXPERTS, 2).bitcast(I32)
        lgt = F(A_GAP + 4 * DH + 2 * N_EXPERTS, 4, 8)
        lgx = F(A_GAP + 4 * DH + 2 * N_EXPERTS + 32, 8)
        rt = [A_RT]

        def R(*shape):
            n = 1
            for x in shape:
                n *= x
            rt[0] += n
            assert rt[0] <= A_WORDS
            return F(rt[0] - n, *shape)

        rw = R(KC, N_EXPERTS)
        rb = R(N_EXPERTS)
        topi = R(LT, 8).bitcast(U32)
        topv = R(LT, 8)
        topf = R(LT, 8)
        gate = R(LT, TOP_K)
        gsum = R(LT, 2)
        logit = R(LT, N_EXPERTS)
        onehot = R(LT * TOP_K, N_EXPERTS)
        mask3 = R(LT, 3 * N_EXPERTS)
        slot = R(LT * TOP_K)
        junk32 = R(N_EXPERTS)
        lrow = R(LT * TOP_K).bitcast(I32)
        lval = R(LT * TOP_K, 2).bitcast(I32)
        listsb = R(4 * N_EXPERTS, 2).bitcast(I32)
        allone = R(P)

        block = ctx.enter_context(nc.Block())

        def act_gate(act, hi, used, base, done, after=None):
            per = 0
            for cg in range(2):
                hi(base, per, 0, 2 * cg + 2)
                hi(base, per, 0, 2 * cg + 3)
                used(base, per, 0, 2 * cg + 1)
                for f in range(4):
                    c = 4 * cg + f
                    if c >= 2:
                        act.wait_ge(gg_out, done + c - 1)
                    act.activation(F(A_TMP if base == GA0 else A_OY, 2, 512)[:, c % 2, :], ps[:, c, :],
                                   ACT.Tanh, scale=0.5).then_inc(gg_tanh, 1)
                    if after and f:
                        after(c - 1)
                if after:
                    after(4 * cg + 3)

        def bias_thirds(dve, tl, bias, c):
            V = nc.vector
            r1 = F(A_BR, D)
            if c == 0:
                dve.wait_ge(b_loaded, 32)
            cols = slice(c * 1024, (c + 1) * 1024)
            src = F(A_BSRC, 3 * D)[0:32, cols]
            tl.did(V.tensor_copy(bias[0:32, cols], src))
            tl.wait()
            tl.did(V.tensor_tensor(r1[0:32, :], src, bias[0:32, cols], ALU.subtract))
            tl.wait()
            tl.did(V.tensor_copy(bias[32:64, cols], r1[0:32, :]))
            tl.wait()
            tl.did(V.tensor_copy(src, bias[32:64, cols]))
            tl.wait()
            tl.did(V.tensor_tensor(bias[64:96, cols], r1[0:32, :], src, ALU.subtract))
            tl.wait()

        def dve_gate(dve, lo, base, done, summed=None, low=None):
            V = nc.vector
            acc = F(A_ACC, KC, L)
            per = 0
            for cg in range(2):
                lo(base, per, 0, 2 * cg + 1)
                lo(base, per, 0, 2 * cg + 2)
                for f in range(4):
                    c = 4 * cg + f
                    dve.wait_ge(gg_tanh, done + c + 1)
                    if c == 0:
                        if base == GA0:
                            dve.wait_ge(br_out, KC * RET_HEADS)
                        else:
                            dve.wait_ge(bd_out, KC * GROUPS)
                    V.scalar_tensor_tensor(out=acc[:, c, :],
                                           in0=F(A_TMP if base == GA0 else A_OY, 2, 512)[:, c % 2, :], scalar=1.0,
                                           in1=acc[:, c, :], op0=ALU.add, op1=ALU.mult).then_inc(gg_out, 1)
                    if summed:
                        summed(c)
                        if f:
                            low(c - 1)
                if low:
                    low(4 * cg + 3)

        @block.sync
        def _(sp):
            def load(src, base, per, i, j, cols=COL):
                m = base - RET0 + j - NRAW + 1
                if base == MOD0:
                    if j >= NRAW:
                        sp.wait_ge(mod_used, j - NRAW + 1)
                elif isinstance(i, int) and per * i + base - RET0 + j < NRAW:
                    sp.wait_ge(mod_used, MOD_N - NRAW + j + 1)
                else:
                    sp.wait_ge(hi_made, at(i, per, m))
                    sp.wait_ge(lo_made, at(i, per, m))
                dst = raw[:, j % NRAW, :, :]
                if cols != COL:
                    dst = dst.rearrange("p k (s n) -> p (k s) n", n=cols)
                sp.dma_start(dst, src).then_inc(raw_loaded[j % NRAW], 16)

            def rows(w, r0, c0, n=COL):
                return w[r0:r0 + KH * P, c0:c0 + n].rearrange("(k p) n -> p k n", p=P)

            w_in, w_mod = a["w_in"], a["w_mod"]
            for j in range(NRAW):
                load(rows(w_mod, (j % 2) * KH * P, (j // 2) * COL), MOD0, 0, 0, j)
            for t in range(TT):
                src = a["x"] if t < LT else a["ctx"]
                sp.dma_start(F(A_X, TT, D)[:, t, :], src[(t % LT) * P:(t % LT + 1) * P, :]).then_inc(s_x, 16)
            for j in range(NRAW, MOD_N):
                load(rows(w_mod, (j % 2) * KH * P, (j // 2) * COL), MOD0, 0, 0, j)
            def ret_head(h, js):
                for j in js:
                    if j < 2:
                        load(w_in[:, bass.ds(h * DK + (RQ, RK)[j], DK)].rearrange("(k p) n -> p k n", p=P),
                             RET0, RET_N, h, j, cols=DK)
                    elif j < 6:
                        c0 = RV if j < 4 else RG
                        load(w_in[(j % 2) * KH * P:(j % 2 + 1) * KH * P, bass.ds(h * DV + c0, DV)].rearrange(
                            "(k p) n -> p k n", p=P), RET0, RET_N, h, j)
                    else:
                        load(a["w_br_ret"][bass.ds(h * DV, DV), (j - 6) * COL:(j - 5) * COL].rearrange(
                            "(k p) n -> p k n", p=P), RET0, RET_N, h, j)

            ret_head(0, range(RET_N))
            with sp.Fori(1, RET_HEADS) as h:
                ret_head(h, range(RET_N))
            for j in range(4):
                load(rows(w_in, (j % 2) * KH * P, GA + (j // 2) * COL), GA0, 0, 0, j)

            def diff_group(g, js):
                for j in js:
                    if j < 6:
                        c0 = (DQ, DKK, DVV)[j // 2]
                        load(w_in[(j % 2) * KH * P:(j % 2 + 1) * KH * P, bass.ds(g * COL + c0, COL)].rearrange(
                            "(k p) n -> p k n", p=P), DIFF0, DIFF_N, g, j)
                    else:
                        load(a["w_br_diff"][bass.ds(g * COL, COL), (j - 6) * COL:(j - 5) * COL].rearrange(
                            "(k p) n -> p k n", p=P), DIFF0, DIFF_N, g, j)

            with sp.Fori(0, GROUPS) as g:
                diff_group(g, range(DIFF_N))
            for j in range(4):
                load(rows(w_in, (j % 2) * KH * P, GB + (j // 2) * COL), GB0, 0, 0, j)
            sp.wait_ge(bd_out, KC * GROUPS)
            sp.wait_ge(mod_stored, 32)
            for off, src in ((A_GFB, mod_d[0:1, 5 * D:6 * D]), (A_GAB, mod_d[0:1, 2 * D:3 * D]),
                             (A_A2B, mod_d[0:1, 4 * D:5 * D]), (A_SH2B, mod_d[0:1, 3 * D:4 * D]),
                             (A_HT, a["norm2_g"])):
                sp.dma_start(F(off, D), src.broadcast_to((P, D))).then_inc(vec2, 16)
            for j in range(4):
                load(rows(a["w_out"], (j % 2) * KH * P, (j // 2) * COL), OUT0, 0, 0, j)
            sp.wait_ge(m_sum, KC)
            bsrc = F(A_BSRC, 3 * D)
            sp.dma_start(bsrc[0:N_EXPERTS, 0:2 * D], a["exp_b1"]).then_inc(b_loaded, 16)
            sp.dma_start(bsrc[0:N_EXPERTS, 2 * D:3 * D], a["exp_b2"]).then_inc(b_loaded, 16)
            for t in range(LT):
                sp.dma_start(F(A_XN, LT, D)[:, t, :], a["x"][t * P:(t + 1) * P, :]).then_inc(x_again, 16)
            sp.wait_ge(m_lo, KC)
            sp.dma_start(rw[:, :, :], a["router_w"].rearrange("(k p) n -> p k n", p=P)).then_inc(rw_loaded, 16)
            sp.dma_start(rb[:, :], a["router_b"].broadcast_to((P, N_EXPERTS))).then_inc(rw_loaded, 16)

            W1COL = (0, 2, 1, 3)

            def moe_block(e, i, j):
                jj = j % MOE_N
                one = slice(e, e + 1) if isinstance(e, int) else bass.ds(e, 1)
                if jj < 8:
                    src = a["exp_w1"][one, (jj % 2) * KH * P:(jj % 2 + 1) * KH * P,
                                      W1COL[jj // 2] * COL:(W1COL[jj // 2] + 1) * COL]
                else:
                    src = a["exp_w2"][one, (jj - 8) // 2 * KH * P:((jj - 8) // 2 + 1) * KH * P,
                                      (jj % 2) * COL:(jj % 2 + 1) * COL]
                if isinstance(i, int) and j < NRAW:
                    sp.wait_ge(hi_made, OUT0 - RET0 + j + 1)
                    sp.wait_ge(lo_made, OUT0 - RET0 + j + 1)
                elif not isinstance(i, int) or j >= ERAW:
                    sp.wait_ge(e_lo, at(i, MOE_N, j - ERAW + 1))
                sp.dma_start(e_raw[j % ERAW], src.rearrange("o (k p) n -> p (o k) n", p=P)).then_inc(
                    e_loaded[j % ERAW], 16)

            for j in range(NRAW):
                moe_block(0, 0, j)
            for t in range(LT):
                sp.wait_ge(n2_done, t + 1)
                sp.dma_start(h2_d[t * P:(t + 1) * P, :], F(A_HT, 2, D)[:, t % 2, :]).then_inc(h2_stored[t % 2], 16)
            for k in range(2):
                sp.wait_ge(h2_stored[k], 16 * LT // 2)
            sp.wait_ge(h2_turned, 2 * LT)
            for j in range(NRAW, MOE_N + ESPL):
                moe_block(j // MOE_N, 0, j)
            with sp.Fori(1, N_EXPERTS - 1) as i:
                for j in range(ESPL, MOE_N):
                    moe_block(i, i, j)
                for j in range(MOE_N, MOE_N + ESPL):
                    moe_block(i + 1, i, j)
            sp.wait_ge(items_ready, 1)
            n_items = sp.value_load(count_i[0:1, 0:1], min_val=N_EXPERTS, max_val=MAX_BLOCKS)
            with sp.Fori(N_EXPERTS - 1, MAX_BLOCKS) as i:
                with sp.If(i < n_items):
                    e = sp.value_load(items_i[0:1, bass.ds(i + ITEMS, 1)], min_val=0, max_val=N_EXPERTS - 1)
                    e1 = sp.value_load(items_i[0:1, bass.ds(i + ITEMS + 1, 1)], min_val=0, max_val=N_EXPERTS - 1)
                    for j in range(ESPL, MOE_N):
                        moe_block(e, i, j)
                    for j in range(MOE_N, MOE_N + ESPL):
                        moe_block(e1, i, j)

            sp.wait_ge(gathered, n_items * 16 + 16)
            sp.wait_ge(y_added, n_items * 16)
            for t in range(LT):
                sp.dma_start(F(A_XG if t == 0 else A_Y if t == 1 else A_GS if t == 2 else A_HT, D),
                             acc_d[t * P:(t + 1) * P, :]).then_inc(acc_back[t], 16)
            for t in range(LT):
                sp.wait_ge(res_ready, t + 1)
                sp.dma_start(a["out"][t * P:(t + 1) * P, :], F(A_XN, LT, D)[:, t, :]).then_inc(stored, 16)
            sp.wait_ge(stored, 16 * LT)

        @block.gpsimd
        def _(pool):
            st = Steps(pool, pool_pre)
            pool.dma_start(cst[:, :], a["consts"]).then_inc(s_const, 16)
            pool.dma_start(F(A_BMOD, 6 * D)[0:2, :], a["b_mod"].broadcast_to((2, 6 * D))).then_inc(s_bmod, 16)
            pool.dma_start(mcols[:, 4, :], a["norm1_g"].rearrange("o (k p) -> p (o k)", p=P),
                           allow_slow_non_contiguous=True).then_inc(s_small, 16)
            pool.dma_start(lgx[:, :], a["ret_decay_logit"].rearrange("o n -> o n").broadcast_to((P, 8))).then_inc(s_small, 16)
            for h in range(RET_HEADS):
                pool.dma_start(hsc[:, h, 4:8], a["ret_norm_g"][h, :].rearrange("(c p) -> p c", p=P),
                           allow_slow_non_contiguous=True).then_inc(s_small, 16)
            pool.dma_start(gqk[:, 0, :], a["diff_q_norm_g"].broadcast_to((P, DH))).then_inc(s_small, 16)
            pool.dma_start(gqk[:, 1, :], a["diff_k_norm_g"].broadcast_to((P, DH))).then_inc(s_small, 16)
            pool.dma_start(dng[:, :], a["diff_norm_g"].rearrange("o p -> p o"),
                           allow_slow_non_contiguous=True).then_inc(s_small, 16)
            pool.dma_start(lamt[:, :, :].rearrange("p a b -> p (a b)"),
                           a["diff_lambda"].broadcast_to((P, 4 * DH))).then_inc(s_small, 16)
            pool.memset(half[:, :], -0.5)
            pool.memset(ones[:, :], 1.0)
            st.did(pool.memset(small[:, :], 0.0))
            st.did(pool.memset(linit[:, :, :], 0))
            st.did(pool.memset(cur[:, :], 0))
            st.wait()
            st.did(pool.iota(linit[:, :, 0:1], [[0, N_EXPERTS]], base=L, channel_multiplier=1))
            st.wait()
            for b in range(4):
                pool.dma_start(list_d[b * P * N_EXPERTS:(b + 1) * P * N_EXPERTS, :].rearrange(
                    "(p e) w -> p (e w)", e=N_EXPERTS), linit[:, :, :].rearrange("p e w -> p (e w)")).then_inc(s_init, 16)

            st.did(pool.memset(F(A_ACC, 4096), 0.0))
            ZEROED = st.k

            def hold():
                pool.sem_inc(pool_tick, 1)

            def rstd(src, n, mean, st, out=None, m0=0):
                hold()
                st.did(pool.tensor_scalar(sm[:, m0:m0 + n], src, 1.0 / mean, EPS, ALU.mult, ALU.add))
                st.wait()
                return pool.tensor_tensor(out=rs[:, 0:n] if out is None else out, in0=sm[:, m0:m0 + n],
                                          in1=half[:, 0:n], op=ALU.pow)

            pool.wait_ge(x_sq, TT)
            rstd(ss[:, 0:TT], TT, D, st).then_inc(x_rstd, 1)
            pool.wait_ge(mod_used, 2 * MOD_A + 2)
            pool.wait_ge(pool_pre, ZEROED)
            pool.dma_start(h2_d[L:L + P, :], F(A_ACC, D)).then_inc(s_init, 16)
            for t in range(LT + 1):
                pool.dma_start(acc_d[t * P:(t + 1) * P, :], F(A_ACC, D)).then_inc(s_init, 16)
            with pool.Fori(0, RET_HEADS) as h:
                pool.wait_ge(o_sq, at(h, LT, LT))
                rstd(ss[:, 0:LT], LT, DV, Steps(pool, pool_r, h)).then_inc(o_rstd, 1)
            pool.wait_ge(accr_stored, 16)
            pool.memset(F(A_ACC, 4096), 0.0).then_inc(acc_zeroed, 1)
            PD = LT + TT + LT
            with pool.Fori(0, GROUPS) as g:
                for t in range(LT + TT):
                    sq = F(A_AT, 3, 512)[:, 2, :]
                    r = F(A_PROB, TT, 512)[:, t % TT, :]
                    pool.wait_ge(q_raw, at(g, LT + TT, t + 1))
                    hold()
                    pool.tensor_tensor(out=sq, in0=r, in1=r, op=ALU.mult).then_inc(q_sq, 1)
                    pool.wait_ge(q_sum, at(g, LT + TT, t + 1))
                    rstd(ss[:, 0:8], 8, DH, Steps(pool, pool_d, at(g, PD, t)), out=rs[:, 0:8] if t % 2 else rs2[:, 0:8]).then_inc(q_rstd, 1)
                for t in range(LT):
                    pool.wait_ge(ob_sum, at(g, LT, t + 1))
                    rstd(ss[:, 8:12], HG, 2 * DH, Steps(pool, pool_d, at(g, PD, LT + TT + t)),
                         out=rs[:, 8:12]).then_inc(ob_rstd, 1)
            pool.wait_ge(m_lo, KC)
            pool.memset(allone, 1.0).then_inc(ones_made, 1)
            for t in range(LT):
                pool.wait_ge(n2_sq, t + 1)
                rstd(ss[:, t:t + 1], 1, D, Steps(pool, pool_t, t), out=rs[:, t:t + 1], m0=t).then_inc(n2_rstd, 1)
            for t in range(LT):
                pool.wait_ge(route_ready, t + 1)
                for n in range(t * TOP_K, (t + 1) * TOP_K):
                    pool.indirect_dma_start(list_d, bass.IndirectOffsetOnAxis(ap=lrow[:, n:n + 1], axis=0),
                                            lval[:, n, :], None).then_inc(listed, 16)
            pool.wait_ge(listed, 16 * LT * TOP_K)
            pool.dma_start(listsb[:, :, :].rearrange("p (b e) w -> p b (e w)", b=4),
                           list_d.rearrange("(b p e) w -> p b (e w)", p=P, e=N_EXPERTS)).then_inc(list_back, 16)
            pool.wait_ge(items_ready, 1)
            pool.wait_ge(list_back, 16)
            n_items = pool.value_load(count_i[0:1, 0:1], min_val=N_EXPERTS, max_val=MAX_BLOCKS)

            def gather():
                pool.indirect_dma_start(F(A_XG, D), None, h2_d,
                                        bass.IndirectOffsetOnAxis(ap=nxt[:, 0:1], axis=0)).then_inc(gathered, 16)

            pool.tensor_copy(nxt[:, :], listsb[:, 0, :]).then_inc(pool_m, 1)
            eye3 = cst[0:96, C_EYE3:C_EYE3 + N_EXPERTS]
            pool.tensor_copy(sel[0:96, :], eye3[:, 0:1].broadcast_to((96, P))).then_inc(sel_ready, 1)
            pool.wait_ge(pool_m, 1)
            for k in range(2):
                pool.wait_ge(h2_stored[k], 16 * LT // 2)
            gather()
            with pool.Fori(0, MAX_BLOCKS) as i:
                with pool.If(i < n_items):
                    code = pool.value_load(items_i[0:1, bass.ds(i, 1)], min_val=0, max_val=4 * N_EXPERTS - 1)
                    code1 = pool.value_load(items_i[0:1, bass.ds(i + 1, 1)], min_val=0, max_val=4 * N_EXPERTS - 1)
                    e1 = pool.value_load(items_i[0:1, bass.ds(i + ITEMS + 1, 1)], min_val=0, max_val=N_EXPERTS - 1)
                    pool.tensor_copy(cur[:, :], listsb[:, bass.ds(code, 1), :].rearrange(
                        "p o w -> p (o w)")).then_inc(cur_ready, 1)
                    pool.wait_ge(xt_turned, at(i, 2, 2))
                    pool.wait_ge(gathered, at(i, 16, 16))
                    hold()
                    pool.tensor_copy(nxt[:, :], listsb[:, bass.ds(code1, 1), :].rearrange(
                        "p o w -> p (o w)")).then_inc(pool_m, 1)
                    pool.wait_ge(pool_m, at(i, 1, 2))
                    hold()
                    gather()
                    pool.wait_ge(sel_used, at(i, 1, 1))
                    hold()
                    pool.tensor_copy(sel[0:96, :], cst[0:96, bass.ds(e1 + C_EYE3, 1)].broadcast_to(
                        (96, P))).then_inc(sel_ready, 1)
                    pool.wait_ge(y_out, at(i, 2, 4))
                    hold()
                    pool.indirect_dma_start(acc_d, bass.IndirectOffsetOnAxis(ap=cur[:, 0:1], axis=0),
                                            F(A_Y, D), None, compute_op=ALU.add).then_inc(y_added, 16)
                    pool.wait_ge(y_added, at(i, 16, 16))
                    hold()
            pool.wait_ge(gathered, n_items * 16 + 16)
            hold()

        @block.scalar
        def _(act):
            def hi(base, per, i, j):
                s = j % NRAW
                if not (isinstance(i, int) and per * i + base + j - RET0 < NSPL):
                    act.wait_ge(w_used, at(i, per, base - RET0 + j - NSPL + 1))
                act.wait_ge(raw_loaded[s], at(i, 16 * per // NRAW, 16 * (base // NRAW + j // NRAW + 1)))
                act.activation(whi[:, j % NSPL, :, :], raw[:, s, :, :], ACT.Copy).then_inc(hi_made, 1)

            act.dma_start(cc[:, :, 0:1], a["c"].rearrange("o (k p) -> p k o", p=P),
                          allow_slow_non_contiguous=True).then_inc(s_cvec, 16)
            act.dma_start(cc[:, :, 1:2], a["c_ctx"].rearrange("(o k p) -> p k o", p=P, o=1),
                          allow_slow_non_contiguous=True).then_inc(s_cvec, 16)
            act.wait_ge(s_cvec, 32)
            act.activation(ct[:, :, :], cc[:, :, :], ACT.Tanh, scale=0.5).then_inc(c_tanh, 1)
            act.wait_ge(r_arg, 1)
            act.activation(lgt[:, 1, :], lgt[:, 0, :], ACT.Exp).then_inc(r_exp, 1)
            act.activation(lam[:, 2:4], lam[:, 0:2], ACT.Exp).then_inc(r_exp, 1)
            for t in range(TT):
                act.wait_ge(s_x, 16 * TT)
                if t:
                    act.wait_ge(x_sq, t)
                act.activation(F(A_SQ, D), F(A_X, TT, D)[:, t, :], ACT.Square,
                               accum_out=ss[:, t:t + 1]).then_inc(x_sq, 1)
            act.wait_ge(mod_rows, MOD_A)
            act.dma_start(mod_d[:, 0:2 * D], F(A_BMOD, 6 * D)[0:2, 0:2 * D]).then_inc(mod_stored, 16)
            act.wait_ge(mod_stored, 16)
            for k, (r, c0) in enumerate([(0, 0), (0, D), (1, 0), (1, D)]):
                act.dma_start(mcols[:, k, :], mod_d[r, c0:c0 + D].rearrange("(k p) -> p k", p=P),
                              allow_slow_non_contiguous=True).then_inc(mod_cols, 16)
            act.wait_ge(mod_vec, 1)
            for k in range(KC):
                act.wait_ge(h_turned, k + 1)
                act.activation(hhi[:, k, 0:L], ps[:, 2 * (k % 3), :], ACT.Identity,
                               bias=mcols[:, 0, k:k + 1], scale=mcols[:, 1, k:k + 1]).then_inc(h_hi, 1)
                act.activation(hhi[:, k, L:T], ps[:, 2 * (k % 3) + 1, 0:C], ACT.Identity,
                               bias=mcols[:, 2, k:k + 1], scale=mcols[:, 3, k:k + 1]).then_inc(h_hi, 1)
            hi(RET0, RET_N, 0, 0)
            hi(RET0, RET_N, 0, 1)
            act.wait_ge(mod_rows, 12)
            act.dma_start(mod_d[:, 2 * D:6 * D], F(A_BMOD, 6 * D)[0:2, 2 * D:6 * D]).then_inc(mod_stored, 16)
            act.wait_ge(mod_stored, 32)

            def used(base, per, i, j):
                act.wait_ge(w_used, at(i, per, base - RET0 + j + 1))

            with act.Fori(0, RET_HEADS) as h:
                B = (RET0, RET_N, h)
                act.wait_ge(r_head, at(h, 3, 3))
                act.activation(F(A_DEC, 1536)[:, 0:WIN], F(A_DEC, 1536)[:, 0:WIN], ACT.Exp).then_inc(r_exp, 1)
                act.activation(F(A_DEC, 1536)[:, WIN:WIN + 640], cst[:, C_WIN + 256:C_WIN + WIN], ACT.Exp,
                               scale=hs[:, 0:1], bias=hs[:, 2:3]).then_inc(r_exp, 1)
                act.activation(F(A_TMP, 1024)[:, 0:640], cst[:, C_WIN + 256:C_WIN + WIN], ACT.Exp,
                               scale=hs[:, 1:2], bias=hs[:, 3:4]).then_inc(r_exp, 1)
                hi(*B, 2)
                hi(*B, 3)
                used(*B, 1)
                rawqk = F(A_RAWQK, 4, L)
                for f in range(4):
                    act.activation(rawqk[:, f, :], ps[:, f, :], ACT.Copy,
                                   scale=DK ** -0.5 if f < 2 else 1.0).then_inc(qk_out, 1)
                act.activation(F(A_KT, 2, T)[:, :, L:T], ps[:, 4, :].rearrange("p (c n) -> p c n", c=2),
                               ACT.Copy).then_inc(qk_out, 1)
                hi(*B, 4)
                hi(*B, 5)
                used(*B, 3)
                for t in range(TT):
                    act.activation(F(A_V, TT, DV)[:, t, :], ps[:, (5 + t) % 8, :], ACT.Copy).then_inc(v_out, 1)
                hi(*B, 6)
                hi(*B, 7)
                used(*B, 5)
                for t in range(LT):
                    act.activation(F(A_GATE, LT, DV)[:, t, :], ps[:, 3 + t, :], ACT.Tanh,
                                   scale=0.5).then_inc(g_tanh, 1)
                for t in range(LT):
                    act.wait_ge(o_done, at(h, LT, t + 1))
                    if t:
                        act.wait_ge(o_sq, at(h, LT, t))
                    act.activation(F(A_TMP, L), ps[:, (5 + t) % 8, :], ACT.Square,
                                   accum_out=ss[:, t:t + 1]).then_inc(o_sq, 1)
                for c in range(4):
                    act.wait_ge(yt_done, at(h, LT, LT))
                    act.activation(yhi[:, c, :], ps[:, 1 + c, :], ACT.Identity,
                                   scale=hs[:, 4 + c:5 + c]).then_inc(yt_hi, 1)
                hi(*B, 8)
                hi(*B, 9)
            act_gate(act, hi, used, GA0, 0)
            act.wait_ge(gg_out, KC)
            act.dma_start(accr_d, F(A_ACC, 4096)).then_inc(accr_stored, 16)

            with act.Fori(0, GROUPS) as g:
                B = (DIFF0, DIFF_N, g)
                hi(*B, 2)
                hi(*B, 3)
                rawt = F(A_PROB, TT, 512)

                def tile_out(n, bank):
                    act.activation(rawt[:, n % TT, :], ps[:, bank, :], ACT.Copy).then_inc(q_raw, 1)

                used(*B, 1)
                for t in range(LT):
                    tile_out(t, t)
                hi(*B, 4)
                hi(*B, 5)
                used(*B, 3)
                for t in range(TT):
                    n = LT + t
                    if n >= TT:
                        q = n - TT
                        act.wait_ge(q_turned, at(g, LT + TT, q + 1))
                        act.activation(F(A_DQT, HG, L)[:, :, q * P:(q + 1) * P],
                                       ps[:, 2 + q % 2, :].rearrange("p (c n) -> p c n", c=HG),
                                       ACT.Copy).then_inc(q_out, 1)
                    tile_out(n, (4 + t) % 8)

                def k_turned(t):
                    act.wait_ge(q_turned, at(g, LT + TT, LT + t + 1))
                    act.activation(F(A_DKT, HG, T)[:, :, t * P:(t + 1) * P],
                                   ps[:, 2 + t % 2, :].rearrange("p (c n) -> p c n", c=HG),
                                   ACT.Copy).then_inc(q_out, 1)

                for t in range(3):
                    k_turned(t)
                hi(*B, 6)
                for t in range(3, TT - 1):
                    k_turned(t)
                used(*B, 5)
                for t in range(TT):
                    act.activation(F(A_DV, TT, 512)[:, t, :], ps[:, (4 + t) % 8, :],
                                   ACT.Copy).then_inc(dv_out, 1)
                k_turned(TT - 1)
                hi(*B, 7)
                NU = LT * HG

                def softmax(u, s):
                    act.wait_ge(mx_done, at(g, NU, u + 1))
                    act.activation(F(A_PROB, 2, 2, T)[:, u % 2, s, :],
                                   psf[:, (u % 2) * 1536 + s * T:(u % 2) * 1536 + (s + 1) * T],
                                   ACT.Exp, bias=nmx[:, u % 2, s:s + 1],
                                   accum_out=den[:, u % 2, s:s + 1]).then_inc(p_done, 1)

                def turned_out(u):
                    act.wait_ge(at_turned, at(g, NU, u + 1))
                    act.activation(F(A_AT, 2, T)[:, u % 2, :], psf[:, (u % 2) * 1536:(u % 2) * 1536 + T],
                                   ACT.Copy).then_inc(at_out, 1)

                def out_squares(qt):
                    act.wait_ge(ov_done, at(g, NU, HG * qt + HG))
                    for c in range(HG):
                        ins = act.activation(F(A_OY, 2, 512)[:, 0, c * P:(c + 1) * P], ps[:, 6 + qt % 2, c * P:(c + 1) * P],
                                             ACT.Square, scale=rd[:, qt % 2, c, 0:1], accum_out=ss[:, 8 + c:9 + c])
                    ins.then_inc(ob_sum, 1)

                def y_high(qt):
                    act.wait_ge(yd_turned, at(g, LT, qt + 1))
                    act.activation(yhi[:, :, qt * P:(qt + 1) * P],
                                   ps[:, 6 + qt % 2, :].rearrange("p (c n) -> p c n", c=HG),
                                   ACT.Identity, scale=dng[:, 0:1]).then_inc(yd_hi, 1)

                softmax(0, 0)
                softmax(0, 1)
                for u in range(NU):
                    turned_out(u)
                    if u + 1 < NU:
                        softmax(u + 1, 0)
                        softmax(u + 1, 1)
                    if u % HG == 0 and u:
                        out_squares(u // HG - 1)
                    if u % HG == 3 and u > HG:
                        y_high(u // HG - 1)
                out_squares(LT - 1)
                y_high(LT - 1)
                hi(*B, 8)
                hi(*B, 9)
            act.wait_ge(bd_out, KC * GROUPS)
            act.wait_ge(accr_stored, 16)
            act.dma_start(F(A_ACC2, 4096), accr_d).then_inc(accr_back, 16)

            def merged_high(c):
                act.wait_ge(m_sum, c + 1)
                if c == KH:
                    act.wait_ge(w_used, OUT0 - RET0)
                act.activation(mhi[c], F(A_ACC, KC, L)[:, c, :], ACT.Copy, scale=0.5).then_inc(m_hi, 1)

            act_gate(act, hi, used, GB0, 8, merged_high)
            for j in range(2, 4):
                hi(OUT0, 0, 0, j)
            for t in range(LT):
                act.wait_ge(xn_done, LT + t + 1)
                if t:
                    act.wait_ge(n2_sq, t)
                act.activation(F(A_ACC2, D), F(A_XN, LT, D)[:, t, :], ACT.Square,
                               accum_out=ss[:, t:t + 1]).then_inc(n2_sq, 1)
            act.wait_ge(n2_sq, LT)
            def gate_exp(t):
                act.wait_ge(g_arg, t + 1)
                act.activation(gate[:, t, :], topv[:, t, 4:8], ACT.Exp,
                               accum_out=gsum[:, t, 0:1]).then_inc(g_exp, 1)

            for t in range(LT):
                for q in range(2):
                    act.wait_ge(h2_turned, 2 * t + q + 1)
                    act.activation(F(A_H2T, KC, L)[:, 4 * q:4 * q + 4, t * P:(t + 1) * P],
                                   ps[:, q, :].rearrange("p (c n) -> p c n", c=4), ACT.Copy).then_inc(h2_out, 1)
                if t:
                    gate_exp(t - 1)
            gate_exp(LT - 1)
            def hi_e(i, j):
                if isinstance(i, int):
                    act.wait_ge(w_used, MOE0 - RET0)
                else:
                    act.wait_ge(e_used, at(i, MOE_N, j - ESPL + 1))
                act.wait_ge(e_loaded[j % ERAW], at(i, 16 * MOE_N // ERAW, 16 * (j // ERAW + 1)))
                act.activation(e_whi[j % ESPL], e_raw[j % ERAW], ACT.Copy).then_inc(e_hi, 1)

            xthi = yhi[:, 0:2, :].rearrange("p a (k n) -> p (a k) n", n=P)
            acthi = ylo[:, 0:2, :].rearrange("p a (k n) -> p (a k) n", n=P)

            def x_high(n):
                for q in range(2):
                    act.wait_ge(xt_turned, n + q)
                    act.activation(xthi[:, 4 * q:4 * q + 4, :], ps[:, q, :].rearrange("p (c n) -> p c n", c=4),
                                   ACT.Copy).then_inc(xt_hi, 1)

            for j in range(ESPL):
                hi_e(0, j)
            act.wait_ge(items_ready, 1)
            n_items = act.value_load(count_i[0:1, 0:1], min_val=N_EXPERTS, max_val=MAX_BLOCKS)
            x_high(1)
            act.sem_inc(y_out, 2)
            with act.Fori(0, MAX_BLOCKS) as i:
                with act.If(i < n_items):
                    def tanh(hf):
                        act.wait_ge(glu_min, at(i, 2, hf + 1))
                        act.activation(F(A_TH, COL), F(A_GS, COL), ACT.Tanh, scale=0.5 * ALPHA).then_inc(glu_tanh, 1)

                    def act_high(hf):
                        act.wait_ge(act_turned, at(i, 2, hf + 1))
                        act.activation(acthi[:, 4 * hf:4 * hf + 4, :],
                                       ps[:, 2 * hf, :].rearrange("p (c n) -> p c n", c=4),
                                       ACT.Copy, scale=0.5).then_inc(act_hi, 1)

                    hi_e(i, 4)
                    tanh(0)
                    for j in range(5, 9):
                        hi_e(i, j)
                    tanh(1)
                    act_high(0)
                    for j in range(9, 12):
                        hi_e(i, j)
                    x_high(at(i, 2, 3))
                    act_high(1)
                    for j in range(12, 16):
                        hi_e(i, j)
                    act.wait_ge(cur_ready, at(i, 1, 1))
                    act.wait_ge(e_used, at(i, MOE_N, MOE_N))
                    for c in range(2):
                        act.activation(F(A_Y, D)[:, c * COL:(c + 1) * COL], ps[:, 6 + c, :], ACT.Copy,
                                       scale=cur[:, 1:2].bitcast(F32)).then_inc(y_out, 1)

        @block.vector
        def _(dve):
            V = nc.vector
            st = Steps(dve, dve_pre)

            def lo(base, per, i, j):
                s = j % NRAW
                dve.wait_ge(hi_made, at(i, per, base - RET0 + j + 1))
                dve.wait_ge(raw_loaded[s], at(i, 16 * per // NRAW, 16 * (base // NRAW + j // NRAW + 1)))
                V.tensor_tensor(wlo[:, j % NSPL, :, :], raw[:, s, :, :], whi[:, j % NSPL, :, :].bitcast(F32),
                                ALU.subtract).then_inc(lo_made, 1)

            def branch_ready(base, per, i, done, f):
                if f % 4 == 3:
                    dve.wait_ge(w_used, at(i, per, base - RET0 + 6 + f // 4 + 1))
                else:
                    dve.wait_ge(done, at(i, 6, f // 4 * 3 + f % 4 + 1))

            dve.wait_ge(c_tanh, 1)
            st.did(V.scalar_tensor_tensor(out=ct[:, :, :], in0=ct[:, :, :], scalar=1.0, in1=cc[:, :, :],
                                          op0=ALU.add, op1=ALU.mult))
            st.wait()
            V.tensor_scalar(ct[:, :, :], ct[:, :, :], 0.5, None, ALU.mult).then_inc(c_silu, 1)
            dve.wait_ge(s_small, 16 * 10)
            st.did(V.tensor_scalar(lgt[:, 2, :], lgx[:, :], -1.0, None, ALU.mult))
            st.wait()
            st.did(V.tensor_tensor(lgt[:, 0, :], lgx[:, :], lgt[:, 2, :], ALU.min))
            st.did(V.tensor_tensor(lamt[:, 0:4:2, :], lamt[:, 0:4:2, :], lamt[:, 1:4:2, :], ALU.mult))
            st.wait()
            V.tensor_reduce(lam[:, 0:2], lamt[:, 0:4:2, :], AX.X, ALU.add).then_inc(r_arg, 1)
            dve.wait_ge(r_exp, 2)
            st.did(V.tensor_scalar(lgt[:, 2, :], lgt[:, 1, :], 2.0, None, ALU.add))
            st.wait()
            st.did(V.reciprocal(lgt[:, 3, :], lgt[:, 2, :]))
            st.wait()
            st.did(V.tensor_tensor(lgt[:, 1, :], lgt[:, 1, :], lgt[:, 3, :], ALU.mult))
            st.wait()
            st.did(V.tensor_tensor(lgt[:, 2, :], lgt[:, 1, :], lgt[:, 1, :], ALU.mult))
            st.wait()
            st.did(V.tensor_scalar(lgt[:, 3, :], lgt[:, 2, :], 2.0 / 17, 2.0 / 15, ALU.mult, ALU.add))
            for n in (13, 11, 9, 7, 5, 3, 1):
                st.wait()
                st.did(V.tensor_tensor(lgt[:, 3, :], lgt[:, 3, :], lgt[:, 2, :], ALU.mult))
                st.wait()
                st.did(V.tensor_scalar(lgt[:, 3, :], lgt[:, 3, :], 2.0 / n, None, ALU.add))
            st.wait()
            st.did(V.tensor_tensor(lgt[:, 3, :], lgt[:, 3, :], lgt[:, 1, :], ALU.mult))
            st.did(V.tensor_scalar(lgt[:, 0, :], lgx[:, :], 0.0, None, ALU.min))
            st.wait()
            st.did(V.tensor_tensor(lgt[:, 0, :], lgt[:, 0, :], lgt[:, 3, :], ALU.subtract))
            st.wait()
            lf = lgt[:, 0, 0:RET_HEADS].unsqueeze(2)
            lb = lgt[:, 0, RET_HEADS:8].unsqueeze(2)
            st.did(V.tensor_scalar(hsc[:, :, 0:1], lf, 1.0, None, ALU.mult))
            st.did(V.tensor_scalar(hsc[:, :, 1:2], lb, -1.0, None, ALU.mult))
            st.did(V.tensor_scalar(hsc[:, :, 2:3], lf, float(C), None, ALU.mult))
            st.did(V.tensor_scalar(hsc[:, :, 3:4], lb, float(L), None, ALU.mult))
            st.did(V.tensor_scalar(hsc[:, :, 4:8], hsc[:, :, 4:8], 0.5, None, ALU.mult))
            st.did(V.tensor_scalar(gqk[:, 0, :], gqk[:, 0, :], DH ** -0.5, None, ALU.mult))
            st.did(V.tensor_scalar(dng[:, :], dng[:, :], 1.0 - LAMBDA_INIT, None, ALU.mult))
            st.did(V.tensor_tensor(lam[:, 4:5], lam[:, 3:4], lam[:, 2:3], ALU.subtract))
            st.wait()
            st.did(V.tensor_scalar(lam[:, 5:6], lam[:, 4:5], -LAMBDA_INIT, None, ALU.add))
            dve.wait_ge(s_const, 16)

            dve.wait_ge(s_bmod, 16)
            bm = F(A_BMOD, 12, COL)

            def mod_row(c):
                dve.wait_ge(mod_used, 2 * c + 2)
                V.tensor_tensor(bm[0:2, c, :], ps[0:2, mod_bank(c), :], bm[0:2, c, :], ALU.add).then_inc(mod_rows, 1)

            for c in range(MOD_A):
                mod_row(c)
            dve.wait_ge(x_rstd, 1)
            for t in range(TT):
                V.tensor_scalar(F(A_X, TT, D)[:, t, :], F(A_X, TT, D)[:, t, :], rs[:, t:t + 1], None,
                                ALU.mult).then_inc(x_normed, 1)
            dve.wait_ge(mod_cols, 64)
            st.did(V.scalar_tensor_tensor(out=mcols[:, 1, :], in0=mcols[:, 1, :], scalar=1.0, in1=mcols[:, 4, :],
                                          op0=ALU.add, op1=ALU.mult))
            V.scalar_tensor_tensor(out=mcols[:, 3, :], in0=mcols[:, 3, :], scalar=1.0, in1=mcols[:, 4, :],
                                   op0=ALU.add, op1=ALU.mult).then_inc(mod_vec, 1)
            dve.wait_ge(mod_vec, 1)
            tm = F(A_SQ, 2, COL)
            for k in range(KC):
                if k >= 3:
                    for c in MOD_BEFORE[k]:
                        mod_row(c)
                for s, (n0, n1) in enumerate(((0, L), (L, T))):
                    dve.wait_ge(h_hi, 2 * k + s + 1)
                    if k:
                        dve.wait_ge(h_lo, 2 * (k - 1) + s + 1)
                    st.did(V.tensor_scalar(tm[:, s, 0:n1 - n0], ps[:, 2 * (k % 3) + s, 0:n1 - n0],
                                           mcols[:, 2 * s + 1, k:k + 1], mcols[:, 2 * s, k:k + 1], ALU.mult, ALU.add))
                    st.wait()
                    V.tensor_tensor(hlo[:, k, n0:n1], tm[:, s, 0:n1 - n0], hhi[:, k, n0:n1].bitcast(F32),
                                    ALU.subtract).then_inc(h_lo, 1)
            lo(RET0, RET_N, 0, 0)
            mod_row(11)
            acc = F(A_ACC, KC, L)
            dve.wait_ge(s_init, 16 * (4 + 2 + LT))
            dve.wait_ge(h_lo, 2 * KC)
            RS = 7
            with dve.Fori(0, RET_HEADS) as h:
                B = (RET0, RET_N, h)
                sr = Steps(dve, r_step, h * RS)
                win = cst[:, C_WIN:C_WIN + WIN]
                dec = F(A_DEC, 1536)
                V.tensor_scalar(hs[:, :], hsc[:, bass.ds(h, 1), :].rearrange("p o n -> p (o n)"), 1.0, None,
                                ALU.mult).then_inc(r_head, 1)
                dve.wait_ge(r_head, at(h, 3, 1))
                sr.did(V.tensor_scalar(dec[:, 0:WIN], win, 0.0, hs[:, 0:1], ALU.max, ALU.mult))
                V.tensor_scalar(F(A_TMP, 1024)[:, 0:WIN], win, 0.0, hs[:, 1:2], ALU.min, ALU.mult).then_inc(r_head, 1)
                sr.wait()
                dve.wait_ge(r_head, at(h, 3, 2))
                V.tensor_tensor(dec[:, 0:WIN], dec[:, 0:WIN], F(A_TMP, 1024)[:, 0:WIN], ALU.add).then_inc(r_head, 1)
                lo(*B, 1)
                dve.wait_ge(r_exp, at(h, 3, 5))
                sr.did(V.tensor_tensor(dec[:, WIN:WIN + 640], dec[:, WIN:WIN + 640], F(A_TMP, 1024)[:, 0:640], ALU.add))
                sr.did(V.tensor_tensor(dec[:, L - P:L], dec[:, L - P:L], ident, ALU.add))
                lo(*B, 2)
                lo(*B, 3)
                rawqk = F(A_RAWQK, 4, L)
                tmp = F(A_TMP, 2, L)
                c0 = C_ROPE_R
                sr.wait()
                for f in range(4):
                    dve.wait_ge(qk_out, at(h, 5, f + 1))
                    if f:
                        dve.wait_ge(rope_done, at(h, 4, f))
                    if f % 2 == 0:
                        cos = cst[:, c0:c0 + GRID_H].unsqueeze(2).broadcast_to((P, GRID_H, GRID_W))
                        sin = cst[:, c0 + GRID_H:c0 + 2 * GRID_H].unsqueeze(2).broadcast_to((P, GRID_H, GRID_W))
                    else:
                        b0 = c0 + 2 * GRID_H
                        cos = cst[:, b0:b0 + GRID_W].unsqueeze(1).broadcast_to((P, GRID_H, GRID_W))
                        sin = cst[:, b0 + GRID_W:b0 + 2 * GRID_W].unsqueeze(1).broadcast_to((P, GRID_H, GRID_W))
                    grid = lambda v: v.rearrange("p (r c) -> p r c", c=GRID_W)
                    V.tensor_tensor(grid(tmp[:, 0, :]), grid(rawqk[:, f, :]), cos, ALU.mult)
                    V.tensor_tensor(grid(tmp[0:64, 1, :]), grid(rawqk[64:128, f, :]), sin[64:128], ALU.mult)
                    sr.did(V.tensor_tensor(grid(tmp[64:128, 1, :]), grid(rawqk[0:64, f, :]), sin[0:64], ALU.mult))
                    sr.wait()
                    dst = F(A_QT, 2, L)[:, f, :] if f < 2 else F(A_KT, 2, T)[:, f - 2, 0:L]
                    V.tensor_tensor(dst, tmp[:, 0, :], tmp[:, 1, :], ALU.add).then_inc(rope_done, 1)
                lo(*B, 4)
                lo(*B, 5)
                lo(*B, 6)
                gt = F(A_GATE, LT, DV)
                for t in range(LT):
                    dve.wait_ge(g_tanh, at(h, LT, t + 1))
                    V.scalar_tensor_tensor(out=gt[:, t, :], in0=gt[:, t, :], scalar=1.0, in1=ps[:, 3 + t, :],
                                           op0=ALU.add, op1=ALU.mult).then_inc(g_out, 1)
                lo(*B, 7)
                sr.wait()
                for m in range(TT):
                    dve.wait_ge(sc_done, at(h, TT, m + 1))
                    w0 = L - P - P * m if m < LT else WIN + P - P * (m - LT)
                    V.tensor_tensor(F(A_RAWQK, TT, L)[:, m, :], ps[:, (7 + m) % 8, :], dec[:, w0:w0 + L],
                                    ALU.mult).then_inc(pt_done, 1)
                dve.wait_ge(o_rstd, at(h, 1, 1))
                dve.wait_ge(g_out, at(h, LT, LT))
                for t in range(LT):
                    V.scalar_tensor_tensor(out=gt[:, t, :], in0=ps[:, (5 + t) % 8, :], scalar=rs[:, t:t + 1],
                                           in1=gt[:, t, :], op0=ALU.mult, op1=ALU.mult).then_inc(y_done, 1)
                for c in range(4):
                    dve.wait_ge(yt_hi, at(h, 4, c + 1))
                    V.scalar_tensor_tensor(out=ylo[:, c, :], in0=ps[:, 1 + c, :], scalar=hs[:, 4 + c:5 + c],
                                           in1=yhi[:, c, :].bitcast(F32), op0=ALU.mult,
                                           op1=ALU.subtract).then_inc(yt_lo, 1)
                for f in range(KC):
                    if f == 4:
                        lo(*B, 8)
                    branch_ready(*B, br_done, f)
                    V.tensor_tensor(acc[:, f, :], acc[:, f, :], ps[:, branch_bank(f), :], ALU.add).then_inc(br_out, 1)
                assert sr.k == RS, sr.k
            dve_gate(dve, lo, GA0, 0)

            sq = F(A_AT, 3, 512)
            with dve.Fori(0, GROUPS) as g:
                B = (DIFF0, DIFF_N, g)
                NQ = LT + TT
                NU = LT * HG
                DS = 8 * 6 + 2 * 1 + 2 * NU + LT
                sd = Steps(dve, d_step, g * DS)
                lo(*B, 1)
                lo(*B, 2)
                lo(*B, 3)
                rawt = F(A_PROB, TT, 512)

                def norm_rope(n):
                    r = rawt[:, n % TT, :]
                    heads = lambda v: v.rearrange("p (g d) -> p g d", d=DH)
                    is_k, t = (0, n) if n < LT else (1, n - LT)
                    dve.wait_ge(q_raw, at(g, NQ, n + 1))
                    if n:
                        dve.wait_ge(q_ready, at(g, NQ, n))
                    dve.wait_ge(q_sq, at(g, NQ, n + 1))
                    V.tensor_reduce(ss[:, 0:8], heads(sq[:, 2, :]), AX.X, ALU.add).then_inc(q_sum, 1)
                    sd.did(V.tensor_tensor(heads(r), heads(r), gqk[:, is_k, :].unsqueeze(1).broadcast_to((P, 8, DH)),
                                           ALU.mult))
                    sd.wait()
                    if t < LT:
                        tab = cst[:, C_ROPE_D + t * 2 * DH:C_ROPE_D + (t + 1) * 2 * DH]
                        cos = tab[:, 0:DH].unsqueeze(1).broadcast_to((P, 8, DH))
                        V.tensor_tensor(heads(sq[:, 0, :]), heads(r), cos, ALU.mult)
                        halves = lambda v: v.rearrange("p (g s d) -> p g s d", s=2, d=16)
                        sin = tab[:, DH:2 * DH].rearrange("p (a s d) -> p a s d", s=2, d=16)
                        for hf in range(2):
                            for ax in range(2):
                                pick = lambda v, s: v.rearrange("p (g x s d) -> p g x s d", x=2, s=2, d=16)[:, :, ax, s, :]
                                sd.did(V.tensor_tensor(pick(sq[:, 1, :], hf), pick(r, 1 - hf),
                                                       sin[:, ax, hf, :].unsqueeze(1).broadcast_to((P, 8, 16)),
                                                       ALU.mult))
                        sd.wait()
                        sd.did(V.tensor_tensor(r, sq[:, 0, :], sq[:, 1, :], ALU.add))
                        sd.wait()
                    dve.wait_ge(q_rstd, at(g, NQ, n + 1))
                    V.tensor_tensor(heads(r), heads(r), (rs if n % 2 else rs2)[:, 0:8].unsqueeze(2).broadcast_to((P, 8, DH)),
                                    ALU.mult).then_inc(q_ready, 1)

                for n in range(LT):
                    norm_rope(n)
                lo(*B, 4)
                lo(*B, 5)
                for n in range(LT, TT):
                    norm_rope(n)
                for n in range(TT, NQ):
                    norm_rope(n)
                lo(*B, 6)
                lo(*B, 7)

                def biggest(u):
                    dve.wait_ge(s_done, at(g, NU, u + 1))
                    s0 = (u % 2) * 1536
                    V.tensor_reduce(nmx[:, u % 2, :], psf[:, s0:s0 + 2 * T].rearrange("p (s n) -> p s n", s=2),
                                    AX.X, ALU.max, negate=True).then_inc(mx_done, 1)

                def combine(u):
                    pr = F(A_PROB, 2, 2, T)[:, u % 2]
                    r = rd[:, u // HG % 2, u % HG, :]
                    dve.wait_ge(p_done, at(g, 2 * NU, 2 * u + 2))
                    sd.did(V.reciprocal(r, den[:, u % 2, :]))
                    sd.wait()
                    sd.did(V.scalar_tensor_tensor(out=ratio[:, u % 2, :], in0=r[:, 1:2], scalar=den[:, u % 2, 0:1],
                                                  in1=lam[:, 5:6], op0=ALU.mult, op1=ALU.mult))
                    sd.wait()
                    V.scalar_tensor_tensor(out=pr[:, 0, :], in0=pr[:, 1, :], scalar=ratio[:, u % 2, :], in1=pr[:, 0, :],
                                           op0=ALU.mult, op1=ALU.add).then_inc(a_done, 1)

                def out_tile(qt):
                    heads = lambda v: v.rearrange("p (g d) -> p g d", d=2 * DH)
                    dve.wait_ge(ob_rstd, at(g, LT, qt + 1))
                    if qt:
                        dve.wait_ge(yd_turned, at(g, LT, qt))
                    sd.did(V.tensor_tensor(yscale[:, :], rs[:, 8:12], rd[:, qt % 2, :, 0:1].rearrange("p g o -> p (g o)"),
                                           ALU.mult))
                    sd.wait()
                    V.tensor_tensor(heads(F(A_OY, 2, 512)[:, 1, :]), heads(ps[:, 6 + qt % 2, :]),
                                    yscale[:, :].unsqueeze(2).broadcast_to((P, HG, 2 * DH)), ALU.mult).then_inc(yd_done, 1)

                def y_low(qt):
                    dve.wait_ge(yd_hi, at(g, LT, qt + 1))
                    cols = lambda v: v[:, :, qt * P:(qt + 1) * P]
                    V.scalar_tensor_tensor(out=cols(ylo), in0=ps[:, 6 + qt % 2, :].rearrange("p (c n) -> p c n", c=HG),
                                           scalar=dng[:, 0:1], in1=cols(yhi).bitcast(F32), op0=ALU.mult,
                                           op1=ALU.subtract).then_inc(yd_lo, 1)

                for u in range(NU):
                    biggest(u)
                    combine(u)
                    if u % HG == 2 and u > HG:
                        out_tile(u // HG - 1)
                    if u % HG == 0 and u > HG:
                        y_low(u // HG - 2)
                y_low(LT - 2)
                out_tile(LT - 1)
                y_low(LT - 1)
                dve.wait_ge(acc_zeroed, 1)
                for f in range(KC):
                    if f == 4:
                        lo(*B, 8)
                    branch_ready(*B, bd_done, f)
                    V.tensor_tensor(acc[:, f, :], acc[:, f, :], ps[:, branch_bank(f), :], ALU.add).then_inc(bd_out, 1)
                assert sd.k == DS, sd.k
            tl = Steps(dve, tail)
            acc2 = F(A_ACC2, KC, L)

            def merged(c):
                if c == 0:
                    dve.wait_ge(accr_back, 16)
                dve.wait_ge(gg_out, KC + c + 1)
                V.tensor_tensor(acc[:, c, :], acc[:, c, :], acc2[:, c, :], ALU.add).then_inc(m_sum, 1)

            def merged_low(c):
                dve.wait_ge(m_hi, c + 1)
                V.scalar_tensor_tensor(out=mlo[c], in0=acc[:, c, :], scalar=0.5, in1=mhi[c].bitcast(F32),
                                       op0=ALU.mult, op1=ALU.subtract).then_inc(m_lo, 1)

            dve_gate(dve, lo, GB0, 8, merged, merged_low)
            bias = F(A_BIAS, 1536).bitcast(BF16)
            dve.wait_ge(m_lo, KC)
            lo(OUT0, 0, 0, 1)
            lo(OUT0, 0, 0, 2)
            bias_thirds(dve, tl, bias, 0)
            xn = F(A_XN, LT, D)
            dve.wait_ge(x_again, 16 * LT)
            dve.wait_ge(vec2, 16 * 5)
            tl.did(V.scalar_tensor_tensor(out=F(A_A2B, D), in0=F(A_A2B, D), scalar=1.0, in1=F(A_HT, D),
                                          op0=ALU.add, op1=ALU.mult))
            def new_x(c, t):
                if t == 0 and c == 0:
                    dve.wait_ge(w_used, OUT0 - RET0 + 2)
                elif c == 1 and t < LT - 1:
                    dve.wait_ge(xp_done, t + 1)
                elif c == 1:
                    dve.wait_ge(w_used, MOE0 - RET0)
                tmpx = cst[:, (C_WIN, C_ROPE_D)[t % 2]:(C_WIN, C_ROPE_D)[t % 2] + COL]
                if 4 * c + t >= 2:
                    dve.wait_ge(xn_done, 4 * c + t - 1)
                tl.did(V.tensor_tensor(tmpx, ps[:, 4 * c + t, :], F(A_GAB, D)[:, c * COL:(c + 1) * COL], ALU.mult))
                tl.wait()
                V.tensor_tensor(xn[:, t, c * COL:(c + 1) * COL], xn[:, t, c * COL:(c + 1) * COL], tmpx,
                                ALU.add).then_inc(xn_done, 1)

            def norm2(t):
                ht = F(A_HT, 2, D)[:, t % 2, :]
                dve.wait_ge(n2_rstd, t + 1)
                if t >= 2:
                    dve.wait_ge(h2_turned, 2 * (t - 2) + 2)
                    dve.wait_ge(h2_stored[t % 2], 16 * (t // 2))
                tl.did(V.scalar_tensor_tensor(out=ht, in0=xn[:, t, :], scalar=rs[:, t:t + 1], in1=F(A_A2B, D),
                                              op0=ALU.mult, op1=ALU.mult))
                tl.wait()
                V.tensor_tensor(ht, ht, F(A_SH2B, D), ALU.add).then_inc(n2_done, 1)

            for t in range(LT):
                new_x(0, t)
            lo(OUT0, 0, 0, 3)
            bias_thirds(dve, tl, bias, 1)
            bias_thirds(dve, tl, bias, 2)
            for t in range(LT):
                new_x(1, t)
                if 1 <= t <= 2:
                    norm2(t - 1)
            norm2(2)
            norm2(3)
            iota = cst[:, C_IOTA:C_IOTA + N_EXPERTS]
            def choose(t):
                dve.wait_ge(lg_done, t + 1)
                tl.did(V.tensor_tensor(logit[:, t, :], ps[:, 2 + t % 2, 0:N_EXPERTS], rb[:, :], ALU.add))
                tl.wait()
                tl.did(V.max(topv[:, t, :], logit[:, t, :]))
                tl.wait()
                tl.did(V.max_index(topi[:, t, :], topv[:, t, :], logit[:, t, :]))
                tl.wait()
                tl.did(V.tensor_copy(topf[:, t, :], topi[:, t, :]))
                V.tensor_scalar(topv[:, t, 4:8], topv[:, t, 0:4], topv[:, t, 0:1], None, ALU.subtract).then_inc(g_arg, 1)
                tl.wait()
                for k in range(TOP_K):
                    tl.did(V.tensor_scalar(onehot[:, t * TOP_K + k, :], iota, topf[:, t, k:k + 1], None, ALU.is_equal))
                tl.wait()
                tl.did(V.tensor_tensor(mask3[:, t, 0:32], onehot[:, t * TOP_K, :], onehot[:, t * TOP_K + 1, :], ALU.add))
                tl.did(V.tensor_tensor(mask3[:, t, 32:64], onehot[:, t * TOP_K + 2, :], onehot[:, t * TOP_K + 3, :],
                                       ALU.add))
                tl.wait()
                tl.did(V.tensor_tensor(mask3[:, t, 0:32], mask3[:, t, 0:32], mask3[:, t, 32:64], ALU.add))
                tl.wait()
                tl.did(V.tensor_copy(mask3[:, t, 32:64], mask3[:, t, 0:32]))
                V.tensor_copy(mask3[:, t, 64:96], mask3[:, t, 0:32]).then_inc(m_ready, 1)
            lvf = lval[:, :, :].bitcast(F32)

            def place(t):
                n0, n1 = t * TOP_K, (t + 1) * TOP_K
                dve.wait_ge(g_exp, t + 1)
                tl.did(V.reciprocal(gsum[:, t, 1:2], gsum[:, t, 0:1]))
                tl.wait()
                tl.did(V.tensor_scalar(lvf[:, n0:n1, 1:2], gate[:, t, :].unsqueeze(2), gsum[:, t, 1:2], None, ALU.mult))
                tl.did(V.tensor_copy(lval[:, n0:n1, 0:1],
                                     cst[:, C_TOK + t:C_TOK + t + 1].unsqueeze(1).broadcast_to((P, TOP_K, 1))))
                dve.wait_ge(pos_done, t + 1)
                for n in range(n0, n1):
                    tl.wait()
                    tl.did(V.tensor_tensor_reduce(out=junk32[:, :], in0=onehot[:, n, :], in1=ps[:, 4 + t, 0:N_EXPERTS],
                                                  scale=1.0, scalar=0.0, op0=ALU.mult, op1=ALU.add,
                                                  accum_out=slot[:, n:n + 1]))
                tl.wait()
                V.scalar_tensor_tensor(out=lrow[:, n0:n1], in0=slot[:, n0:n1], scalar=float(N_EXPERTS),
                                       in1=topf[:, t, 0:TOP_K], op0=ALU.mult, op1=ALU.add).then_inc(route_ready, 1)

            dve.wait_ge(rw_loaded, 32)
            for t in range(LT):
                choose(t)
                if t:
                    place(t - 1)
            place(LT - 1)
            dve.wait_ge(cnt_done, 1)
            V.tensor_scalar(small[0:96, 0:1], ps[0:96, 0, 0:1], cst[0:96, C_THR:C_THR + 1], None,
                            ALU.is_gt).then_inc(flag_ready, 1)
            dve.wait_ge(opos_done, 1)
            tl.did(V.tensor_copy(small[0:96, 1:2], ps[0:96, 0, 0:1]))
            tl.wait()
            dve.wait_ge(flag_ready, 1)
            V.tensor_scalar(small[0:96, 8:8 + OVER + 1], iota[0:96, 0:OVER + 1], small[0:96, 1:2], small[0:96, 0:1],
                            ALU.is_equal, ALU.mult).then_inc(oh_ready, 1)
            dve.wait_ge(items_done, 1)
            for q in range(2):
                tl.did(V.tensor_copy(items_i[0:1, q * ITEMS:q * ITEMS + N_EXPERTS], iota[0:1, :]))
                tl.did(V.tensor_copy(items_i[0:1, q * ITEMS + N_EXPERTS:(q + 1) * ITEMS],
                                     ps[0:1, 0, q * (OVER + 1):(q + 1) * (OVER + 1)]))
            V.tensor_scalar(count_i[0:1, 0:1], ps[0:1, 0, 2 * (OVER + 1):2 * (OVER + 1) + 1], float(N_EXPERTS), None,
                            ALU.add).then_inc(items_ready, 1)
            xthi = yhi[:, 0:2, :].rearrange("p a (k n) -> p (a k) n", n=P)
            xtlo = yhi[:, 2:4, :].rearrange("p a (k n) -> p (a k) n", n=P)
            acthi = ylo[:, 0:2, :].rearrange("p a (k n) -> p (a k) n", n=P)
            actlo = ylo[:, 2:4, :].rearrange("p a (k n) -> p (a k) n", n=P)

            def x_low(n):
                for q in range(2):
                    dve.wait_ge(xt_hi, n + q)
                    V.tensor_tensor(xtlo[:, 4 * q:4 * q + 4, :], ps[:, q, :].rearrange("p (c n) -> p c n", c=4),
                                    xthi[:, 4 * q:4 * q + 4, :].bitcast(F32), ALU.subtract).then_inc(xt_lo, 1)

            def lo_e(i, j):
                dve.wait_ge(e_hi, at(i, MOE_N, j + 1))
                dve.wait_ge(e_loaded[j % ERAW], at(i, 16 * MOE_N // ERAW, 16 * (j // ERAW + 1)))
                V.tensor_tensor(e_wlo[j % ESPL], e_raw[j % ERAW], e_whi[j % ESPL].bitcast(F32),
                                ALU.subtract).then_inc(e_lo, 1)

            for j in range(ESPL):
                lo_e(0, j)
            dve.wait_ge(items_ready, 1)
            n_items = dve.value_load(count_i[0:1, 0:1], min_val=N_EXPERTS, max_val=MAX_BLOCKS)
            x_low(1)
            MS = 4
            with dve.Fori(0, MAX_BLOCKS) as i:
                with dve.If(i < n_items):
                    ms = Steps(dve, moe_step, i * MS)

                    def used(j):
                        dve.wait_ge(e_used, at(i, MOE_N, j + 1))

                    def glu(hf):
                        used(4 * hf + 1)
                        V.tensor_scalar(F(A_GS, COL), ps[:, 2 + 2 * hf, :], LIMIT, None, ALU.min).then_inc(glu_min, 1)

                    def activate(hf):
                        used(4 * hf + 3)
                        ms.did(V.tensor_scalar(F(A_LS, COL), ps[:, 3 + 2 * hf, :], -LIMIT, LIMIT, ALU.max, ALU.min))
                        dve.wait_ge(glu_tanh, at(i, 2, hf + 1))
                        ms.did(V.scalar_tensor_tensor(out=F(A_GS, COL), in0=F(A_TH, COL), scalar=1.0, in1=F(A_GS, COL),
                                                      op0=ALU.add, op1=ALU.mult))
                        ms.wait()
                        V.scalar_tensor_tensor(out=F(A_AC, 2, COL)[:, hf, :], in0=F(A_LS, COL), scalar=1.0,
                                               in1=F(A_GS, COL), op0=ALU.add, op1=ALU.mult).then_inc(act_done, 1)

                    def act_low(hf):
                        dve.wait_ge(act_hi, at(i, 2, hf + 1))
                        V.scalar_tensor_tensor(out=actlo[:, 4 * hf:4 * hf + 4, :],
                                               in0=ps[:, 2 * hf, :].rearrange("p (c n) -> p c n", c=4), scalar=0.5,
                                               in1=acthi[:, 4 * hf:4 * hf + 4, :].bitcast(F32), op0=ALU.mult,
                                               op1=ALU.subtract).then_inc(act_lo, 1)

                    lo_e(i, 4)
                    glu(0)
                    lo_e(i, 5)
                    activate(0)
                    lo_e(i, 6)
                    lo_e(i, 7)
                    dve.wait_ge(act_done, at(i, 2, 1))
                    glu(1)
                    lo_e(i, 8)
                    act_low(0)
                    activate(1)
                    lo_e(i, 9)
                    lo_e(i, 10)
                    act_low(1)
                    x_low(at(i, 2, 3))
                    for j in range(11, 16):
                        lo_e(i, j)
                    assert ms.k == MS
            fin = Steps(dve, tail, tl.k)
            for t in range(LT):
                s = F(A_XG if t == 0 else A_Y if t == 1 else A_GS if t == 2 else A_HT, D)
                dve.wait_ge(acc_back[t], 16)
                fin.did(V.tensor_tensor(s, s, F(A_GFB, D), ALU.mult))
                fin.wait()
                V.tensor_tensor(xn[:, t, :], xn[:, t, :], s, ALU.add).then_inc(res_ready, 1)

        @block.tensor
        def _(pe):
            def mm(out, lhsT, rhs, start, stop, skip=False):
                return pe.matmul(out, lhsT, rhs, start=start, stop=stop, skip_group_check=skip)

            def split_ready(base, per, i, j):
                pe.wait_ge(lo_made, at(i, per, base - RET0 + j + 1))

            def proj_tokens(base, per, i, j0, tiles, bank, ready=None, half=None, xh=None, xl=None,
                            tile_done=None, between=None):
                xh = xh or [hhi[:, k, :] for k in range(KC)]
                xl = xl or [hlo[:, k, :] for k in range(KC)]
                for kh in range(2):
                    j = j0 + kh
                    split_ready(base, per, i, j)
                    if half:
                        half(kh)
                    order = [(kq, t) for kq in range(KH) for t in range(tiles)]
                    if tile_done and kh == 1:
                        order.sort(key=lambda x: x[1])
                    for kq, t in order:
                        kk = KH * kh + kq
                        if kk == 0 and ready:
                            ready(t)
                        o = ps[:, bank(t), :]
                        wh, wl = whi[:, j % NSPL, kq, :], wlo[:, j % NSPL, kq, :]
                        lh, ll = xh[kk][:, t * P:(t + 1) * P], xl[kk][:, t * P:(t + 1) * P]
                        mm(o, lh, wh, kk == 0, False)
                        mm(o, lh, wl, False, False)
                        last = mm(o, ll, wh, False, kk == KC - 1)
                        if tile_done and kk == KC - 1 and t < tiles - 1:
                            last.then_inc(tile_done, 1)
                        if between and t == tiles - 1 and kk < KC - 1:
                            between(kk)
                    last.then_inc(w_used, 1)

            def branch(base, per, i, done, ready):
                for jj in range(2):
                    j = 6 + jj
                    split_ready(base, per, i, j)
                    order = [(f, kq) for kq in range(KH) for f in range(4)] if jj == 0 else \
                        [(f, kq) for f in range(4) for kq in range(KH)]
                    for f, kq in order:
                        if jj == 0 and f == 0:
                            ready(kq)
                        wh = whi[:, j % NSPL, kq, f * P:(f + 1) * P]
                        wl = wlo[:, j % NSPL, kq, f * P:(f + 1) * P]
                        o = ps[:, branch_bank(4 * jj + f), :]
                        mm(o, wh, yhi[:, kq, :], kq == 0, False)
                        mm(o, wh, ylo[:, kq, :], False, False)
                        last = mm(o, wl, yhi[:, kq, :], False, kq == KH - 1)
                        if kq == KH - 1:
                            last.then_inc(done if f < 3 else w_used, 1)

            def gates(base, ready):
                for cg in range(2):
                    for kh in range(2):
                        j = 2 * cg + kh
                        split_ready(base, 0, 0, j)
                        for kq in range(KH):
                            kk = KH * kh + kq
                            for f in range(4):
                                if kk == 0:
                                    ready(4 * cg + f)
                                wh = whi[:, j % NSPL, kq, f * P:(f + 1) * P]
                                wl = wlo[:, j % NSPL, kq, f * P:(f + 1) * P]
                                o = ps[:, 4 * cg + f, :]
                                mm(o, wh, hhi[:, kk, 0:L], kk == 0, False)
                                mm(o, wh, hlo[:, kk, 0:L], False, False)
                                last = mm(o, wl, hhi[:, kk, 0:L], False, kk == KC - 1)
                        last.then_inc(w_used, 1)

            pe.wait_ge(c_silu, 1)

            def mod_product(c):
                for kh in range(2):
                    j = 2 * c + kh
                    pe.wait_ge(raw_loaded[j % NRAW], 16 * (j // NRAW + 1))
                    if c >= MOD_A + 2 and kh == 0:
                        pe.wait_ge(mod_rows, c - 1)
                    for kq in range(KH):
                        kk = KH * kh + kq
                        last = mm(ps[0:2, mod_bank(c), :], ct[:, kk, :], raw[:, j % NRAW, kq, :], kk == 0, kk == KC - 1)
                    last.then_inc(mod_used, 1)

            for c in range(MOD_A):
                mod_product(c)
            pe.wait_ge(s_const, 16)
            pe.wait_ge(x_normed, TT)
            pe.wait_ge(mod_rows, MOD_A)
            for k in range(KC):
                if k >= 3:
                    for c in MOD_BEFORE[k]:
                        mod_product(c)
                    pe.wait_ge(h_lo, 2 * (k - 3) + 2)
                for t in range(TT):
                    o = ps[:, 2 * (k % 3) + t // LT, (t % LT) * P:(t % LT + 1) * P]
                    last = pe.transpose(o, F(A_X, TT, D)[:, t, k * P:(k + 1) * P], ident)
                last.then_inc(h_turned, 1)
            mod_product(11)
            pe.wait_ge(h_lo, 2 * KC)

            with pe.Fori(0, RET_HEADS) as h:
                B = (RET0, RET_N, h)
                for s in range(2):
                    split_ready(*B, s)
                    sh, sl = (w[:, s, :, :].rearrange("p k (s n) -> p (k s) n", n=DK) for w in (whi, wlo))
                    for kk in range(KC):
                        for f in (2 * s, 2 * s + 1):
                            c = f % 2
                            wh, wl = sh[:, kk, c * P:(c + 1) * P], sl[:, kk, c * P:(c + 1) * P]
                            o = ps[:, f, :]
                            first, end = kk == 0, kk == KC - 1
                            mm(o, wh, hhi[:, kk, 0:L], first, False)
                            mm(o, wh, hlo[:, kk, 0:L], False, False)
                            last = mm(o, wl, hhi[:, kk, 0:L], False, end)
                            if s == 1:
                                oc = ps[:, 4, c * C:(c + 1) * C]
                                mm(oc, wh, hhi[:, kk, L:T], first and c == 0, False, True)
                                mm(oc, wh, hlo[:, kk, L:T], False, False, True)
                                last = mm(oc, wl, hhi[:, kk, L:T], False, end and c == 1, True)
                    last.then_inc(w_used, 1)

                def v_ready(t):
                    if t == 3:
                        pe.wait_ge(qk_out, at(h, 5, 1))
                    elif t > 3:
                        pe.wait_ge(qk_out, at(h, 5, t - 2))

                proj_tokens(*B, 2, TT, lambda t: (5 + t) % 8, v_ready)

                def g_ready(t):
                    if t < 2:
                        pe.wait_ge(qk_out, at(h, 5, 4 + t))
                    else:
                        pe.wait_ge(v_out, at(h, TT, t - 1))

                proj_tokens(*B, 4, LT, lambda t: 3 + t, g_ready)
                qT, kT = F(A_QT, 2, L), F(A_KT, 2, T)
                pe.wait_ge(rope_done, at(h, 4, 4))
                pe.wait_ge(v_out, at(h, TT, TT))
                for m in range(TT):
                    if m >= 4:
                        pe.wait_ge(g_out, at(h, LT, m - 3))
                    for c in range(2):
                        last = mm(ps[:, (7 + m) % 8, :], kT[:, c, m * P:(m + 1) * P], qT[:, c, :], c == 0, c == 1)
                    last.then_inc(sc_done, 1)
                pe.wait_ge(g_out, at(h, LT, LT))
                for m in range(TT):
                    pe.wait_ge(pt_done, at(h, TT, m + 1))
                    for t in range(LT):
                        if m == 0 and t == 2:
                            pe.wait_ge(pt_done, at(h, TT, 2))
                        last = mm(ps[:, (5 + t) % 8, :], F(A_RAWQK, TT, L)[:, m, t * P:(t + 1) * P],
                                  F(A_V, TT, DV)[:, m, :], m == 0, m == TT - 1)
                        if m == TT - 1:
                            last.then_inc(o_done, 1)
                for t in range(LT):
                    pe.wait_ge(y_done, at(h, LT, t + 1))
                    for c in range(4):
                        last = pe.transpose(ps[:, 1 + c, t * P:(t + 1) * P],
                                            F(A_GATE, LT, DV)[:, t, c * P:(c + 1) * P], ident)
                    last.then_inc(yt_done, 1)

                def row_ready(kq):
                    pe.wait_ge(yt_lo, at(h, 4, kq + 1))

                branch(*B, br_done, row_ready)
                pe.wait_ge(br_out, at(h, KC, 8))

            gates(GA0, lambda c: None)

            with pe.Fori(0, GROUPS) as g:
                B = (DIFF0, DIFF_N, g)
                NQ, NU = LT + TT, LT * HG
                pe.wait_ge(gg_out, 4)
                proj_tokens(*B, 0, LT, lambda t: t)

                def k_ready(t):
                    if t == 0:
                        pe.wait_ge(gg_out, 8)
                    if t >= 4:
                        pe.wait_ge(q_raw, at(g, NQ, t - 3))

                def turn(n):
                    pe.wait_ge(q_ready, at(g, NQ, n + 1))
                    if n % NQ >= 2:
                        pe.wait_ge(q_out, at(g, NQ, n - 1))
                    for c in range(HG):
                        last = pe.transpose(ps[:, 2 + (n % 2), c * P:(c + 1) * P],
                                            F(A_PROB, TT, 512)[:, n % TT, c * P:(c + 1) * P], ident)
                    last.then_inc(q_turned, 1)

                def q_between(kk):
                    if kk == 5:
                        pe.wait_ge(q_raw, at(g, NQ, 4))
                    if kk in (5, 6):
                        turn(kk - 5)

                proj_tokens(*B, 2, TT, lambda t: (4 + t) % 8, k_ready, between=q_between)
                for n in range(2, LT):
                    turn(n)

                def dv_ready(t):
                    pe.wait_ge(q_raw, at(g, NQ, LT + t + 1))

                def turn_between(kk):
                    if kk in TURN_K:
                        turn(LT + TURN_K.index(kk))

                proj_tokens(*B, 4, TT, lambda t: (4 + t) % 8, dv_ready, between=turn_between)
                for n in range(LT + len(TURN_K), NQ):
                    turn(n)
                qT, kT = F(A_DQT, HG, L), F(A_DKT, HG, T)
                vv = F(A_DV, TT, 512)

                def scores(u):
                    qt, c = u // HG, u % HG
                    s0 = (u % 2) * 3
                    for s in range(2):
                        q = qT[s * DH:(s + 1) * DH, c, qt * P:(qt + 1) * P]
                        k = kT[s * DH:(s + 1) * DH, c, :]
                        cuts = ((512, 768), (0, 512)) if s == 0 else ((256, 768), (0, 256))
                        for n, (k0, k1) in enumerate(cuts):
                            col = s * T + k0
                            if s == 1 and n == 1:
                                pe.wait_ge(s_middle, at(g, NU, u + 1))
                            last = mm(psf[:, s0 * 512 + col:s0 * 512 + col + k1 - k0], q, k[:, k0:k1], True, True)
                            if s == 0 and n == 0:
                                last.then_inc(s_middle, 1)
                    last.then_inc(s_done, 1)

                def turn_probs(u):
                    pe.wait_ge(a_done, at(g, NU, u + 1))
                    s0 = (u % 2) * 1536
                    for m in range(TT):
                        last = pe.transpose(psf[:, s0 + m * P:s0 + (m + 1) * P],
                                            F(A_PROB, 2, 2, T)[:, u % 2, 0, m * P:(m + 1) * P], ident)
                    last.then_inc(at_turned, 1)

                def values(u):
                    qt, c = u // HG, u % HG
                    pe.wait_ge(at_out, at(g, NU, u + 1))
                    for m in range(TT):
                        last = mm(ps[:, 6 + qt % 2, c * P:(c + 1) * P], F(A_AT, 2, T)[:, u % 2, m * P:(m + 1) * P],
                                  vv[:, m, c * P:(c + 1) * P], m == 0, m == TT - 1)
                    last.then_inc(ov_done, 1)

                def turn_y(qt):
                    pe.wait_ge(yd_done, at(g, LT, qt + 1))
                    for c in range(HG):
                        last = pe.transpose(ps[:, 6 + qt % 2, c * P:(c + 1) * P],
                                            F(A_OY, 2, 512)[:, 1, c * P:(c + 1) * P], ident)
                    last.then_inc(yd_turned, 1)

                pe.wait_ge(q_out, at(g, NQ, NQ))
                pe.wait_ge(dv_out, at(g, TT, TT))
                scores(0)
                scores(1)
                for u in range(NU):
                    turn_probs(u)
                    if u >= 1:
                        if (u - 1) % HG == 0 and u - 1 >= 2 * HG:
                            pe.wait_ge(yd_lo, at(g, LT, (u - 1) // HG - 1))
                        values(u - 1)
                    if u % HG == 3 and u > HG:
                        turn_y(u // HG - 1)
                    if u + 2 < NU:
                        pe.wait_ge(at_out, at(g, NU, u + 1))
                        scores(u + 2)
                values(NU - 1)
                turn_y(LT - 1)
                pe.wait_ge(yd_lo, at(g, LT, LT))
                branch(*B, bd_done, lambda c: None)
                pe.wait_ge(bd_out, at(g, KC, 8))
            gates(GB0, lambda c: None)
            pe.wait_ge(gg_out, 12)
            def half_ready(c):
                pe.wait_ge(m_lo, KH if c == 0 else KC)

            proj_tokens(OUT0, 0, 0, 0, LT, lambda t: t, half=half_ready, xh=mhi, xl=mlo)
            proj_tokens(OUT0, 0, 0, 2, LT, lambda t: 4 + t, xh=mhi, xl=mlo, tile_done=xp_done)
            tri = cst[:, C_TRI:C_TRI + P]
            pe.wait_ge(pool_pre, 1)

            def places(t):
                pe.wait_ge(m_ready, t + 1)
                if t == 0:
                    pe.wait_ge(ones_made, 1)
                for s in range(t):
                    mm(ps[:, 4 + t, 0:N_EXPERTS], allone, mask3[:, s, 0:32], s == 0, False)
                mm(ps[:, 4 + t, 0:N_EXPERTS], tri, mask3[:, t, 0:32], t == 0, True).then_inc(pos_done, 1)

            pe.wait_ge(rw_loaded, 32)
            for t in range(LT):
                pe.wait_ge(n2_done, t + 1)
                if t == 0:
                    pe.wait_ge(xn_done, 4)
                for q in range(2):
                    if t:
                        pe.wait_ge(h2_out, 2 * (t - 1) + q + 1)
                    for c in range(4):
                        k = 4 * q + c
                        last = pe.transpose(ps[:, q, c * P:(c + 1) * P],
                                            F(A_HT, 2, D)[:, t % 2, k * P:(k + 1) * P], ident)
                    last.then_inc(h2_turned, 1)
                pe.wait_ge(h2_out, 2 * t + 2)
                if t >= 2:
                    pe.wait_ge(m_ready, t - 1)
                for k in range(KC):
                    last = mm(ps[:, 2 + t % 2, 0:N_EXPERTS], F(A_H2T, KC, L)[:, k, t * P:(t + 1) * P], rw[:, k, :],
                              k == 0, k == KC - 1)
                last.then_inc(lg_done, 1)
                if t:
                    places(t - 1)
            places(LT - 1)
            for t in range(LT):
                last = mm(ps[0:96, 0, 0:1], mask3[:, t, :], ones[:, 0:1], t == 0, t == LT - 1)
            last.then_inc(cnt_done, 1)
            pe.wait_ge(flag_ready, 1)
            mm(ps[0:96, 0, 0:1], tri[0:96, 0:96], small[0:96, 0:1], True, True).then_inc(opos_done, 1)
            pe.wait_ge(oh_ready, 1)
            oh = small[0:96, 8:8 + OVER + 1]
            mm(ps[0:1, 0, 0:OVER + 1], cst[0:96, C_CODE:C_CODE + 1], oh, True, True)
            mm(ps[0:1, 0, OVER + 1:2 * OVER + 2], cst[0:96, C_EXP:C_EXP + 1], oh, True, True)
            mm(ps[0:1, 0, 2 * OVER + 2:2 * OVER + 3], small[0:96, 0:1], ones[0:96, 0:1], True, True).then_inc(items_done, 1)

            xthi = yhi[:, 0:2, :].rearrange("p a (k n) -> p (a k) n", n=P)
            xtlo = yhi[:, 2:4, :].rearrange("p a (k n) -> p (a k) n", n=P)
            acthi = ylo[:, 0:2, :].rearrange("p a (k n) -> p (a k) n", n=P)
            actlo = ylo[:, 2:4, :].rearrange("p a (k n) -> p (a k) n", n=P)
            bias = F(A_BIAS, 1536).bitcast(BF16)
            W1COL = (0, 2, 1, 3)

            def turn_x():
                for q in range(2):
                    for c in range(4):
                        k = 4 * q + c
                        last = pe.transpose(ps[:, q, c * P:(c + 1) * P], F(A_XG, D)[:, k * P:(k + 1) * P], ident)
                    last.then_inc(xt_turned, 1)

            pe.wait_ge(items_ready, 1)
            n_items = pe.value_load(count_i[0:1, 0:1], min_val=N_EXPERTS, max_val=MAX_BLOCKS)
            pe.wait_ge(gathered, 16)
            turn_x()
            with pe.Fori(0, MAX_BLOCKS) as i:
                with pe.If(i < n_items):
                    def up(gidx):
                        for kh in range(2):
                            j = 2 * gidx + kh
                            pe.wait_ge(e_lo, at(i, MOE_N, j + 1))
                            for kq in range(KH):
                                kk = KH * kh + kq
                                o = ps[:, 2 + gidx, :]
                                wh, wl = e_whi[j % ESPL][:, kq, :], e_wlo[j % ESPL][:, kq, :]
                                if kk == 0:
                                    c = W1COL[gidx]
                                    mm(o, sel[0:96, :], bias[0:96, c * COL:(c + 1) * COL], True, False)
                                mm(o, xthi[:, kk, :], wh, False, False)
                                mm(o, xthi[:, kk, :], wl, False, False)
                                last = mm(o, xtlo[:, kk, :], wh, False, kk == KC - 1)
                            last.then_inc(e_used, 1)

                    def down(kh):
                        for c in range(2):
                            if kh == 0 and c == 1:
                                turn_act(1)
                            j = 8 + 2 * kh + c
                            pe.wait_ge(e_lo, at(i, MOE_N, j + 1))
                            o = ps[:, 6 + c, :]
                            if kh == 0:
                                last = mm(o, sel[0:96, :], bias[0:96, 2048 + c * COL:2048 + (c + 1) * COL], True, False)
                                if c == 1:
                                    last.then_inc(sel_used, 1)
                            for kq in range(KH):
                                kk = KH * kh + kq
                                wh, wl = e_whi[j % ESPL][:, kq, :], e_wlo[j % ESPL][:, kq, :]
                                mm(o, acthi[:, kk, :], wh, False, False)
                                mm(o, acthi[:, kk, :], wl, False, False)
                                last = mm(o, actlo[:, kk, :], wh, False, kk == KC - 1)
                            last.then_inc(e_used, 1)

                    def turn_act(hf):
                        pe.wait_ge(act_done, at(i, 2, hf + 1))
                        for c in range(4):
                            last = pe.transpose(ps[:, 2 * hf, c * P:(c + 1) * P],
                                                F(A_AC, 2, COL)[:, hf, c * P:(c + 1) * P], ident)
                        last.then_inc(act_turned, 1)

                    pe.wait_ge(xt_lo, at(i, 2, 2))
                    pe.wait_ge(sel_ready, at(i, 1, 1))
                    up(0)
                    up(1)
                    up(2)
                    turn_act(0)
                    up(3)
                    pe.wait_ge(gathered, at(i, 16, 32))
                    pe.wait_ge(act_lo, at(i, 2, 1))
                    turn_x()
                    pe.wait_ge(y_out, at(i, 2, 2))
                    down(0)
                    pe.wait_ge(act_lo, at(i, 2, 2))
                    down(1)


_INS = {
    "x": (L, D), "c": (1, D), "ctx": (C, D), "c_ctx": (D,), "norm1_g": (1, D), "norm2_g": (1, D),
    "w_mod": (D, 6 * D), "b_mod": (1, 6 * D), "w_in": (D, 11 * D), "ret_decay_logit": (1, 8),
    "ret_norm_g": (RET_HEADS, DV), "diff_q_norm_g": (1, DH), "diff_k_norm_g": (1, DH),
    "diff_lambda": (1, 4 * DH), "diff_norm_g": (1, 2 * DH), "w_br_ret": (2 * D, D), "w_br_diff": (D, D),
    "w_out": (D, D), "router_w": (D, N_EXPERTS), "router_b": (1, N_EXPERTS),
    "exp_w1": (N_EXPERTS, D, 2 * D), "exp_b1": (N_EXPERTS, 2 * D),
    "exp_w2": (N_EXPERTS, D, D), "exp_b2": (N_EXPERTS, D),
}


def constants(np):
    c = np.zeros((P, N_CONST), np.float32)
    p = np.arange(P)
    c[:, C_ID:C_ID + P] = np.eye(P)
    c[:, C_TRI:C_TRI + P] = p[:, None] < p[None, :]
    c[:, C_WIN:C_WIN + WIN] = np.arange(WIN)[None, :] - (L - P) - p[:, None]

    def angles(half, pos):
        inv = np.float32(10000.0) ** (-np.arange(half, dtype=np.float32) / np.float32(half))
        return pos.astype(np.float32)[None, :] * inv.astype(np.float32)[:, None]

    sign = np.where(p < 64, 1.0, -1.0)[:, None]
    o = C_ROPE_R
    for n in (GRID_H, GRID_W):
        ang = angles(DK // 4, np.arange(n))[p % (DK // 4)].astype(np.float64)
        c[:, o:o + n] = np.cos(ang)
        c[:, o + n:o + 2 * n] = sign * np.sin(ang)
        o += 2 * n
    for t in range(LT):
        tok = t * P + p
        tab = np.zeros((P, 2, 2, 2, 16))
        for ax, pos in enumerate((tok // GRID_W, tok % GRID_W)):
            ang = angles(DH // 4, pos).T.astype(np.float64)
            for s in range(2):
                tab[:, 0, ax, s] = np.cos(ang)
                tab[:, 1, ax, s] = np.sin(ang) * (-1.0 if s == 0 else 1.0)
        c[:, C_ROPE_D + t * 2 * DH:C_ROPE_D + (t + 1) * 2 * DH] = tab.reshape(P, 2 * DH)
        c[:, C_TOK + t] = tok
    c[:, C_IOTA:C_IOTA + N_EXPERTS] = np.arange(N_EXPERTS)[None, :]
    c[:, C_THR] = P * (p // 32 + 1)
    c[:, C_CODE] = p + 32
    c[:, C_EXP] = p % 32
    c[:, C_EYE3:C_EYE3 + N_EXPERTS] = (p % 32)[:, None] == np.arange(32)[None, :]
    return c


def kernel(**inputs):
    import numpy as np
    import concourse.bacc as bacc
    from concourse.bass_utils import run_bass_kernel_spmd

    nc = bacc.Bacc("TRN2", target_bir_lowering=False, num_devices=1)
    arrays, aps = {}, {}
    for name, shape in _INS.items():
        arrays[f"in_{name}"] = np.ascontiguousarray(np.asarray(inputs[name]).reshape(shape))
        aps[name] = nc.dram_tensor(f"in_{name}", shape, F32, kind="ExternalInput").ap()
    arrays["in_consts"] = constants(np)
    aps["consts"] = nc.dram_tensor("in_consts", (P, N_CONST), F32, kind="ExternalInput").ap()
    aps["out"] = nc.dram_tensor("out_x", (L, D), F32, kind="ExternalOutput").ap()
    scratch = (
        nc.dram_tensor("mod_rows_d", (2, 6 * D), F32, kind="Internal").ap(),
        nc.dram_tensor("h2_d", (L + P, D), F32, kind="Internal").ap(),
        nc.dram_tensor("list_d", (L * N_EXPERTS, 2), I32, kind="Internal").ap(),
        nc.dram_tensor("acc_d", (L + P, D), F32, kind="Internal").ap(),
        nc.dram_tensor("accr_d", (P, 4096), F32, kind="Internal").ap(),
    )
    build(nc, aps, scratch)
    r = run_bass_kernel_spmd(nc, [arrays], core_ids=[0])
    return r.results[0]["out_x"].reshape(1, L, D)
```
